# Optimizing a Trainium2 kernel written in Bass

```python
import jax, jax.numpy as jnp
from jax import lax
import numpy as np

D_MODEL = 2048
BATCH = 1
SEQ = 256
DEPTH = 1

N_MEM = 256
EPS = 1e-6
CONV_WIDTH = D_MODEL // 2
CONV_K = 3
GLA_HEADS = 4
GLA_DK = D_MODEL // 2
GLA_DV = D_MODEL
GLA_RANK = 16
GLA_TAU = 16.0
GLA_CHUNK = 64
MEM_HEADS = 4
MEM_WIDTH = D_MODEL // 2
N_BRANCH = 3
N_GROUPS = 4
EXPERTS_PER_GROUP = 4
N_EXPERTS = N_GROUPS * EXPERTS_PER_GROUP
TOP_K = 2
D_EXPERT = D_MODEL // 4
IN_SPLITS = (CONV_WIDTH, CONV_WIDTH, CONV_WIDTH, GLA_DK, GLA_DK, GLA_DV, GLA_DV, GLA_RANK, MEM_WIDTH, D_MODEL, D_MODEL, D_MODEL)
D_IN = 3 * CONV_WIDTH + 2 * GLA_DK + 2 * GLA_DV + GLA_RANK + MEM_WIDTH + N_BRANCH * D_MODEL

kernel_name = "hybrid_gated_conv_gla_memxattn_hiermoe"

def rms_norm(x, g):
    xf = x.astype(jnp.float32)
    y = xf * lax.rsqrt(jnp.mean(xf * xf, axis=-1, keepdims=True) + EPS)
    return (y * g.astype(jnp.float32)).astype(x.dtype)

def split_columns(z):
    idx = np.cumsum(np.array(IN_SPLITS))[:-1].tolist()
    return jnp.split(z, idx, axis=-1)

def short_conv_mixer(gb, gc, v, w_conv):
    u = gc * v
    s = u.shape[1]
    y = w_conv[0] * u
    for k in range(1, CONV_K):
        y = y + w_conv[k] * jnp.pad(u, ((0, 0), (k, 0), (0, 0)))[:, :s]
    return gb * y

def gla_mixer(q, k, v, r, a_lr, w_a2, b_a2, g_norm):
    f32 = jnp.float32
    bsz, s, _ = q.shape
    H, C = GLA_HEADS, GLA_CHUNK
    dk, dv = GLA_DK // H, GLA_DV // H
    n = s // C
    log_a = jax.nn.log_sigmoid((a_lr @ w_a2 + b_a2).astype(f32)) / GLA_TAU

    def heads(t, d):
        return t.astype(f32).reshape(bsz, n, C, H, d).transpose(0, 3, 1, 2, 4)

    qh = heads(q, dk) * (dk ** -0.5)
    kh = heads(k, dk)
    vh = heads(v, dv)
    bcum = jnp.cumsum(heads(log_a, dk), axis=3)
    b_last = bcum[:, :, :, -1:]
    q_dec = qh * jnp.exp(bcum)
    k_dec = kh * jnp.exp(-bcum)
    k_to_end = kh * jnp.exp(b_last - bcum)
    mask = jnp.tril(jnp.ones((C, C), dtype=bool))
    att = jnp.where(mask, jnp.einsum('bhnid,bhnjd->bhnij', q_dec, k_dec), 0.0)
    o_intra = jnp.einsum('bhnij,bhnjv->bhniv', att, vh)

    def step(state, xs):
        qd, kd, vv, bl = xs
        o = jnp.einsum('bhcd,bhdv->bhcv', qd, state)
        state = jnp.exp(bl[:, :, 0, :])[..., None] * state + jnp.einsum('bhcd,bhcv->bhdv', kd, vv)
        return state, o

    xs = (jnp.moveaxis(q_dec, 2, 0), jnp.moveaxis(k_to_end, 2, 0), jnp.moveaxis(vh, 2, 0), jnp.moveaxis(b_last, 2, 0))
    s0 = jnp.zeros((bsz, H, dk, dv), f32)
    _, o_inter = lax.scan(step, s0, xs)
    o = o_intra + jnp.moveaxis(o_inter, 0, 2)
    o = o * lax.rsqrt(jnp.mean(o * o, axis=-1, keepdims=True) + EPS)
    o = o.transpose(0, 2, 3, 1, 4).reshape(bsz, s, GLA_DV) * g_norm.astype(f32)
    return (o * jax.nn.silu(r.astype(f32))).astype(q.dtype)

def memory_cross_attention(q, mem_n, w_mem_kv):
    bsz, s, _ = q.shape
    hd = MEM_WIDTH // MEM_HEADS
    kmem, vmem = jnp.split(mem_n @ w_mem_kv, 2, axis=-1)
    qh = q.reshape(bsz, s, MEM_HEADS, hd)
    kh = kmem.reshape(bsz, N_MEM, MEM_HEADS, hd)
    vh = vmem.reshape(bsz, N_MEM, MEM_HEADS, hd)
    sc = jnp.einsum('bshd,bmhd->bhsm', qh, kh).astype(jnp.float32) * (hd ** -0.5)
    p = jax.nn.softmax(sc, axis=-1).astype(q.dtype)
    return jnp.einsum('bhsm,bmhd->bshd', p, vh).reshape(bsz, s, MEM_WIDTH)

def hybrid_mixer(h, mem, w_in, conv_w, gla_w_a2, gla_b_a2, gla_norm, norm_mem, w_mem_kv,
                 w_br_conv, w_br_gla, w_br_mem, w_o):
    f32 = jnp.float32
    z = h @ w_in
    cb, cc, cv, gq, gk, gv, gr, ga, mq, gate_a, gate_b, gate_m = split_columns(z)
    y_a = short_conv_mixer(cb, cc, cv, conv_w)
    y_b = gla_mixer(gq, gk, gv, gr, ga, gla_w_a2, gla_b_a2, gla_norm)
    y_m = memory_cross_attention(mq, rms_norm(mem, norm_mem), w_mem_kv)
    merged = (jax.nn.sigmoid(gate_a.astype(f32)) * (y_a @ w_br_conv).astype(f32)
              + jax.nn.sigmoid(gate_b.astype(f32)) * (y_b @ w_br_gla).astype(f32)
              + jax.nn.sigmoid(gate_m.astype(f32)) * (y_m @ w_br_mem).astype(f32))
    return merged.astype(h.dtype) @ w_o

def hierarchical_moe(h, w_rg, w_re, w_gate, w_up, w_down):
    f32 = jnp.float32
    bsz, s, d = h.shape
    t = h.reshape(bsz * s, d)
    pg = jax.nn.softmax((t @ w_rg).astype(f32), axis=-1)
    gsel = jnp.argmax(pg, axis=-1)
    wg = jnp.take_along_axis(pg, gsel[:, None], axis=-1)
    le = (t @ w_re).astype(f32).reshape(-1, N_GROUPS, EXPERTS_PER_GROUP)
    le_sel = jnp.take_along_axis(le, gsel[:, None, None], axis=1)[:, 0]
    top_p, top_i = lax.top_k(jax.nn.softmax(le_sel, axis=-1), TOP_K)
    top_p = top_p / jnp.sum(top_p, axis=-1, keepdims=True)
    eid = gsel[:, None] * EXPERTS_PER_GROUP + top_i
    comb = jnp.sum(jax.nn.one_hot(eid, N_EXPERTS, dtype=f32) * (wg * top_p)[..., None], axis=1)
    out = jnp.zeros((bsz * s, d), f32)
    for e in range(N_EXPERTS):
        hid = jax.nn.silu(t @ w_gate[e]) * (t @ w_up[e])
        out = out + comb[:, e:e + 1] * (hid @ w_down[e]).astype(f32)
    return out.astype(h.dtype).reshape(bsz, s, d)

def _normal(key, shape, scale):
    return jax.random.normal(key, shape, jnp.float32) * scale

def setup_inputs(seed: int = 0) -> dict:
    key = jax.random.key(seed)
    ks = jax.random.split(key, 24)
    D = D_MODEL
    gain = lambda k, shape: 1.0 + _normal(k, shape, 0.02)
    return {
        "x": _normal(ks[0], (BATCH, SEQ, D), 1.0),
        "mem": _normal(ks[1], (BATCH, N_MEM, D), 1.0),
        "norm_mix": gain(ks[2], (DEPTH, D)),
        "w_in": _normal(ks[3], (DEPTH, D, D_IN), D ** -0.5),
        "conv_w": _normal(ks[4], (DEPTH, CONV_K, CONV_WIDTH), CONV_K ** -0.5),
        "gla_w_a2": _normal(ks[5], (DEPTH, GLA_RANK, GLA_DK), GLA_RANK ** -0.5),
        "gla_b_a2": _normal(ks[6], (DEPTH, GLA_DK), 0.1),
        "gla_norm": gain(ks[7], (DEPTH, GLA_DV)),
        "norm_mem": gain(ks[8], (DEPTH, D)),
        "w_mem_kv": _normal(ks[9], (DEPTH, D, 2 * MEM_WIDTH), D ** -0.5),
        "w_br_conv": _normal(ks[10], (DEPTH, CONV_WIDTH, D), CONV_WIDTH ** -0.5),
        "w_br_gla": _normal(ks[11], (DEPTH, GLA_DV, D), GLA_DV ** -0.5),
        "w_br_mem": _normal(ks[12], (DEPTH, MEM_WIDTH, D), MEM_WIDTH ** -0.5),
        "w_o": _normal(ks[13], (DEPTH, D, D), D ** -0.5),
        "norm_ffn": gain(ks[14], (DEPTH, D)),
        "w_router_group": _normal(ks[15], (DEPTH, D, N_GROUPS), D ** -0.5),
        "w_router_expert": _normal(ks[16], (DEPTH, D, N_EXPERTS), D ** -0.5),
        "w_gate": _normal(ks[17], (DEPTH, N_EXPERTS, D, D_EXPERT), D ** -0.5),
        "w_up": _normal(ks[18], (DEPTH, N_EXPERTS, D, D_EXPERT), D ** -0.5),
        "w_down": _normal(ks[19], (DEPTH, N_EXPERTS, D_EXPERT, D), D_EXPERT ** -0.5),
        "norm_final": gain(ks[20], (D,)),
    }

def reference(x, mem, norm_mix, w_in, conv_w, gla_w_a2, gla_b_a2, gla_norm, norm_mem, w_mem_kv,
              w_br_conv, w_br_gla, w_br_mem, w_o, norm_ffn, w_router_group, w_router_expert,
              w_gate, w_up, w_down, norm_final):
    for l in range(DEPTH):
        h = rms_norm(x, norm_mix[l])
        x = x + hybrid_mixer(h, mem, w_in[l], conv_w[l], gla_w_a2[l], gla_b_a2[l], gla_norm[l],
                             norm_mem[l], w_mem_kv[l], w_br_conv[l], w_br_gla[l], w_br_mem[l], w_o[l])
        h = rms_norm(x, norm_ffn[l])
        x = x + hierarchical_moe(h, w_router_group[l], w_router_expert[l], w_gate[l], w_up[l], w_down[l])
    return rms_norm(x, norm_final)


_drawn_inputs = setup_inputs


def setup_inputs(seed=0):
    import zlib

    import numpy as np

    out = dict(_drawn_inputs(seed))
    spreads = {}
    factors = {'gla_norm': 32.969,
     'norm_mem': 8.0,
     'norm_final': 8.278,
     'gla_b_a2': 2.842,
     'norm_ffn': 8.0}
    for name, (base, spread) in spreads.items():
        noise = np.random.default_rng([zlib.crc32(name.encode()), seed]).standard_normal(out[name].shape)
        drawn = base * np.exp(spread * noise) if base else spread * noise
        out[name] = __import__('jax').numpy.asarray(drawn.astype(out[name].dtype))
    for name, factor in factors.items():
        out[name] = (out[name] * factor).astype(out[name].dtype)
    return out
```

```python
import concourse.bass as bass
from concourse import mybir
from contextlib import ExitStack, contextmanager

P = 128
S = 256
TT = S // P
D = 2048
KD = D // P
BLK = 512
CONV = 1024
KC = CONV // P
HEADS = 4
DK = 256
DV = 512
CH = 64
NCH = S // CH
RANK = 16
EPS = 1e-6
N_GROUPS = 4
EPG = 4
N_EXPERTS = 16
DE = 512
KE = DE // P
SLOTS = 64
IN_COLS = 16400
COL_CONV, COL_GQ, COL_GV, COL_GR = 0, 3072, 5120, 7168
COL_GA, COL_MQ, COL_GATE_A, COL_GATE_B, COL_GATE_M = 9216, 9232, 10256, 12304, 14352

RAW_SLOTS = 4
SPLIT_SLOTS = 4
MOE_SLOTS = 8
START = 1


class Phase:

    def __init__(self, iters, granules, q0, j0):
        self.iters, self.granules, self.q0, self.j0 = iters, granules, q0, j0
        self.per = sum(granules)
        self.jobs = len(granules)
        self.q_end = q0 + iters * self.per
        self.j_end = j0 + iters * self.jobs


def phases():
    out, q, j = {}, 0, 0
    for name, iters, granules in (
        ("mem_kv", 2, (8, 8)), ("mem_q", 1, (8, 8)), ("branch_m", 2, (8, 4, 8, 4)),
        ("gla_qk", 2, (8, 8)), ("gla_v", 2, (8, 8)), ("gla_r", 2, (8, 8)),
        ("conv_cv", 2, (8, 8)), ("conv_b", 1, (8, 8)), ("branch_b", 4, (8, 8)),
        ("branch_a", 2, (8, 4, 8, 4)), ("out_a", 1, (8, 8)), ("out_b", 1, (8, 8)),
    ):
        out[name] = Phase(iters, granules, q, j)
        q, j = out[name].q_end, out[name].j_end
    return out, q


@contextmanager
def rounds_of(eng, n):
    if n == 1:
        yield 0
    else:
        with eng.Fori(0, n) as it:
            yield it


def hybrid_layer(nc, x, mem, norm_mix, w_in, conv_w, gla_w_a2, gla_b_a2, gla_norm, norm_mem,
                 w_mem_kv, w_br_conv, w_br_gla, w_br_mem, w_o, norm_ffn, w_router_group,
                 w_router_expert, w_gate, w_up, w_down, norm_final, out):
    f32, f32r, i32 = mybir.dt.float32, mybir.dt.float32r, mybir.dt.int32
    ALU, ACT, AX = mybir.AluOpType, mybir.ActivationFunctionType, mybir.AxisListType
    PH, TOTAL_Q = phases()

    def k_major(w):
        return w.rearrange("(kc p) n -> p kc n", p=P)

    x_v = x[0].rearrange("(t p) d -> p t d", p=P)
    mem_v = mem[0].rearrange("(t p) d -> p t d", p=P)
    out_v = out[0].rearrange("(t p) d -> p t d", p=P)
    in_v, kv_v, o_v = k_major(w_in[0]), k_major(w_mem_kv[0]), k_major(w_o[0])
    bra_v, brb_v, brm_v = k_major(w_br_conv[0]), k_major(w_br_gla[0]), k_major(w_br_mem[0])
    gate_v = w_gate[0].rearrange("e (kc p) n -> p e kc n", p=P)
    up_v = w_up[0].rearrange("e (kc p) n -> p e kc n", p=P)
    down_v = w_down[0].rearrange("e (kc p) n -> p e kc n", p=P)

    KB = 1024
    base = (nc.sbuf_base + 31) // 32 * 32

    def at(name, kb, shape, dt=f32):
        return nc.alloc_sbuf_tensor_at(name, shape, dt, offset=base + int(kb * KB))

    ident = at("ident", 0, [P, P])
    pcol = at("pcol", 0.5, [P, 96])
    w_ga = at("w_ga", 1, [P, KD, RANK])
    w_rt = at("w_rt", 2, [P, KD, N_GROUPS + N_EXPERTS])
    chunk_keep = at("chunk_keep", 3.25, [P, S])
    decay_last = at("decay_last", 4.25, [P, KC, NCH])
    stat = at("stat", 4.5, [P, 64])
    n_rounds = at("n_rounds", 4.75, [P, 1], i32)
    merged = at("merged", 6, [P, TT, D])
    x2 = at("x2", 6, [P, TT, D])
    junk = at("junk", 6, [P, D])
    raw = at("raw", 22, [P, RAW_SLOTS, 4 * BLK])
    w_hi = at("w_hi", 54, [P, SPLIT_SLOTS, 2 * BLK], f32r)
    w_lo = at("w_lo", 70, [P, SPLIT_SLOTS, 2 * BLK], f32r)
    h_hi = at("h_hi", 86, [P, KD, S], f32r)
    h_lo = at("h_lo", 102, [P, KD, S], f32r)
    y_hi = at("y_hi", 118, [P, KD, S], f32r)
    y_lo = at("y_lo", 134, [P, KD, S], f32r)
    A, B, C = 150, 166, 182
    x_tok = at("x_tok", A, [P, TT, D])
    mem_tok = at("mem_tok", B, [P, TT, D])
    prow = at("prow", C, [96, P])
    kv = at("kv", A, [P, TT, D])
    mq = at("mq", B, [P, TT, CONV])
    kT = at("kT", B + 8, [P, KC, S])
    qT = at("qT", C, [P, KC, S])
    prob = at("prob", C + 8, [P, HEADS, TT, S])
    probT = at("probT", C + 16, [P, HEADS, TT, S])
    sig = at("sig", C, [P, TT, BLK])
    gated = at("gated", C + 4, [P, TT, BLK])
    gqk = at("gqk", A, [P, TT, D])
    gv = at("gv", B, [P, TT, D])
    w_a2 = at("w_a2", A, [RANK, CONV])
    a_lr = at("a_lr", A + 4, [RANK, S])
    h_full = at("h_full", B, [P, KD, S])
    dec_k = at("dec_k", C, [P, KC, S])
    dec_end = at("dec_end", C + 8, [P, KC, S])
    dec_q = at("dec_q", C + 16, [P, KC, S])
    q_far = at("q_far", A, [P, KC, 2 * CH])
    q_skip = at("q_skip", A + 4, [P, KC, CH])
    attT = [at(f"attT{i}", A + 6 + 1.5 * i, [P, 3 * P]) for i in range(2)]
    sq_junk = at("sq_junk", A + 9, [P, BLK])
    gr = at("gr", C, [P, TT, D])
    ccv = at("ccv", A, [P, TT, D])
    cb = at("cb", C + 16, [P, TT, CONV])
    uT = at("uT", B, [P, KC, S + 2])
    cbT = at("cbT", C + 8, [P, KC, S])
    conv = at("conv", A, [P, KC, S])
    conv_t = at("conv_t", A + 8, [P, S])
    xn = at("xn", 22, [P, TT, D])
    hT = at("hT", 38, [P, KD, S])
    dispT = at("dispT", 54, [P, EPG, S])
    disp = at("disp", 58, [P, TT, EPG * SLOTS])
    disp_w = at("disp_w", 60, [P, TT, EPG, 2 * SLOTS])
    y_exp = at("y_exp", 64, [P, 2, 2, BLK])
    hidT = at("hidT", 72, [P, 2, KE, SLOTS])
    act_gate = at("act_gate", 74, [P, BLK])
    hid = at("hid", 76, [P, 2, BLK])
    slot_no = at("slot_no", 94, [P, SLOTS])
    tri = at("tri", 94.5, [P, P])
    ones = at("ones", 95, [P, P])
    logitT = at("logitT", 95.5, [N_GROUPS + N_EXPERTS, S])
    g_fin = at("g_fin", 80.5, [P, D])
    rt = at("rt", 88.5, [P, 40, TT * 16])
    fin = at("fin", 22, [P, TT, D])
    moe_raw = at("moe_raw", 143, [P, MOE_SLOTS, 4 * BLK])
    G_MIX, G_MEM, G_GLA, G_FFN, B_A2, W_CONV = 0, 16, 32, 48, 64, 72

    ctx = ExitStack()
    with ctx:
        bank = [ctx.enter_context(nc.psum_tensor(f"bank{i}", [P, BLK], f32)) for i in range(8)]
        pair = [bank[0:2], bank[2:4]]

        def turn_bank(u):
            return bank[4 + u % 2]

        def aux_bank(u):
            return bank[6 + u % 2]

        def half(b, i):
            return b[:, i * S:(i + 1) * S]

        def sem(name):
            return ctx.enter_context(nc.semaphore(name))

        consts_made = sem("consts_made")
        params_in = sem("params_in")
        x_in = [sem(f"x_in{t}") for t in range(TT)]
        mem_in = [sem(f"mem_in{t}") for t in range(TT)]
        small_in = sem("small_in")
        a2_in = sem("a2_in")
        x_again = sem("x_again")
        gfin_in, out_stored = sem("gfin_in"), sem("out_stored")
        raw_loaded = [sem(f"raw_loaded{i}") for i in range(RAW_SLOTS)]
        hi_split, lo_split = sem("hi_split"), sem("lo_split")
        mm_done = sem("mm_done")
        pair_taken = [sem(f"pair_taken{i}") for i in range(2)]
        sq_ready, ms_ready, rms_ready, normed = (sem("sq_ready"), sem("ms_ready"),
                                                 sem("rms_ready"), sem("normed"))
        turned = sem("turned")
        turn_taken = [sem(f"turn_taken{i}") for i in range(2)]
        aux_done = sem("aux_done")
        aux_taken = [sem(f"aux_taken{i}") for i in range(2)]
        hi_written, lo_written = sem("hi_written"), sem("lo_written")
        params_ready = sem("params_ready")
        act_chain, dve_chain, pool_chain = sem("act_chain"), sem("dve_chain"), sem("pool_chain")
        max_ready, prob_raw, prob_ready = sem("max_ready"), sem("prob_raw"), sem("prob_ready")
        h_full_ready, a_lr_ready = sem("h_full_ready"), sem("a_lr_ready")
        pre_ready, soft_ready, decay_sum_ready = (sem("pre_ready"), sem("soft_ready"),
                                                  sem("decay_sum_ready"))
        decay_ready, decayed_qk = sem("decay_ready"), sem("decayed_qk")
        att_done, att_masked = sem("att_done"), sem("att_masked")
        att_lower_taken, att_upper_taken = sem("att_lower_taken"), sem("att_upper_taken")
        o_done, o_sq, o_taken = sem("o_done"), sem("o_sq"), sem("o_taken")
        swish_ready, yb_ready = sem("swish_ready"), sem("yb_ready")
        conv_u, conv_in, conv_out = sem("conv_u"), sem("conv_in"), sem("conv_out")
        merged_done, residual_ready = sem("merged_done"), sem("residual_ready")
        y_ready = sem("y_ready")
        router_exp, router_d = sem("router_exp"), sem("router_d")
        route_ready, pos_done, rounds_ready = sem("route_ready"), sem("pos_done"), sem("rounds_ready")
        moe_loaded = [sem(f"moe_loaded{i}") for i in range(MOE_SLOTS)]
        moe_freed = {by: sem(f"moe_freed_by_{by}") for by in ("tensor", "scalar")}
        freed_loads, freed_in_group = moe_frees()
        disp_ready, dispw_ready = sem("disp_ready"), sem("dispw_ready")
        gt_done, gathered = sem("gt_done"), sem("gathered")
        gt_taken = [sem(f"gt_taken{i}") for i in range(2)]
        gu_done, silu_ready, hid_ready = sem("gu_done"), sem("silu_ready"), sem("hid_ready")
        down_done = sem("down_done")
        y_taken = [sem(f"y_taken{i}") for i in range(2)]
        comb_done = sem("comb_done")
        acc_done = sem("acc_done")
        stored = sem("stored")

        T_H, T_MEM, T_MEMK, T_MEMQ, T_PROB = 0, 8, 16, 20, 24
        T_GQ, T_GK, T_YB, T_U, T_CB, T_MERGED, T_XN, T_ROUTE = 28, 32, 36, 44, 48, 52, 60, 68
        U_PARAMS = 0
        MEM_ORDER = [("s", 0), ("s", 1), ("y", 0), ("s", 2), ("y", 1), ("s", 3), ("y", 2), ("y", 3)]
        U_MEM = {what: 1 + n for n, what in enumerate(MEM_ORDER)}
        U_GA, U_A2, U_LOGIT = 9, 10, 14
        GATHER, BACK, HIDDEN, GT_USES = 0, 8, 10, 14

        def turned_before(eng, u):
            for s in range(2):
                eng.wait_ge(turn_taken[s], (u + 1 - s) // 2)

        def aux_before(eng, u):
            for s in range(2):
                eng.wait_ge(aux_taken[s], (u + 1 - s) // 2)

        block = ctx.enter_context(nc.Block())

        @block.sync
        def _(sp):
            vecs = ((norm_mix[0], 16, G_MIX), (norm_mem[0], 16, G_MEM), (gla_norm[0], 16, G_GLA),
                    (norm_ffn[0], 16, G_FFN), (gla_b_a2[0], 8, B_A2))
            sp.dma_start(x_tok[:, 0, :], x_v[:, 0, :]).then_inc(x_in[0], 16)
            sp.dma_start(x_tok[:, 1, :], x_v[:, 1, :]).then_inc(x_in[1], 16)
            for v, n, row in vecs:
                sp.dma_start(prow[row:row + n, :], v.rearrange("(a b) -> a b", b=P))\
                  .then_inc(params_in, 16)
            sp.dma_start(prow[W_CONV:W_CONV + 24, :],
                         conv_w[0].rearrange("k (c b) -> (k c) b", b=P)).then_inc(params_in, 16)
            for t in range(TT):
                sp.dma_start(mem_tok[:, t, :], mem_v[:, t, :]).then_inc(mem_in[t], 16)

            def load(ph, load_no, it, src, slots=1):
                n = ph.q0 // 2 + load_no
                if slots and not (isinstance(it, int) and n + it * ph.per // 2 < RAW_SLOTS):
                    sp.wait_ge(lo_split, 2 * (n - RAW_SLOTS) + 2 * slots + it * ph.per)
                sp.dma_start(raw[:, n % RAW_SLOTS, :].rearrange("p (k n) -> p k n", k=4), src)\
                  .then_inc(raw_loaded[n % RAW_SLOTS], 16)

            def load_columns(name, view, col, unrolled=False):
                ph = PH[name]
                for first in range(ph.iters if unrolled else 1):
                    with rounds_of(sp, 1 if unrolled else ph.iters) as i:
                        it = first if unrolled else i
                        off = it * 2 * BLK if isinstance(it, int) else sp.snap(it * (2 * BLK))
                        for jb in range(2):
                            for l in range(4):
                                load(ph, 4 * jb + l, it,
                                     view[:, 4 * l:4 * l + 4, bass.ds(off + (col + jb * BLK), BLK)])

            def load_branch(name, gate_col, branch_v):
                ph = PH[name]
                kl = [g // 2 for g in ph.granules]
                with rounds_of(sp, ph.iters) as it:
                    off = sp.snap(it * (ph.jobs // 2 * BLK))
                    n = 0
                    for jb in range(ph.jobs):
                        view, col = ((in_v, gate_col), (branch_v, 0))[jb % 2]
                        for l in range(kl[jb]):
                            load(ph, n, it, view[:, 4 * l:4 * l + 4,
                                                 bass.ds(off + (col + jb // 2 * BLK), BLK)],
                                 slots=2 if jb % 2 == 0 and l == kl[jb] - 1 else 0 if jb % 2 and l == 0 else 1)
                            n += 1

            load_columns("mem_kv", kv_v, 0, unrolled=True)
            load_columns("mem_q", in_v, COL_MQ)
            load_branch("branch_m", COL_GATE_M, brm_v)
            load_columns("gla_qk", in_v, COL_GQ)
            load_columns("gla_v", in_v, COL_GV)
            load_columns("gla_r", in_v, COL_GR)
            load_columns("conv_cv", in_v, COL_CONV + CONV)
            load_columns("conv_b", in_v, COL_CONV)
            load_branch("branch_b", COL_GATE_B, brb_v)
            load_branch("branch_a", COL_GATE_A, bra_v)
            load_columns("out_a", o_v, 0)
            load_columns("out_b", o_v, 2 * BLK)

            turned_before(sp, T_XN)
            for by in ("tensor", "scalar"):
                sp.sem_inc(moe_freed[by], freed_in_group[by])

            def expert_loads(group, per_group):
                def load_moe(n, src):
                    by, count = freed_loads[n - MOE_SLOTS]
                    groups = 1 if n >= MOE_SLOTS else 0
                    sp.wait_ge(moe_freed[by], (per_group + groups) * freed_in_group[by] + count)
                    sp.dma_start(moe_raw[:, n % MOE_SLOTS, :].rearrange("p (k n) -> p k n", n=src.shape[-1]),
                                 src).then_inc(moe_loaded[n % MOE_SLOTS], 16)
                n = 0
                for kind, i in MOE_ORDER:
                    e = bass.ds(group * EPG + i, 1)
                    for l in range(4):
                        if kind == "gu":
                            load_moe(n, gate_v[:, e, 4 * l:4 * l + 4, :].rearrange("p e k n -> p (e k) n"))
                            load_moe(n + 1, up_v[:, e, 4 * l:4 * l + 4, :].rearrange("p e k n -> p (e k) n"))
                            n += 2
                        elif kind == "d":
                            load_moe(n, down_v[:, e, l:l + 1, :].rearrange("p e k n -> p (e k) n"))
                            n += 1

            with sp.Fori(0, N_GROUPS) as g:
                expert_loads(g, g)
            sp.wait_ge(rounds_ready, 1)
            rounds = sp.value_load(n_rounds[0:1, 0:1], min_val=1, max_val=S // SLOTS)
            with sp.If(rounds > 1):
                with sp.Fori(1, rounds) as r:
                    with sp.Fori(0, N_GROUPS) as g:
                        expert_loads(g, r * N_GROUPS + g)
            for t in range(TT):
                sp.wait_ge(stored, t + 1)
                sp.dma_start(out_v[:, t, :], fin[:, t, :]).then_inc(out_stored, 16)
            sp.wait_ge(out_stored, 16 * TT)

        @block.gpsimd
        def _(pool):
            n = [0]

            def chain(ins):
                n[0] += 1
                ins.then_inc(pool_chain, 1)
                pool.wait_ge(pool_chain, n[0])

            chain(nc.gpsimd.memset(ident[:], 0.0))
            nc.gpsimd.affine_select(out=ident[:], in_=ident[:], compare_op=ALU.not_equal, fill=1.0, base=0,
                                    pattern=[[-1, P]], channel_multiplier=1).then_inc(consts_made, 1)
            chain(nc.gpsimd.memset(chunk_keep[:], 1.0))
            chain(nc.gpsimd.memset(chunk_keep[:].rearrange("p (n c) -> p n c", c=CH)[:, :, 0:1], 0.0))
            pool.dma_start(w_ga[:], in_v[:, :, COL_GA:COL_GA + RANK]).then_inc(small_in, 16)
            pool.dma_start(w_rt[:, :, 0:N_GROUPS], k_major(w_router_group[0])).then_inc(small_in, 16)
            pool.dma_start(w_rt[:, :, N_GROUPS:], k_major(w_router_expert[0])).then_inc(small_in, 16)
            turned_before(pool, T_GQ)
            aux_before(pool, U_GA)
            pool.dma_start(w_a2[:], gla_w_a2[0]).then_inc(a2_in, 16)
            nc.gpsimd.tensor_tensor(h_full[:], h_hi[:].bitcast(f32), h_lo[:].bitcast(f32), ALU.add)\
                     .then_inc(h_full_ready, 1)
            pool.wait_ge(decayed_qk, 1)
            for i in range(2):
                nc.gpsimd.memset(attT[i][:], 0.0).then_inc(att_masked, 1)
            for h in range(HEADS):
                pool.wait_ge(att_lower_taken, h + 1)
                pool.wait_ge(att_upper_taken, 2 * h + 2)
                a = attT[h % 2]
                nc.gpsimd.affine_select(out=a[:, 0:S], in_=a[:, 0:S], compare_op=ALU.is_ge, fill=0.0, base=0,
                                        pattern=[[1, S]], channel_multiplier=-1).then_inc(att_masked, 1)
                nc.gpsimd.affine_select(out=a[:, S:], in_=a[:, S:], compare_op=ALU.is_ge, fill=0.0, base=0,
                                        pattern=[[1, P]], channel_multiplier=-1).then_inc(att_masked, 1)
            pool.wait_ge(pair_taken[0], PH["conv_b"].j0)
            pool.wait_ge(pair_taken[1], PH["conv_b"].j0)
            for t in range(TT):
                nc.gpsimd.tensor_tensor(ccv[:, t, 0:CONV], ccv[:, t, 0:CONV], ccv[:, t, CONV:], ALU.mult)\
                         .then_inc(conv_u, 1)
            turned_before(pool, T_U)
            chain(nc.gpsimd.memset(uT[:, :, 0:2], 0.0))
            turned_before(pool, T_MERGED)
            for c in range(KC):
                tap = [pcol[:, W_CONV + k * KC + c:W_CONV + k * KC + c + 1] for k in range(3)]
                chain(nc.gpsimd.tensor_scalar(conv[:, c, :], uT[:, c, 2:S + 2], tap[0], 1.0, ALU.mult, ALU.mult))
                for k in (1, 2):
                    chain(nc.gpsimd.tensor_scalar(conv_t[:], uT[:, c, 2 - k:S + 2 - k], tap[k], 1.0,
                                                  ALU.mult, ALU.mult))
                    chain(nc.gpsimd.tensor_tensor(conv[:, c, :], conv[:, c, :], conv_t[:], ALU.add))
                nc.gpsimd.tensor_tensor(conv[:, c, :], conv[:, c, :], cbT[:, c, :], ALU.mult)\
                         .then_inc(conv_out, 1)
            pool.wait_ge(mm_done, TOTAL_Q)
            chain(nc.gpsimd.iota(slot_no[:], pattern=[[1, SLOTS]], base=0, channel_multiplier=0,
                                 allow_small_or_imprecise_dtypes=True))
            chain(nc.gpsimd.memset(ones[:], 1.0))
            chain(nc.gpsimd.memset(tri[:], 1.0))
            chain(nc.gpsimd.affine_select(out=tri[:], in_=tri[:], compare_op=ALU.is_gt, fill=0.0, base=0,
                                          pattern=[[1, P]], channel_multiplier=-1))
            nc.gpsimd.iota(rt[:, 0, 0:4], pattern=[[-1, 4]], base=4, channel_multiplier=0,
                           allow_small_or_imprecise_dtypes=True).then_inc(consts_made, 1)
            pool.dma_start(g_fin[:], norm_final.rearrange("(a d) -> a d", a=1).to_broadcast([P, D]))\
                .then_inc(gfin_in, 16)

        @block.scalar
        def _(act):
            A_ = nc.scalar
            chained = [0]

            def chain(ins):
                chained[0] += 1
                ins.then_inc(act_chain, 1)
                act.wait_ge(act_chain, chained[0])

            def turn_hi(u0, dst, gain=None):
                for c in range(KD):
                    if c % 2 == 0:
                        act.wait_ge(turned, u0 + c // 2 + 1)
                    A_.activation(dst[:, c, :], half(turn_bank(u0 + c // 2), c % 2), ACT.Copy,
                                  scale=1.0 if gain is None else pcol[:, gain + c:gain + c + 1])\
                      .then_inc(hi_written, 1)

            def turn_copy(u0, dst):
                for u in range(u0 + 1, u0 + KC // 2, 2):
                    act.wait_ge(turned, u + 1)
                    c = 2 * (u - u0)
                    A_.copy(dst[:, c:c + 2, :], turn_bank(u)[:].rearrange("p (c s) -> p c s", c=2))\
                      .then_inc(turn_taken[u % 2], 1)

            def square_sum(src, k):
                if k:
                    act.wait_ge(sq_ready, k)
                A_.activation(junk[:], src, ACT.Square, accum_out=stat[:, k:k + 1]).then_inc(sq_ready, 1)

            for k in range(2 * TT):
                act.wait_ge((x_in + mem_in)[k], 16)
                square_sum((x_tok if k < TT else mem_tok)[:, k % TT, :], k)
                if k % TT == 1:
                    act.wait_ge(ms_ready, k // TT + 1)
                    A_.activation(stat[:, 8 + k - 1:8 + k + 1], stat[:, 4 + k - 1:4 + k + 1], ACT.Sqrt)\
                      .then_inc(rms_ready, 1)

            def split_hi(ph, q, it):
                n = ph.q0 + q + SPLIT_SLOTS
                if isinstance(it, int) and n + it * ph.per >= TOTAL_Q:
                    return
                slot = n // 2 % RAW_SLOTS
                if n % 2 == 0:
                    act.wait_ge(raw_loaded[slot], 16 * (n // 2 // RAW_SLOTS + 1) + it * (ph.per * 2))
                act.wait_ge(mm_done, ph.q0 + q + 1 + it * ph.per)
                A_.activation(w_hi[:, n % SPLIT_SLOTS, :], raw[:, slot, n % 2 * 1024:n % 2 * 1024 + 1024],
                              ACT.Copy).then_inc(hi_split, 1)

            def run(name, take):
                ph = PH[name]
                with rounds_of(act, ph.iters) as it:
                    q = 0
                    for jb, granules in enumerate(ph.granules):
                        for _ in range(granules):
                            split_hi(ph, q, it)
                            q += 1
                        act.wait_ge(mm_done, ph.q0 + q + it * ph.per)
                        take(ph, jb, it)

            def store_tile0(dst, col=0):
                def take(ph, jb, it):
                    A_.copy(dst[:, 0, bass.ds(it * 2 * BLK + col + jb * BLK, BLK)], pair[jb % 2][0][:])\
                      .then_inc(pair_taken[jb % 2], 1)
                return take

            def gate(ph, jb, it):
                if jb % 2 == 0:
                    act.wait_ge(pair_taken[1], ph.j0 + jb + it * ph.jobs)
                    for t in range(TT):
                        A_.activation(sig[:, t, :], pair[0][t][:], ACT.Sigmoid).then_inc(pair_taken[0], 1)

            for n in range(SPLIT_SLOTS):
                if n % 2 == 0:
                    act.wait_ge(raw_loaded[n // 2], 16)
                A_.activation(w_hi[:, n, :], raw[:, n // 2, n % 2 * 1024:n % 2 * 1024 + 1024], ACT.Copy)\
                  .then_inc(hi_split, 1)
            act.wait_ge(params_ready, 1)
            turn_hi(T_H, h_hi, G_MIX)
            turn_hi(T_MEM, y_hi, G_MEM)

            run("mem_kv", store_tile0(kv))
            run("mem_q", store_tile0(mq))

            turn_copy(T_MEMK, kT[:])
            turn_copy(T_MEMQ, qT[:])

            def exponentials(h):
                act.wait_ge(max_ready, h + 1)
                for t in range(TT):
                    A_.activation(prob[:, h, t, :], half(aux_bank(U_MEM["s", h]), t), ACT.Exp, scale=DK ** -0.5,
                                  bias=stat[:, 16 + 2 * h + t:17 + 2 * h + t],
                                  accum_out=stat[:, 24 + 2 * h + t:25 + 2 * h + t])\
                      .then_inc(prob_raw, 1)

            def memory_out_hi(h):
                u = U_MEM["y", h]
                act.wait_ge(aux_done, u + 1)
                A_.copy(y_hi[:, 2 * h:2 * h + 2, :], aux_bank(u)[:].rearrange("p (c s) -> p c s", c=2))\
                  .then_inc(hi_written, 1)

            for kind, h in MEM_ORDER:
                (exponentials if kind == "s" else memory_out_hi)(h)
            run("branch_m", gate)

            act.wait_ge(pair_taken[1], PH["branch_m"].j_end)
            act.wait_ge(aux_done, U_GA + 1)
            A_.copy(a_lr[:], aux_bank(U_GA)[0:RANK, 0:S]).then_inc(a_lr_ready, 1)
            act.wait_ge(a_lr_ready, 1)
            for c in range(KC):
                act.wait_ge(aux_done, U_A2 + c // 2 + 1)
                A_.activation(dec_k[:, c, :], half(aux_bank(U_A2 + c // 2), c % 2), ACT.Identity,
                              bias=pcol[:, B_A2 + c:B_A2 + c + 1]).then_inc(pre_ready, 1)
            run("gla_qk", store_tile0(gqk))
            act.wait_ge(pre_ready, KC)
            chain(A_.activation(dec_end[:], dec_k[:], ACT.Abs))
            chain(A_.activation(dec_end[:], dec_end[:], ACT.Exp, scale=-1.0))
            A_.activation(dec_end[:], dec_end[:], ACT.Ln, bias=1.0).then_inc(soft_ready, 1)
            run("gla_v", store_tile0(gv))
            act.wait_ge(decay_sum_ready, 1)
            A_.activation(dec_k[:], dec_q[:], ACT.Exp, scale=-1.0 / 16).then_inc(decay_ready, 1)
            A_.activation(dec_end[:], dec_end[:], ACT.Exp, scale=-1.0 / 16).then_inc(decay_ready, 1)
            A_.activation(decay_last[:], decay_last[:], ACT.Exp, scale=1.0 / 16).then_inc(decay_ready, 1)
            act.wait_ge(decay_ready, 3)
            A_.activation(dec_q[:], dec_q[:], ACT.Exp, scale=1.0 / 16).then_inc(decay_ready, 1)

            def scores_out(h):
                act.wait_ge(att_done, h + 1)
                act.wait_ge(att_masked, 2 if h < 2 else 2 + 2 * (h - 1))
                if h >= 2:
                    act.wait_ge(o_done, 2 * (h - 1))
                A_.copy(attT[h % 2][0:CH, :], bank[4 + h % 2][0:CH, 0:3 * P]).then_inc(att_lower_taken, 1)

            def squares(h):
                for t in range(TT):
                    act.wait_ge(o_done, 2 * h + t + 1)
                    if h or t:
                        act.wait_ge(o_sq, 2 * h + t)
                    A_.activation(sq_junk[:], bank[6 + t][:], ACT.Square,
                                  accum_out=stat[:, 32 + 2 * h + t:33 + 2 * h + t]).then_inc(o_sq, 1)

            for h in range(HEADS):
                scores_out(h)
                if h >= 1:
                    squares(h - 1)
            squares(HEADS - 1)
            act.wait_ge(ms_ready, 3)
            A_.activation(stat[:, 48:56], stat[:, 40:48], ACT.Sqrt).then_inc(rms_ready, 1)
            run("gla_r", store_tile0(gr))
            act.wait_ge(pair_taken[0], PH["gla_r"].j_end)
            act.wait_ge(pair_taken[1], PH["gla_r"].j_end)
            for t in range(TT):
                A_.activation(gr[:, t, :], gr[:, t, :], ACT.Silu).then_inc(swish_ready, 1)
            run("conv_cv", store_tile0(ccv))
            act.wait_ge(yb_ready, HEADS * TT)
            run("conv_b", store_tile0(cb))
            turn_hi(T_YB, y_hi, G_GLA)
            turn_copy(T_U, uT[:, :, 2:])
            turn_copy(T_CB, cbT[:])
            run("branch_b", gate)
            act.wait_ge(conv_out, KC)
            A_.copy(y_hi[:, 0:KC, :], conv[:]).then_inc(hi_written, 1)
            run("branch_a", gate)
            turn_hi(T_MERGED, h_hi)
            act.wait_ge(turned, T_XN)
            act.dma_start(x2[:], x_v).then_inc(x_again, 16)
            nothing = lambda ph, jb, it: None
            run("out_a", nothing)
            run("out_b", nothing)

            def residual_squares(first, ready, value):
                for t in range(TT):
                    act.wait_ge(ready, value)
                    act.wait_ge(sq_ready, 4 + first + t)
                    A_.activation(fin[:, t, :], x2[:, t, :], ACT.Square,
                                  accum_out=stat[:, t:t + 1]).then_inc(sq_ready, 1)

            residual_squares(0, residual_ready, 1)
            act.wait_ge(ms_ready, 4)
            A_.activation(stat[:, 8:10], stat[:, 4:6], ACT.Sqrt).then_inc(rms_ready, 1)
            for u in range(1, KD // 2, 2):
                act.wait_ge(turned, T_XN + u + 1)
                for c in (2 * u, 2 * u + 1):
                    ins = A_.activation(hT[:, c, :], half(turn_bank(u), c % 2), ACT.Copy,
                                        scale=pcol[:, G_FFN + c:G_FFN + c + 1])
                    ins.then_inc(act_chain if c % 2 == 0 else turn_taken[1], 1)
                chained[0] += 1
            for i in range(2):
                act.wait_ge(router_d, i + 1)
                A_.activation(rt[:, 3, 0:8], rt[:, 2, 0:8], ACT.Exp).then_inc(router_exp, 1)

            act.wait_ge(rounds_ready, 1)
            for started in (gt_taken[1], y_taken[0]):
                act.sem_inc(started, START)
            rounds = act.value_load(n_rounds[0:1, 0:1], min_val=1, max_val=S // SLOTS)
            with act.Fori(0, rounds) as r, act.Fori(0, N_GROUPS) as g:
                it = r * N_GROUPS + g
                for u in range(1, KD // 2, 2):
                    act.wait_ge(gt_done, it * GT_USES + u + 1 + START)
                    for c in (2 * u, 2 * u + 1):
                        A_.activation(hT[:, c, :], half(turn_bank(u), c % 2), ACT.Copy,
                                      scale=pcol[:, G_FFN + c:G_FFN + c + 1])\
                          .then_inc(gathered if c % 2 == 0 else gt_taken[1], 1)
                for kind, i in MOE_ORDER:
                    if kind == "gu":
                        act.wait_ge(gu_done, it * EPG + i + 1)
                        act.sem_inc(moe_freed["scalar"], 1)
                        act.wait_ge(hid_ready, it * EPG + i + START)
                        A_.activation(act_gate[SLOTS:, :], bank[i % 2][0:SLOTS, :], ACT.Silu)\
                          .then_inc(silu_ready, 1)
                    elif kind == "ht":
                        u = HIDDEN + i
                        act.wait_ge(gt_done, it * GT_USES + u + 1 + START)
                        A_.copy(hidT[:, i % 2].rearrange("p k s -> p (k s)"), half(turn_bank(u), 0))\
                          .then_inc(gt_taken[u % 2], 1)
                    elif kind == "d":
                        act.wait_ge(down_done, it * EPG + i + 1)
                        act.sem_inc(moe_freed["scalar"], 1)
                        A_.copy(y_exp[:, i % 2, 0, :], bank[2][:]).then_inc(y_taken[0], 1)

            residual_squares(2, acc_done, rounds * (N_EXPERTS * 8) + START)
            act.wait_ge(ms_ready, 5)
            A_.activation(stat[:, 8:10], stat[:, 4:6], ACT.Sqrt).then_inc(rms_ready, 1)

        @block.vector
        def _(dve):
            V = nc.vector
            chained, hi_n = [0], [0]

            def chain(ins):
                chained[0] += 1
                ins.then_inc(dve_chain, 1)
                dve.wait_ge(dve_chain, chained[0])

            def turn_lo(u0, dst_lo, dst_hi, gain=None):
                for c in range(KD):
                    if c % 2 == 0:
                        hi_n[0] += 2
                        dve.wait_ge(hi_written, hi_n[0])
                    u = u0 + c // 2
                    ins = V.scalar_tensor_tensor(out=dst_lo[:, c, :], in0=half(turn_bank(u), c % 2),
                                                 scalar=1.0 if gain is None else pcol[:, gain + c:gain + c + 1],
                                                 in1=dst_hi[:, c, :].bitcast(f32),
                                                 op0=ALU.mult, op1=ALU.subtract)
                    ins.then_inc(lo_written if c % 2 == 0 else turn_taken[u % 2], 1)

            def turn_copy(u0, dst):
                for u in range(u0, u0 + KC // 2, 2):
                    dve.wait_ge(turned, u + 1)
                    c = 2 * (u - u0)
                    V.tensor_copy(dst[:, c:c + 2, :], turn_bank(u)[:].rearrange("p (c s) -> p c s", c=2))\
                     .then_inc(turn_taken[u % 2], 1)

            def inverse_rms(lo, n, width, count):
                V.tensor_scalar(stat[:, lo + 4:lo + 4 + n], stat[:, lo:lo + n], 1.0 / width, EPS,
                                ALU.mult, ALU.add).then_inc(ms_ready, 1)
                dve.wait_ge(rms_ready, count)
                chain(V.reciprocal(stat[:, lo + 8:lo + 8 + n], stat[:, lo + 8:lo + 8 + n]))

            dve.wait_ge(params_in, 16 * 6)
            dve.wait_ge(aux_done, U_PARAMS + 1)
            V.tensor_copy(pcol[:], aux_bank(U_PARAMS)[:, 0:96]).then_inc(params_ready, 1)
            dve.wait_ge(params_ready, 1)
            dve.sem_inc(aux_taken[U_PARAMS % 2], 1)
            for k, src in ((0, x_tok), (2, mem_tok)):
                dve.wait_ge(sq_ready, k + 2)
                inverse_rms(k, TT, D, k // 2 + 1)
                for t in range(TT):
                    V.tensor_scalar(src[:, t, :], src[:, t, :], stat[:, 8 + k + t:9 + k + t], None, ALU.mult)\
                     .then_inc(normed, 1)

            def split_lo(ph, q, it):
                n = ph.q0 + q + SPLIT_SLOTS
                if isinstance(it, int) and n + it * ph.per >= TOTAL_Q:
                    return
                slot = n // 2 % RAW_SLOTS
                dve.wait_ge(hi_split, n + 1 + it * ph.per)
                V.tensor_tensor(w_lo[:, n % SPLIT_SLOTS, :], raw[:, slot, n % 2 * 1024:n % 2 * 1024 + 1024],
                                w_hi[:, n % SPLIT_SLOTS, :].bitcast(f32), ALU.subtract).then_inc(lo_split, 1)

            def run(name, take):
                ph = PH[name]
                with rounds_of(dve, ph.iters) as it:
                    q = 0
                    for jb, granules in enumerate(ph.granules):
                        for _ in range(granules):
                            split_lo(ph, q, it)
                            q += 1
                        dve.wait_ge(mm_done, ph.q0 + q + it * ph.per)
                        take(ph, jb, it)

            def store_tile1(dst, col=0):
                def take(ph, jb, it):
                    V.tensor_copy(dst[:, 1, bass.ds(it * 2 * BLK + col + jb * BLK, BLK)], pair[jb % 2][1][:])\
                     .then_inc(pair_taken[jb % 2], 1)
                return take

            def branch(first, adds):
                def take(ph, jb, it):
                    if jb % 2 == 0:
                        return
                    done = ph.j0 + jb - 1 + it * ph.jobs
                    dve.wait_ge(pair_taken[0], done + 2)
                    for t in range(TT):
                        cols = bass.ds(it * (ph.jobs // 2) * BLK + jb // 2 * BLK, BLK)
                        if first:
                            V.tensor_tensor(merged[:, t, cols], sig[:, t, :], pair[1][t][:], ALU.mult)\
                             .then_inc(pair_taken[1], 1)
                            continue
                        dve.wait_ge(merged_done, adds + jb // 2 * 2 + it * ph.jobs)
                        V.tensor_tensor(gated[:, t, :], sig[:, t, :], pair[1][t][:], ALU.mult)\
                         .then_inc(pair_taken[1], 1)
                        dve.wait_ge(pair_taken[1], done + t + 1)
                        V.tensor_tensor(merged[:, t, cols], merged[:, t, cols], gated[:, t, :], ALU.add)\
                         .then_inc(merged_done, 1)
                return take

            for n in range(SPLIT_SLOTS):
                dve.wait_ge(hi_split, n + 1)
                V.tensor_tensor(w_lo[:, n, :], raw[:, n // 2, n % 2 * 1024:n % 2 * 1024 + 1024],
                                w_hi[:, n, :].bitcast(f32), ALU.subtract).then_inc(lo_split, 1)
            turn_lo(T_H, h_lo, h_hi, G_MIX)
            turn_lo(T_MEM, y_lo, y_hi, G_MEM)

            run("mem_kv", store_tile1(kv))
            run("mem_q", store_tile1(mq))

            turn_copy(T_MEMK, kT[:])
            turn_copy(T_MEMQ, qT[:])

            def row_max(h):
                u, k = U_MEM["s", h], 16 + 2 * h
                dve.wait_ge(aux_done, u + 1)
                chain(V.reduce_max(stat[:, k:k + 2].unsqueeze(2),
                                   aux_bank(u)[:].rearrange("p (t m) -> p t m", t=TT), AX.X))
                V.tensor_scalar(stat[:, k:k + 2], stat[:, k:k + 2], -DK ** -0.5, None, ALU.mult)\
                 .then_inc(max_ready, 1)

            def normalise(h):
                k = 24 + 2 * h
                dve.wait_ge(prob_raw, TT * h + TT)
                dve.sem_inc(aux_taken[U_MEM["s", h] % 2], 1)
                chain(V.reciprocal(stat[:, k:k + 2], stat[:, k:k + 2]))
                for t in range(TT):
                    V.tensor_scalar(prob[:, h, t, :], prob[:, h, t, :], stat[:, k + t:k + t + 1], None, ALU.mult)\
                     .then_inc(prob_ready, 1)

            def memory_out(h):
                u = T_PROB + h
                dve.wait_ge(turned, u + 1)
                V.tensor_copy(probT[:, h], turn_bank(u)[:].rearrange("p (c s) -> p c s", c=2))\
                 .then_inc(turn_taken[u % 2], 1)
                u = U_MEM["y", h]
                hi_n[0] += 1
                dve.wait_ge(hi_written, hi_n[0])
                V.tensor_tensor(y_lo[:, 2 * h:2 * h + 2, :], aux_bank(u)[:].rearrange("p (c s) -> p c s", c=2),
                                y_hi[:, 2 * h:2 * h + 2, :].bitcast(f32), ALU.subtract)\
                 .then_inc(aux_taken[u % 2], 1)

            for kind, h in MEM_ORDER:
                if kind == "s":
                    row_max(h)
                else:
                    if h == 0:
                        normalise(0)
                    memory_out(h)
                    if h < HEADS - 1:
                        normalise(h + 1)
            run("branch_m", branch(True, 0))
            dve.wait_ge(a_lr_ready, 1)
            dve.sem_inc(aux_taken[U_GA % 2], 1)
            for i in range(KC // 2):
                dve.wait_ge(pre_ready, 2 * i + 2)
                dve.sem_inc(aux_taken[(U_A2 + i) % 2], 1)
            run("gla_qk", store_tile1(gqk))
            dve.wait_ge(soft_ready, 1)
            chain(V.scalar_tensor_tensor(out=dec_k[:], in0=dec_k[:], scalar=0.0, in1=dec_end[:],
                                         op0=ALU.min, op1=ALU.subtract))
            for c in range(KC):
                ins = V.tensor_tensor_scan(dec_q[:, c, :], chunk_keep[:], dec_k[:, c, :], 0.0, ALU.mult, ALU.add)
                if c < KC - 1:
                    ins.then_inc(dve_chain, 1)
                    chained[0] += 1
            chain(ins)
            run("gla_v", store_tile1(gv))
            sums = dec_q[:].rearrange("p c (n s) -> p (c n) s", s=CH)
            last = decay_last[:].rearrange("p c n -> p (c n)").unsqueeze(2)
            chain(V.tensor_copy(last, sums[:, :, CH - 1:CH]))
            V.tensor_tensor(dec_end[:].rearrange("p c (n s) -> p (c n) s", s=CH), sums,
                            last.to_broadcast([P, KC * NCH, CH]), ALU.subtract).then_inc(decay_sum_ready, 1)
            dve.wait_ge(decay_ready, 4)
            for c in range(KC):
                u = T_GQ + c // 2
                dve.wait_ge(turned, u + 1)
                V.scalar_tensor_tensor(out=dec_q[:, c, :], in0=half(turn_bank(u), c % 2), scalar=DK ** -0.5,
                                       in1=dec_q[:, c, :], op0=ALU.mult, op1=ALU.mult)\
                 .then_inc(dve_chain if c % 2 == 0 else turn_taken[u % 2], 1)
                chained[0] += 1 - c % 2
            for c in range(KC):
                u = T_GK + c // 2
                dve.wait_ge(turned, u + 1)
                chain(V.tensor_tensor(dec_k[:, c, :], half(turn_bank(u), c % 2), dec_k[:, c, :], ALU.mult))
                V.tensor_tensor(dec_end[:, c, :], half(turn_bank(u), c % 2), dec_end[:, c, :], ALU.mult)\
                 .then_inc(dve_chain if c % 2 == 0 else turn_taken[u % 2], 1)
                chained[0] += 1 - c % 2
            turned_before(dve, T_YB)

            def chunk_decay(n):
                return decay_last[:, :, n:n + 1].to_broadcast([P, KC, CH])

            V.tensor_tensor(q_far[:, :, 0:CH], dec_q[:, :, 2 * CH:3 * CH], chunk_decay(1), ALU.mult)\
             .then_inc(dve_chain, 1)
            chained[0] += 1
            chain(V.tensor_tensor(q_skip[:], dec_q[:, :, 3 * CH:4 * CH], chunk_decay(2), ALU.mult))
            V.tensor_tensor(q_far[:, :, CH:], q_skip[:], chunk_decay(1), ALU.mult).then_inc(decayed_qk, 1)

            def scores_out(h):
                a = attT[h % 2]
                dve.wait_ge(att_done, h + 1)
                dve.wait_ge(att_masked, 2 if h < 2 else 2 + 2 * (h - 1))
                if h >= 2:
                    dve.wait_ge(o_done, 2 * (h - 1))
                V.tensor_copy(a[CH:, CH:S], bank[4 + h % 2][CH:, CH:S]).then_inc(att_upper_taken, 1)
                V.tensor_copy(a[CH:, S + CH:], bank[4 + h % 2][CH:, S + CH:3 * P]).then_inc(att_upper_taken, 1)

            def outputs_out(h):
                dve.wait_ge(o_done, 2 * h + 2)
                for t in range(TT):
                    dve.wait_ge(o_sq, 2 * h + t + 1)
                    V.tensor_copy(gv[:, t, h * DV:(h + 1) * DV], bank[6 + t][:]).then_inc(o_taken, 1)

            for h in range(HEADS):
                scores_out(h)
                if h >= 1:
                    outputs_out(h - 1)
            outputs_out(HEADS - 1)
            dve.wait_ge(o_sq, HEADS * TT)
            V.tensor_scalar(stat[:, 40:48], stat[:, 32:40], 1.0 / DV, EPS, ALU.mult, ALU.add)\
             .then_inc(ms_ready, 1)
            run("gla_r", store_tile1(gr))
            dve.wait_ge(rms_ready, 3)
            chain(V.reciprocal(stat[:, 48:56], stat[:, 48:56]))
            dve.wait_ge(o_taken, HEADS * TT)
            for t in range(TT):
                dve.wait_ge(swish_ready, t + 1)
                for h in range(HEADS):
                    cols = slice(h * DV, (h + 1) * DV)
                    k = 48 + 2 * h + t
                    V.scalar_tensor_tensor(out=gv[:, t, cols], in0=gv[:, t, cols], scalar=stat[:, k:k + 1],
                                           in1=gr[:, t, cols], op0=ALU.mult, op1=ALU.mult)\
                     .then_inc(yb_ready, 1)
            run("conv_cv", store_tile1(ccv))
            run("conv_b", store_tile1(cb))
            turn_lo(T_YB, y_lo, y_hi, G_GLA)
            turn_copy(T_U, uT[:, :, 2:])
            turn_copy(T_CB, cbT[:])
            run("branch_b", branch(False, 0))
            hi_n[0] += 1
            dve.wait_ge(hi_written, hi_n[0])
            V.tensor_tensor(y_lo[:, 0:KC, :], conv[:], y_hi[:, 0:KC, :].bitcast(f32), ALU.subtract)\
             .then_inc(y_ready, 1)
            run("branch_a", branch(False, 8))
            turn_lo(T_MERGED, h_lo, h_hi)

            def add_residual(ph, jb, it):
                if jb == 0 and ph is PH["out_a"]:
                    dve.wait_ge(x_again, 16)
                n = (ph.j0 - PH["out_a"].j0 + jb)
                for t in range(TT):
                    dst = x2[:, t, n * BLK:(n + 1) * BLK]
                    V.tensor_tensor(dst, pair[jb % 2][t][:], dst, ALU.add).then_inc(pair_taken[jb % 2], 1)

            run("out_a", add_residual)
            run("out_b", add_residual)
            for i in range(2):
                dve.wait_ge(pair_taken[i], PH["out_b"].j_end)
            dve.sem_inc(residual_ready, 1)

            dve.wait_ge(sq_ready, 6)
            V.tensor_scalar(stat[:, 4:6], stat[:, 0:2], 1.0 / D, EPS, ALU.mult, ALU.add).then_inc(ms_ready, 1)
            dve.wait_ge(rms_ready, 4)
            chain(V.reciprocal(stat[:, 8:10], stat[:, 8:10]))
            for t in range(TT):
                V.tensor_scalar(xn[:, t, :], x2[:, t, :], stat[:, 8 + t:9 + t], None, ALU.mult).then_inc(normed, 1)
            for u in range(0, KD // 2, 2):
                dve.wait_ge(turned, T_XN + u + 1)
                for c in (2 * u, 2 * u + 1):
                    V.tensor_scalar(hT[:, c, :], half(turn_bank(u), c % 2), pcol[:, G_FFN + c:G_FFN + c + 1],
                                    None, ALU.mult).then_inc(dve_chain if c % 2 == 0 else turn_taken[0], 1)
                chained[0] += 1
            dve.wait_ge(aux_done, U_LOGIT + 1)
            V.tensor_copy(logitT[:], aux_bank(U_LOGIT)[0:N_GROUPS + N_EXPERTS, 0:S])\
             .then_inc(aux_taken[U_LOGIT % 2], 1)
            dve.wait_ge(turned, T_ROUTE + 1)
            NE = N_GROUPS + N_EXPERTS
            logit = rt[:, 30:32, :].rearrange("p a b -> p (a b)")[:, 0:TT * NE].rearrange("p (t e) -> p t e", e=NE)
            V.tensor_copy(logit, turn_bank(T_ROUTE)[:, 0:TT * NE].rearrange("p (t e) -> p t e", e=NE))\
             .then_inc(turn_taken[T_ROUTE % 2], 1)
            dve.wait_ge(turn_taken[T_ROUTE % 2], T_ROUTE // 2 + 1)
            dve.wait_ge(consts_made, 2)

            def four(k):
                return rt[:, k, 0:8].rearrange("p (t e) -> p t e", e=4)

            def one(k):
                return rt[:, k, 0:2].unsqueeze(2)

            def wide(k):
                return one(k).to_broadcast([P, TT, 4])

            def sixteen(k):
                return rt[:, k, 0:32].rearrange("p (t g e) -> p t g e", g=N_GROUPS, e=EPG)

            rank = rt[:, 0, 0:4].unsqueeze(1).to_broadcast([P, TT, 4])

            def softmax(src, dst, n):
                chain(V.reduce_max(one(1), src, AX.X))
                V.tensor_tensor(four(2), src, wide(1), ALU.subtract).then_inc(router_d, 1)
                dve.wait_ge(router_exp, n)
                chain(V.tensor_reduce(one(4), four(3), AX.X, ALU.add))
                chain(V.reciprocal(one(5), one(4)))
                chain(V.tensor_tensor(dst, four(3), wide(5), ALU.mult))

            def first_largest(src, best, pick):
                chain(V.reduce_max(one(best), src, AX.X))
                chain(V.tensor_tensor(four(6), src, wide(best), ALU.is_equal))
                chain(V.tensor_tensor(four(7), four(6), rank, ALU.mult))
                chain(V.reduce_max(one(8), four(7), AX.X))
                chain(V.tensor_tensor(four(pick), four(7), wide(8), ALU.is_equal))

            softmax(logit[:, :, 0:N_GROUPS], four(9), 1)
            first_largest(four(9), 10, 11)
            picked = four(11).unsqueeze(3).to_broadcast([P, TT, N_GROUPS, EPG])
            chain(V.tensor_tensor(sixteen(12), logit[:, :, N_GROUPS:].rearrange("p t (g e) -> p t g e", e=EPG),
                                  picked, ALU.mult))
            chain(V.tensor_reduce(four(13), sixteen(12).rearrange("p t g e -> p t e g"), AX.X, ALU.add))
            softmax(four(13), four(14), 2)
            first_largest(four(14), 15, 16)
            chain(V.scalar_tensor_tensor(out=four(17), in0=four(16), scalar=-2.0, in1=four(14),
                                         op0=ALU.mult, op1=ALU.add))
            first_largest(four(17), 18, 19)
            chain(V.tensor_tensor(one(20), one(15), one(18), ALU.add))
            chain(V.reciprocal(one(20), one(20)))
            chain(V.tensor_tensor(one(21), one(15), one(20), ALU.mult))
            chain(V.tensor_tensor(one(22), one(18), one(20), ALU.mult))
            chain(V.tensor_tensor(four(23), four(16), wide(21), ALU.mult))
            chain(V.tensor_tensor(four(24), four(19), wide(22), ALU.mult))
            chain(V.tensor_tensor(four(23), four(23), four(24), ALU.add))
            chain(V.tensor_tensor(four(23), four(23), wide(10), ALU.mult))
            chain(V.tensor_tensor(four(25), four(16), four(19), ALU.add))
            WEIGHT, CHOSEN, PLACE = 26, 27, 28
            for src, dst in ((23, WEIGHT), (25, CHOSEN)):
                chain(V.tensor_tensor(sixteen(dst), four(src).unsqueeze(2).to_broadcast([P, TT, N_GROUPS, EPG]),
                                      picked, ALU.mult))
            dve.sem_inc(route_ready, 1)
            dve.wait_ge(pos_done, 1)
            places = bank[6][:, 0:48]
            chain(V.tensor_scalar(rt[:, PLACE, :], rt[:, CHOSEN, :], -1024.0, 1024.0, ALU.mult, ALU.add))
            chain(V.tensor_tensor(rt[:, PLACE, :], rt[:, PLACE, :], places[:, 0:32], ALU.add))
            longest, more = rt[:, 29, 0:1], rt[:, 29, 1:4]
            chain(V.reduce_max(longest, places[:, 32:48], AX.X))
            for k in range(1, S // SLOTS):
                chain(V.tensor_scalar(more[:, k - 1:k], longest, float(SLOTS * k), None, ALU.is_gt))
            chain(V.tensor_reduce(rt[:, 29, 4:5], more, AX.X, ALU.add))
            V.tensor_scalar(n_rounds[:], rt[:, 29, 4:5], 1.0, None, ALU.add).then_inc(rounds_ready, 1)
            dve.wait_ge(rounds_ready, 1)
            for started in (gt_taken[0], y_taken[1], hid_ready, acc_done):
                dve.sem_inc(started, START)
            rounds = dve.value_load(n_rounds[0:1, 0:1], min_val=1, max_val=S // SLOTS)

            place = rt[:, PLACE, :].rearrange("p (t e) -> p t e", e=N_EXPERTS)
            weight = rt[:, WEIGHT, :].rearrange("p (t e) -> p t e", e=N_EXPERTS)
            with dve.Fori(0, rounds) as r:
                with dve.Fori(0, N_GROUPS) as g:
                    it = r * N_GROUPS + g
                    dve.wait_ge(gt_done, it * GT_USES + START)
                    experts = bass.ds(g * EPG, EPG)
                    for t in range(TT):
                        V.tensor_tensor(disp[:, t, :].rearrange("p (e s) -> p e s", s=SLOTS),
                                        slot_no[:].unsqueeze(1).to_broadcast([P, EPG, SLOTS]),
                                        place[:, t, experts].unsqueeze(2).to_broadcast([P, EPG, SLOTS]),
                                        ALU.is_equal).then_inc(disp_ready, 1)
                    dve.wait_ge(disp_ready, it * TT + TT)
                    for t in range(TT):
                        for side in range(2):
                            V.tensor_tensor(disp_w[:, t, :, side * SLOTS:(side + 1) * SLOTS],
                                            disp[:, t, :].rearrange("p (e s) -> p e s", s=SLOTS),
                                            weight[:, t, experts].unsqueeze(2).to_broadcast([P, EPG, SLOTS]),
                                            ALU.mult).then_inc(dispw_ready, 1)
                    for u in range(0, KD // 2, 2):
                        dve.wait_ge(gt_done, it * GT_USES + u + 1 + START)
                        for c in (2 * u, 2 * u + 1):
                            V.tensor_scalar(hT[:, c, :], half(turn_bank(u), c % 2),
                                            pcol[:, G_FFN + c:G_FFN + c + 1], None, ALU.mult)\
                             .then_inc(gathered if c % 2 == 0 else gt_taken[0], 1)
                    for i in range(0, EPG, 2):
                        u = BACK + i // 2
                        dve.wait_ge(gt_done, it * GT_USES + u + 1 + START)
                        V.tensor_copy(dispT[:, i:i + 2, :], turn_bank(u)[:].rearrange("p (e s) -> p e s", e=2))\
                         .then_inc(gt_taken[u % 2], 1)
                    for kind, i in MOE_ORDER:
                        if kind == "gu":
                            dve.wait_ge(silu_ready, it * EPG + i + 1)
                            if i >= 2:
                                dve.wait_ge(gt_done, it * GT_USES + HIDDEN + i - 1 + START)
                            V.tensor_tensor(hid[SLOTS:, i % 2, :], act_gate[SLOTS:, :], bank[i % 2][SLOTS:, :], ALU.mult)\
                             .then_inc(hid_ready, 1)
                        elif kind == "d":
                            dve.wait_ge(down_done, it * EPG + i + 1)
                            V.tensor_copy(y_exp[:, i % 2, 1, :], bank[3][:]).then_inc(y_taken[1], 1)
                        elif kind == "c":
                            for k in range(8):
                                n, t = k // 4 * 2 + k % 2, k // 2 % 2
                                dve.wait_ge(comb_done, it * 32 + 8 * i + k + 1)
                                dve.wait_ge(acc_done, it * 32 + 8 * i + START)
                                dst = x2[:, t, n * BLK:(n + 1) * BLK]
                                V.tensor_tensor(dst, dst, bank[6 + k % 2][:], ALU.add).then_inc(acc_done, 1)
                dve.wait_ge(disp_ready, r * (N_GROUPS * TT) + N_GROUPS * TT)
                V.tensor_scalar(rt[:, PLACE, :], rt[:, PLACE, :], -float(SLOTS), None, ALU.add)\
                 .then_inc(pos_done, 1)
                dve.wait_ge(pos_done, r + 2)

            dve.wait_ge(sq_ready, 8)
            V.tensor_scalar(stat[:, 4:6], stat[:, 0:2], 1.0 / D, EPS, ALU.mult, ALU.add).then_inc(ms_ready, 1)
            dve.wait_ge(rms_ready, 5)
            chain(V.reciprocal(stat[:, 8:10], stat[:, 8:10]))
            dve.wait_ge(gfin_in, 16)
            for t in range(TT):
                V.scalar_tensor_tensor(out=fin[:, t, :], in0=x2[:, t, :], scalar=stat[:, 8 + t:9 + t],
                                       in1=g_fin[:], op0=ALU.mult, op1=ALU.mult).then_inc(stored, 1)

        @block.tensor
        def _(pe):
            T = nc.tensor

            def turn(u0, n, src, col=0):
                for c in range(n):
                    u = u0 + c // 2
                    if c % 2 == 0 and u >= 2:
                        pe.wait_ge(turn_taken[u % 2], u // 2)
                    for t in range(TT):
                        ins = T.transpose(half(turn_bank(u), c % 2)[:, t * P:(t + 1) * P],
                                          src[:, t, col + c * P:col + (c + 1) * P], ident[:])
                    if c % 2:
                        ins.then_inc(turned, 1)

            def aux_free(u):
                if u >= 2:
                    pe.wait_ge(aux_taken[u % 2], u // 2)
                return aux_bank(u)

            def multiply(name, lhs):
                ph = PH[name]
                with rounds_of(pe, ph.iters) as it:
                    q = 0
                    for jb, granules in enumerate(ph.granules):
                        hi, lo = lhs[jb % len(lhs)]
                        pe.wait_ge(pair_taken[jb % 2], (ph.j0 + jb) // 2 * 2 + it * ph.jobs)
                        for g in range(granules):
                            n = ph.q0 + q
                            pe.wait_ge(lo_split, n + 1 + it * ph.per)
                            for c in range(2):
                                k = 2 * g + c
                                wh = w_hi[:, n % SPLIT_SLOTS, c * BLK:(c + 1) * BLK]
                                wl = w_lo[:, n % SPLIT_SLOTS, c * BLK:(c + 1) * BLK]
                                for t in range(TT):
                                    acc = pair[jb % 2][t][:]
                                    tok = slice(t * P, (t + 1) * P)
                                    last = k == 2 * granules - 1
                                    T.matmul(acc, hi[:, k, tok], wh, start=k == 0, stop=False)
                                    T.matmul(acc, hi[:, k, tok], wl, start=False, stop=False)
                                    ins = T.matmul(acc, lo[:, k, tok], wh, start=False, stop=last)
                            ins.then_inc(mm_done, 1)
                            q += 1

            H, Y = (h_hi, h_lo), (y_hi, y_lo)
            pe.wait_ge(consts_made, 1)
            pe.wait_ge(params_in, 16 * 6)
            T.transpose(aux_bank(U_PARAMS)[:, 0:96], prow[:], ident[0:96, 0:96]).then_inc(aux_done, 1)
            pe.wait_ge(normed, TT)
            turn(T_H, KD, x_tok)
            pe.wait_ge(normed, 2 * TT)
            turn(T_MEM, KD, mem_tok)
            turned_before(pe, T_MEMK)
            multiply("mem_kv", [Y])
            multiply("mem_q", [H])

            for p in range(2):
                pe.wait_ge(pair_taken[p], PH["mem_q"].j_end)
            turn(T_MEMK, KC, kv)
            turn(T_MEMQ, KC, mq)
            turned_before(pe, T_PROB)
            for kind, h in MEM_ORDER:
                acc = aux_free(U_MEM[kind, h])
                if kind == "s":
                    for t in range(TT):
                        for i in range(2):
                            ins = T.matmul(half(acc, t), qT[:, 2 * h + i, t * P:(t + 1) * P], kT[:, 2 * h + i, :],
                                           start=i == 0, stop=i == 1)
                    ins.then_inc(aux_done, 1)
                    continue
                pe.wait_ge(prob_ready, TT * h + TT)
                turn(T_PROB + h, TT, prob[:, h])
                turned_before(pe, T_PROB + h + 1)
                for i in range(2):
                    col = CONV + h * DK + i * P
                    for m in range(TT):
                        ins = T.matmul(half(acc, i), kv[:, m, col:col + P], probT[:, h, m, :],
                                       start=m == 0, stop=m == 1)
                ins.then_inc(aux_done, 1)
            aux_before(pe, U_GA)
            multiply("branch_m", [H, Y])

            pe.wait_ge(h_full_ready, 1)
            pe.wait_ge(small_in, 48)
            acc = aux_free(U_GA)
            for c in range(KD):
                ins = T.matmul(acc[0:RANK, 0:S], w_ga[:, c, :], h_full[:, c, :], start=c == 0, stop=c == KD - 1)
            ins.then_inc(aux_done, 1)
            pe.wait_ge(a_lr_ready, 1)
            pe.wait_ge(a2_in, 16)
            for c in range(KC):
                if c % 2 == 0:
                    acc = aux_free(U_A2 + c // 2)
                ins = T.matmul(half(acc, c % 2), w_a2[:, c * P:(c + 1) * P], a_lr[:], start=True, stop=True)
                if c % 2:
                    ins.then_inc(aux_done, 1)
            multiply("gla_qk", [H])
            multiply("gla_v", [H])

            turn(T_GQ, KC, gqk)
            turn(T_GK, KC, gqk, col=CONV)
            for p in range(2):
                pe.wait_ge(pair_taken[p], PH["gla_v"].j_end)
            pe.wait_ge(decayed_qk, 1)

            def scores(h):
                att = bank[4 + h % 2]
                if h >= 2:
                    pe.wait_ge(att_lower_taken, h - 1)
                    pe.wait_ge(att_upper_taken, 2 * (h - 1))
                blocks = []
                for n in range(NCH):
                    part = slice(n % 2 * CH, n % 2 * CH + CH)
                    base_col = 0 if n < 2 else P
                    cols = lambda a, b: slice(base_col + a * CH, base_col + b * CH)
                    keys = slice(n * CH, (n + 1) * CH)
                    blocks.append((part, cols(n, n + 1), dec_k, keys, dec_q, slice(n * CH, (n + 1) * CH)))
                    if n + 1 < NCH:
                        blocks.append((part, cols(n + 1, n + 2), dec_end, keys, dec_q,
                                       slice((n + 1) * CH, (n + 2) * CH)))
                    if n == 0:
                        blocks.append((part, cols(2, 4), dec_end, keys, q_far, slice(0, 2 * CH)))
                    if n == 1:
                        blocks.append((part, cols(3, 4), dec_end, keys, q_skip, slice(0, CH)))
                for part, cols, k_side, keys, q_side, queries in blocks:
                    for i in range(2):
                        ins = T.matmul(att[part, cols], k_side[:, 2 * h + i, keys],
                                       q_side[:, 2 * h + i, queries], start=i == 0, stop=i == 1)
                ins.then_inc(att_done, 1)

            def outputs(h):
                pe.wait_ge(att_masked, 2 + 2 * (h + 1))
                if h >= 1:
                    pe.wait_ge(o_taken, 2 * h)
                    pe.wait_ge(o_sq, 2 * h)
                a, cols = attT[h % 2], slice(h * DV, (h + 1) * DV)
                T.matmul(bank[6][:], a[:, 0:P], gv[:, 0, cols], start=True, stop=True).then_inc(o_done, 1)
                T.matmul(bank[7][:], a[:, P:S], gv[:, 0, cols], start=True, stop=False)
                T.matmul(bank[7][:], a[:, S:], gv[:, 1, cols], start=False, stop=True).then_inc(o_done, 1)

            aux_before(pe, U_LOGIT)
            for h in range(HEADS):
                scores(h)
                if h >= 1:
                    outputs(h - 1)
            outputs(HEADS - 1)
            multiply("gla_r", [H])
            multiply("conv_cv", [H])
            multiply("conv_b", [H])
            pe.wait_ge(yb_ready, HEADS * TT)
            pe.wait_ge(att_lower_taken, HEADS)
            pe.wait_ge(att_upper_taken, 2 * HEADS)
            turn(T_YB, KD, gv)
            pe.wait_ge(conv_u, TT)
            for p in range(2):
                pe.wait_ge(pair_taken[p], PH["conv_b"].j_end)
            turn(T_U, KC, ccv)
            turn(T_CB, KC, cb)
            multiply("branch_b", [H, Y])
            pe.wait_ge(y_ready, 1)
            multiply("branch_a", [H, Y])
            pe.wait_ge(merged_done, 16)
            turn(T_MERGED, KD, merged)
            turned_before(pe, T_XN)
            multiply("out_a", [H])
            multiply("out_b", [H])

            pe.wait_ge(normed, 3 * TT)
            turn(T_XN, KD, xn)
            turned_before(pe, T_ROUTE)
            pe.wait_ge(o_taken, HEADS * TT)
            pe.wait_ge(o_sq, HEADS * TT)
            NE = N_GROUPS + N_EXPERTS
            for c in range(KD):
                ins = T.matmul(aux_bank(U_LOGIT)[0:NE, 0:S], w_rt[:, c, :], hT[:, c, :], start=c == 0, stop=c == KD - 1)
            ins.then_inc(aux_done, 1)
            aux_before(pe, U_LOGIT + 1)
            for t in range(TT):
                ins = T.transpose(turn_bank(T_ROUTE)[:, t * NE:(t + 1) * NE], logitT[:, t * P:(t + 1) * P],
                                  ident[0:NE, 0:NE])
            ins.then_inc(turned, 1)
            pe.wait_ge(route_ready, 1)
            CHOSEN = 27
            chosen = [rt[:, CHOSEN, t * 16:(t + 1) * 16] for t in range(TT)]
            T.matmul(bank[6][:, 0:16], tri[:], chosen[0], start=True, stop=True)
            T.matmul(bank[6][:, 16:32], ones[:], chosen[0], start=True, stop=False)
            T.matmul(bank[6][:, 16:32], tri[:], chosen[1], start=False, stop=True)
            T.matmul(bank[6][:, 32:48], ones[:], chosen[0], start=True, stop=False)
            T.matmul(bank[6][:, 32:48], ones[:], chosen[1], start=False, stop=True).then_inc(pos_done, 1)

            pe.wait_ge(rounds_ready, 1)
            pe.sem_inc(gt_done, START)
            rounds = pe.value_load(n_rounds[0:1, 0:1], min_val=1, max_val=S // SLOTS)
            turned_before(pe, T_ROUTE + 1)
            with pe.Fori(0, rounds) as r, pe.Fori(0, N_GROUPS) as g:
                it = r * N_GROUPS + g

                def gt_bank(u):
                    pe.wait_ge(gt_taken[u % 2], it * (GT_USES // 2) + u // 2 + START)
                    return turn_bank(u)

                def ht_waits(i):
                    gt_bank(HIDDEN + i)
                    pe.wait_ge(hid_ready, it * EPG + i + 1 + START)

                pe.wait_ge(disp_ready, it * TT + TT)
                for c in range(KD):
                    if c % 2 == 0:
                        acc = gt_bank(GATHER + c // 2)
                    for t in range(TT):
                        ins = T.matmul(half(acc, c % 2), xn[:, t, c * P:(c + 1) * P], disp[:, t, :],
                                       start=t == 0, stop=t == 1)
                    if c % 2:
                        ins.then_inc(gt_done, 1)
                pe.wait_ge(dispw_ready, it * 4 + 4)
                for i in range(EPG):
                    if i % 2 == 0:
                        acc = gt_bank(BACK + i // 2)
                    for t in range(TT):
                        ins = T.transpose(half(acc, i % 2)[:, t * P:(t + 1) * P], disp_w[:, t, i, :], ident[:])
                    if i % 2:
                        ins.then_inc(gt_done, 1)
                for s in range(2):
                    pe.wait_ge(gt_taken[s], it * (GT_USES // 2) + HIDDEN // 2 + START)
                n = 0
                for kind, i in MOE_ORDER:
                    rows = [slice(0, SLOTS), slice(SLOTS, P)]
                    if kind == "gu":
                        acc = bank[i % 2]
                        if i >= 2:
                            pe.wait_ge(hid_ready, it * EPG + i - 1 + START)
                        else:
                            pe.wait_ge(hid_ready, it * EPG + START)
                        for l in range(4):
                            for side in range(2):
                                m = n + side
                                pe.wait_ge(moe_loaded[m % MOE_SLOTS], it * (48 // MOE_SLOTS * 16) + 16 * (m // MOE_SLOTS + 1))
                            for k in range(4):
                                c = 4 * l + k
                                if c == KD - 1 and i == 1:
                                    ht_waits(0)
                                for side in range(2):
                                    w = moe_raw[:, (n + side) % MOE_SLOTS, k * BLK:(k + 1) * BLK]
                                    ins = T.matmul(acc[rows[side], :], hT[:, c, i * SLOTS:(i + 1) * SLOTS], w,
                                                   start=c == 0, stop=c == KD - 1)
                                    if k == 3 and l * 2 + side < 7:
                                        ins.then_inc(moe_freed["tensor"], 1)
                            n += 2
                        ins.then_inc(gu_done, 1)
                    elif kind == "ht":
                        slot = turn_bank(HIDDEN + i)
                        for k in range(KE):
                            ins = T.transpose(slot[:, k * SLOTS:(k + 1) * SLOTS], hid[SLOTS:, i % 2, k * P:(k + 1) * P],
                                              ident[SLOTS:, SLOTS:])
                        ins.then_inc(gt_done, 1)
                    elif kind == "d":
                        u = HIDDEN + i
                        pe.wait_ge(gt_taken[u % 2], it * (GT_USES // 2) + u // 2 + 1 + START)
                        for b in range(2):
                            pe.wait_ge(y_taken[b], it * EPG + i + START)
                        for l in range(KE):
                            pe.wait_ge(moe_loaded[n % MOE_SLOTS], it * (48 // MOE_SLOTS * 16) + 16 * (n // MOE_SLOTS + 1))
                            for b in range(4):
                                w = moe_raw[:, n % MOE_SLOTS, b * BLK:(b + 1) * BLK]
                                ins = T.matmul(bank[2 + b // 2][rows[b % 2], :], hidT[:, i % 2, l, :], w,
                                               start=l == 0, stop=l == KE - 1)
                            ins.then_inc(moe_freed["tensor"] if l < KE - 1 else down_done, 1)
                            n += 1
                    elif kind == "c":
                        for b in range(2):
                            pe.wait_ge(y_taken[b], it * EPG + i + 1 + START)
                        for k in range(8):
                            b, t = k // 4 * 2 + k % 2, k // 2 % 2
                            if 8 * i + k >= 2:
                                pe.wait_ge(acc_done, it * 32 + 8 * i + k - 1 + START)
                            else:
                                pe.wait_ge(acc_done, it * 32 + START)
                            if k == 7 and i < EPG - 1:
                                ht_waits(i + 1)
                            T.matmul(bank[6 + k % 2][:], dispT[rows[b % 2], i, t * P:(t + 1) * P],
                                     y_exp[rows[b % 2], i % 2, b // 2, :], start=True, stop=True)\
                             .then_inc(comb_done, 1)


MOE_ORDER = [("gu", 0), ("gu", 1), ("ht", 0), ("d", 0), ("gu", 2), ("c", 0), ("ht", 1), ("d", 1),
             ("gu", 3), ("c", 1), ("ht", 2), ("d", 2), ("c", 2), ("ht", 3), ("d", 3), ("c", 3)]



def moe_frees():
    out, count = [], {"tensor": 0, "scalar": 0}
    for kind, _ in MOE_ORDER:
        for l in range({"gu": 8, "d": 4}.get(kind, 0)):
            by = "scalar" if l == {"gu": 7, "d": 3}[kind] else "tensor"
            count[by] += 1
            out.append((by, count[by]))
    return out, count


_INS = ["x", "mem", "norm_mix", "w_in", "conv_w", "gla_w_a2", "gla_b_a2", "gla_norm", "norm_mem",
        "w_mem_kv", "w_br_conv", "w_br_gla", "w_br_mem", "w_o", "norm_ffn", "w_router_group",
        "w_router_expert", "w_gate", "w_up", "w_down", "norm_final"]


def kernel(**inputs):
    import numpy as _np
    import concourse.bacc as _bacc
    from concourse import mybir as _mybir
    from concourse.bass_utils import run_bass_kernel_spmd as _run

    nc = _bacc.Bacc("TRN2", target_bir_lowering=False, num_devices=1)
    arrays, args = {}, []
    for name in _INS:
        a = _np.ascontiguousarray(inputs[name])
        arrays[f"in_{name}_dram"] = a
        args.append(nc.dram_tensor(f"in_{name}_dram", a.shape, _mybir.dt.from_np(a.dtype),
                                   kind="ExternalInput").ap())
    args.append(nc.dram_tensor("out_dram", (1, S, D), _mybir.dt.float32, kind="ExternalOutput").ap())
    hybrid_layer(nc, *args)
    r = _run(nc, [arrays], core_ids=[0])
    return r.results[0]["out_dram"]
```

```python
import concourse.bass as bass
from concourse import mybir
from contextlib import ExitStack, contextmanager

P = 128
S = 256
TT = S // P
D = 2048
KD = D // P
BLK = 512
CONV = 1024
KC = CONV // P
HEADS = 4
DK = 256
DV = 512
CH = 64
NCH = S // CH
RANK = 16
EPS = 1e-6
N_GROUPS = 4
EPG = 4
N_EXPERTS = 16
DE = 512
KE = DE // P
SLOTS = 64
IN_COLS = 16400
COL_CONV, COL_GQ, COL_GV, COL_GR = 0, 3072, 5120, 7168
COL_GA, COL_MQ, COL_GATE_A, COL_GATE_B, COL_GATE_M = 9216, 9232, 10256, 12304, 14352

RAW_SLOTS = 4
SPLIT_SLOTS = 4
MOE_SLOTS = 12
START = 1


class Phase:

    def __init__(self, iters, granules, q0, j0):
        self.iters, self.granules, self.q0, self.j0 = iters, granules, q0, j0
        self.per = sum(granules)
        self.jobs = len(granules)
        self.q_end = q0 + iters * self.per
        self.j_end = j0 + iters * self.jobs


def phases():
    out, q, j = {}, 0, 0
    for name, iters, granules in (
        ("mem_kv", 2, (8, 8)), ("mem_q", 1, (8, 8)), ("branch_m", 2, (8, 4, 8, 4)),
        ("gla_qk", 2, (8, 8)), ("gla_v", 2, (8, 8)), ("gla_r", 2, (8, 8)),
        ("conv_cv", 2, (8, 8)), ("conv_b", 1, (8, 8)), ("branch_b", 4, (8, 8)),
        ("branch_a", 2, (8, 4, 8, 4)), ("out_a", 1, (8, 8)), ("out_b", 1, (8, 8)),
    ):
        out[name] = Phase(iters, granules, q, j)
        q, j = out[name].q_end, out[name].j_end
    return out, q


@contextmanager
def rounds_of(eng, n):
    if n == 1:
        yield 0
    else:
        with eng.Fori(0, n) as it:
            yield it


def hybrid_layer(nc, x, mem, norm_mix, w_in, conv_w, gla_w_a2, gla_b_a2, gla_norm, norm_mem,
                 w_mem_kv, w_br_conv, w_br_gla, w_br_mem, w_o, norm_ffn, w_router_group,
                 w_router_expert, w_gate, w_up, w_down, norm_final, out):
    f32, f32r, i32 = mybir.dt.float32, mybir.dt.float32r, mybir.dt.int32
    ALU, ACT, AX = mybir.AluOpType, mybir.ActivationFunctionType, mybir.AxisListType
    PH, TOTAL_Q = phases()

    def k_major(w):
        return w.rearrange("(kc p) n -> p kc n", p=P)

    x_v = x[0].rearrange("(t p) d -> p t d", p=P)
    mem_v = mem[0].rearrange("(t p) d -> p t d", p=P)
    out_v = out[0].rearrange("(t p) d -> p t d", p=P)
    in_v, kv_v, o_v = k_major(w_in[0]), k_major(w_mem_kv[0]), k_major(w_o[0])
    bra_v, brb_v, brm_v = k_major(w_br_conv[0]), k_major(w_br_gla[0]), k_major(w_br_mem[0])
    gate_v = w_gate[0].rearrange("e (kc p) n -> p e kc n", p=P)
    up_v = w_up[0].rearrange("e (kc p) n -> p e kc n", p=P)
    down_v = w_down[0].rearrange("e (kc p) n -> p e kc n", p=P)

    KB = 1024
    base = (nc.sbuf_base + 31) // 32 * 32

    def at(name, kb, shape, dt=f32):
        return nc.alloc_sbuf_tensor_at(name, shape, dt, offset=base + int(kb * KB))

    ident = at("ident", 0, [P, P])
    pcol = at("pcol", 0.5, [P, 96])
    w_ga = at("w_ga", 1, [P, KD, RANK])
    w_rt = at("w_rt", 2, [P, KD, N_GROUPS + N_EXPERTS])
    chunk_keep = at("chunk_keep", 3.25, [P, S])
    decay_last = at("decay_last", 4.25, [P, KC, NCH])
    stat = at("stat", 4.5, [P, 64])
    n_rounds = at("n_rounds", 4.75, [P, 1], i32)
    merged = at("merged", 6, [P, TT, D])
    x2 = at("x2", 6, [P, TT, D])
    junk = at("junk", 6, [P, D])
    raw = at("raw", 22, [P, RAW_SLOTS, 4 * BLK])
    w_hi = at("w_hi", 54, [P, SPLIT_SLOTS, 2 * BLK], f32r)
    w_lo = at("w_lo", 70, [P, SPLIT_SLOTS, 2 * BLK], f32r)
    h_hi = at("h_hi", 86, [P, KD, S], f32r)
    h_lo = at("h_lo", 102, [P, KD, S], f32r)
    y_hi = at("y_hi", 118, [P, KD, S], f32r)
    y_lo = at("y_lo", 134, [P, KD, S], f32r)
    A, B, C = 150, 166, 182
    x_tok = at("x_tok", A, [P, TT, D])
    mem_tok = at("mem_tok", B, [P, TT, D])
    prow = at("prow", C, [96, P])
    kv = at("kv", A, [P, TT, D])
    mq = at("mq", B, [P, TT, CONV])
    kT = at("kT", B + 8, [P, KC, S])
    qT = at("qT", C, [P, KC, S])
    prob = at("prob", C + 8, [P, HEADS, TT, S])
    probT = at("probT", C + 16, [P, HEADS, TT, S])
    sig = at("sig", C, [P, TT, BLK])
    gated = at("gated", C + 4, [P, TT, BLK])
    gqk = at("gqk", A, [P, TT, D])
    gv = at("gv", B, [P, TT, D])
    w_a2 = at("w_a2", A, [RANK, CONV])
    a_lr = at("a_lr", A + 4, [RANK, S])
    h_full = at("h_full", B, [P, KD, S])
    dec_k = at("dec_k", C, [P, KC, S])
    dec_end = at("dec_end", C + 8, [P, KC, S])
    dec_q = at("dec_q", C + 16, [P, KC, S])
    q_far = at("q_far", A, [P, KC, 2 * CH])
    q_skip = at("q_skip", A + 4, [P, KC, CH])
    attT = [at(f"attT{i}", A + 6 + 1.5 * i, [P, 3 * P]) for i in range(2)]
    sq_junk = at("sq_junk", A + 9, [P, BLK])
    gr = at("gr", C, [P, TT, D])
    ccv = at("ccv", A, [P, TT, D])
    cb = at("cb", C + 16, [P, TT, CONV])
    uT = at("uT", B, [P, KC, S + 2])
    cbT = at("cbT", C + 8, [P, KC, S])
    conv = at("conv", A, [P, KC, S])
    conv_t = at("conv_t", A + 8, [P, S])
    xn = at("xn", 22, [P, TT, D])
    xn_lo = at("xn_lo", 22, [P, TT, D], f32r)
    hT = at("hT", 38, [P, KD, S])
    dispT = at("dispT", 54, [P, EPG // 2, S], f32r)
    disp = at("disp", 56, [P, TT, EPG * SLOTS], f32r)
    out_hi = at("out_hi", 58, [P, D // BLK, BLK], f32r)
    out_lo = at("out_lo", 66, [P, D // BLK, BLK], f32r)
    hidT = at("hidT", 74, [P, KE, 2 * SLOTS])
    act_gate = at("act_gate", 76, [P, BLK])
    hid = at("hid", 78, [P, EPG // 2, BLK])
    g_fin = at("g_fin", 82, [P, D])
    rt = at("rt", 90, [P, 32, TT * 16])
    slot_no = at("slot_no", 94, [P, SLOTS])
    place = at("place", 94.25, [P, TT, N_EXPERTS + EPG])
    weight = at("weight", 94.5, [P, TT, N_EXPERTS + EPG])
    group_w = at("group_w", 94.75, [P, TT, EPG])
    slot_w = at("slot_w", 94.875, [P, EPG // 2])
    xn_hi = at("xn_hi", 95, [P, TT, D], f32r)
    logitT = at("logitT", 1, [N_GROUPS + N_EXPERTS, S])
    tri = at("tri", 3.25, [P, P])
    ones = at("ones", 3.75, [P, P])
    fin = at("fin", 22, [P, TT, D])
    moe_raw = at("moe_raw", 111.75, [P, MOE_SLOTS, 4 * BLK])
    G_MIX, G_MEM, G_GLA, G_FFN, B_A2, W_CONV = 0, 16, 32, 48, 64, 72

    ctx = ExitStack()
    with ctx:
        bank = [ctx.enter_context(nc.psum_tensor(f"bank{i}", [P, BLK], f32)) for i in range(8)]
        pair = [bank[0:2], bank[2:4]]

        def turn_bank(u):
            return bank[4 + u % 2]

        def aux_bank(u):
            return bank[6 + u % 2]

        def half(b, i):
            return b[:, i * S:(i + 1) * S]

        def sem(name):
            return ctx.enter_context(nc.semaphore(name))

        consts_made = sem("consts_made")
        params_in = sem("params_in")
        x_in = [sem(f"x_in{t}") for t in range(TT)]
        mem_in = [sem(f"mem_in{t}") for t in range(TT)]
        small_in = sem("small_in")
        a2_in = sem("a2_in")
        x_again = sem("x_again")
        gfin_in, out_stored = sem("gfin_in"), sem("out_stored")
        raw_loaded = [sem(f"raw_loaded{i}") for i in range(RAW_SLOTS)]
        hi_split, lo_split = sem("hi_split"), sem("lo_split")
        mm_done = sem("mm_done")
        pair_taken = [sem(f"pair_taken{i}") for i in range(2)]
        sq_ready, ms_ready, rms_ready, normed = (sem("sq_ready"), sem("ms_ready"),
                                                 sem("rms_ready"), sem("normed"))
        turned = sem("turned")
        turn_taken = [sem(f"turn_taken{i}") for i in range(2)]
        aux_done = sem("aux_done")
        aux_taken = [sem(f"aux_taken{i}") for i in range(2)]
        hi_written, lo_written = sem("hi_written"), sem("lo_written")
        params_ready = sem("params_ready")
        act_chain, dve_chain, pool_chain = sem("act_chain"), sem("dve_chain"), sem("pool_chain")
        max_ready, prob_raw, prob_ready = sem("max_ready"), sem("prob_raw"), sem("prob_ready")
        h_full_ready, a_lr_ready = sem("h_full_ready"), sem("a_lr_ready")
        pre_ready, soft_ready, decay_sum_ready = (sem("pre_ready"), sem("soft_ready"),
                                                  sem("decay_sum_ready"))
        decay_ready, decayed_qk = sem("decay_ready"), sem("decayed_qk")
        att_done, att_masked = sem("att_done"), sem("att_masked")
        att_lower_taken, att_upper_taken = sem("att_lower_taken"), sem("att_upper_taken")
        o_done, o_sq, o_taken = sem("o_done"), sem("o_sq"), sem("o_taken")
        swish_ready, yb_ready = sem("swish_ready"), sem("yb_ready")
        conv_u, conv_in, conv_out = sem("conv_u"), sem("conv_in"), sem("conv_out")
        merged_done, residual_ready = sem("merged_done"), sem("residual_ready")
        y_ready = sem("y_ready")
        router_exp, router_d = sem("router_exp"), sem("router_d")
        route_ready, pos_done, rounds_ready = sem("route_ready"), sem("pos_done"), sem("rounds_ready")
        moe_loaded = [sem(f"moe_loaded{i}") for i in range(MOE_SLOTS)]
        moe_freed = {by: sem(f"moe_freed_by_{by}") for by in ("tensor", "scalar")}
        freed_loads, freed_in_group = moe_frees()
        disp_ready = sem("disp_ready")
        gt_done, gathered = sem("gt_done"), sem("gathered")
        gathered_w = sem("gathered_w")
        gt_taken = [sem(f"gt_taken{i}") for i in range(2)]
        gu_done, silu_ready, hid_ready = sem("gu_done"), sem("silu_ready"), sem("hid_ready")
        down_done = sem("down_done")
        hi_scaled, y_taken = sem("hi_scaled"), sem("y_taken")
        xn_hi_ready, xn_split = sem("xn_hi_ready"), sem("xn_split")
        comb_done = sem("comb_done")
        acc_done = sem("acc_done")
        stored = sem("stored")

        T_H, T_MEM, T_MEMK, T_MEMQ, T_PROB = 0, 8, 16, 20, 24
        T_GQ, T_GK, T_YB, T_U, T_CB, T_MERGED, T_XN, T_ROUTE = 28, 32, 36, 44, 48, 52, 60, 68
        U_PARAMS = 0
        MEM_ORDER = [("s", 0), ("s", 1), ("y", 0), ("s", 2), ("y", 1), ("s", 3), ("y", 2), ("y", 3)]
        U_MEM = {what: 1 + n for n, what in enumerate(MEM_ORDER)}
        U_GA, U_A2, U_LOGIT = 9, 10, 14
        GATHER, BACK, SLOT_W, HIDDEN, GT_USES = 0, 8, 9, 10, 12
        out_bank = [bank[b] for b in (2, 3, 6, 7)]

        def moe_slot(n):
            return (n + 1) % MOE_SLOTS

        def turned_before(eng, u):
            for s in range(2):
                eng.wait_ge(turn_taken[s], (u + 1 - s) // 2)

        def aux_before(eng, u):
            for s in range(2):
                eng.wait_ge(aux_taken[s], (u + 1 - s) // 2)

        block = ctx.enter_context(nc.Block())

        @block.sync
        def _(sp):
            vecs = ((norm_mix[0], 16, G_MIX), (norm_mem[0], 16, G_MEM), (gla_norm[0], 16, G_GLA),
                    (norm_ffn[0], 16, G_FFN), (gla_b_a2[0], 8, B_A2))
            sp.dma_start(x_tok[:, 0, :], x_v[:, 0, :]).then_inc(x_in[0], 16)
            sp.dma_start(x_tok[:, 1, :], x_v[:, 1, :]).then_inc(x_in[1], 16)
            for v, n, row in vecs:
                sp.dma_start(prow[row:row + n, :], v.rearrange("(a b) -> a b", b=P))\
                  .then_inc(params_in, 16)
            sp.dma_start(prow[W_CONV:W_CONV + 24, :],
                         conv_w[0].rearrange("k (c b) -> (k c) b", b=P)).then_inc(params_in, 16)
            for t in range(TT):
                sp.dma_start(mem_tok[:, t, :], mem_v[:, t, :]).then_inc(mem_in[t], 16)

            def load(ph, load_no, it, src, slots=1):
                n = ph.q0 // 2 + load_no
                if slots and not (isinstance(it, int) and n + it * ph.per // 2 < RAW_SLOTS):
                    sp.wait_ge(lo_split, 2 * (n - RAW_SLOTS) + 2 * slots + it * ph.per)
                sp.dma_start(raw[:, n % RAW_SLOTS, :].rearrange("p (k n) -> p k n", k=4), src)\
                  .then_inc(raw_loaded[n % RAW_SLOTS], 16)

            def load_columns(name, view, col, unrolled=False):
                ph = PH[name]
                for first in range(ph.iters if unrolled else 1):
                    with rounds_of(sp, 1 if unrolled else ph.iters) as i:
                        it = first if unrolled else i
                        off = it * 2 * BLK if isinstance(it, int) else sp.snap(it * (2 * BLK))
                        for jb in range(2):
                            for l in range(4):
                                load(ph, 4 * jb + l, it,
                                     view[:, 4 * l:4 * l + 4, bass.ds(off + (col + jb * BLK), BLK)])

            def load_branch(name, gate_col, branch_v):
                ph = PH[name]
                kl = [g // 2 for g in ph.granules]
                with rounds_of(sp, ph.iters) as it:
                    off = sp.snap(it * (ph.jobs // 2 * BLK))
                    n = 0
                    for jb in range(ph.jobs):
                        view, col = ((in_v, gate_col), (branch_v, 0))[jb % 2]
                        for l in range(kl[jb]):
                            load(ph, n, it, view[:, 4 * l:4 * l + 4,
                                                 bass.ds(off + (col + jb // 2 * BLK), BLK)],
                                 slots=2 if jb % 2 == 0 and l == kl[jb] - 1 else 0 if jb % 2 and l == 0 else 1)
                            n += 1

            load_columns("mem_kv", kv_v, 0, unrolled=True)
            load_columns("mem_q", in_v, COL_MQ)
            load_branch("branch_m", COL_GATE_M, brm_v)
            load_columns("gla_qk", in_v, COL_GQ)
            load_columns("gla_v", in_v, COL_GV)
            load_columns("gla_r", in_v, COL_GR)
            load_columns("conv_cv", in_v, COL_CONV + CONV)
            load_columns("conv_b", in_v, COL_CONV)
            load_branch("branch_b", COL_GATE_B, brb_v)
            load_branch("branch_a", COL_GATE_A, bra_v)
            load_columns("out_a", o_v, 0)
            load_columns("out_b", o_v, 2 * BLK)

            turned_before(sp, T_XN)
            for by in ("tensor", "scalar"):
                sp.sem_inc(moe_freed[by], freed_in_group[by])

            def expert_loads(group, per_group, in_dense=False):
                def load_moe(n, src):
                    by, count = freed_loads[n - MOE_SLOTS]
                    groups = 1 if n >= MOE_SLOTS else 0
                    sp.wait_ge(moe_freed[by], (per_group + groups) * freed_in_group[by] + count)
                    sp.dma_start(moe_raw[:, moe_slot(n), :].rearrange("p (k n) -> p k n", n=src.shape[-1]),
                                 src).then_inc(moe_loaded[n % MOE_SLOTS], 16)
                n = 0
                for kind, i in MOE_ORDER:
                    if kind not in ("gu", "d"):
                        continue
                    for l in range(4):
                        for side in range(2):
                            if kind == "gu":
                                e = bass.ds(group * EPG + i, 1)
                                load_moe(n, (gate_v, up_v)[side][:, e, 4 * l:4 * l + 4, :]
                                         .rearrange("p e k n -> p (e k) n"))
                            else:
                                e = bass.ds(group * EPG + (2 * i + side), 1)
                                load_moe(n, down_v[:, e, l:l + 1, :].rearrange("p e k n -> p (e k) n"))
                            n += 1
                            if in_dense and n == MOE_SLOTS - 1:
                                sp.wait_ge(mm_done, TOTAL_Q)

            with sp.Fori(0, N_GROUPS) as g:
                expert_loads(g, g, in_dense=True)
            sp.wait_ge(rounds_ready, 1)
            rounds = sp.value_load(n_rounds[0:1, 0:1], min_val=1, max_val=S // SLOTS)
            with sp.If(rounds > 1):
                with sp.Fori(1, rounds) as r:
                    with sp.Fori(0, N_GROUPS) as g:
                        expert_loads(g, r * N_GROUPS + g)
            for t in range(TT):
                sp.wait_ge(stored, t + 1)
                sp.dma_start(out_v[:, t, :], fin[:, t, :]).then_inc(out_stored, 16)
            sp.wait_ge(out_stored, 16 * TT)

        @block.gpsimd
        def _(pool):
            n = [0]

            def chain(ins):
                n[0] += 1
                ins.then_inc(pool_chain, 1)
                pool.wait_ge(pool_chain, n[0])

            chain(nc.gpsimd.memset(ident[:], 0.0))
            nc.gpsimd.affine_select(out=ident[:], in_=ident[:], compare_op=ALU.not_equal, fill=1.0, base=0,
                                    pattern=[[-1, P]], channel_multiplier=1).then_inc(consts_made, 1)
            chain(nc.gpsimd.memset(chunk_keep[:], 1.0))
            chain(nc.gpsimd.memset(chunk_keep[:].rearrange("p (n c) -> p n c", c=CH)[:, :, 0:1], 0.0))
            pool.dma_start(w_ga[:], in_v[:, :, COL_GA:COL_GA + RANK]).then_inc(small_in, 16)
            pool.dma_start(w_rt[:, :, 0:N_GROUPS], k_major(w_router_group[0])).then_inc(small_in, 16)
            pool.dma_start(w_rt[:, :, N_GROUPS:], k_major(w_router_expert[0])).then_inc(small_in, 16)
            turned_before(pool, T_GQ)
            aux_before(pool, U_GA)
            pool.dma_start(w_a2[:], gla_w_a2[0]).then_inc(a2_in, 16)
            nc.gpsimd.tensor_tensor(h_full[:], h_hi[:].bitcast(f32), h_lo[:].bitcast(f32), ALU.add)\
                     .then_inc(h_full_ready, 1)
            pool.wait_ge(decayed_qk, 1)
            for i in range(2):
                nc.gpsimd.memset(attT[i][:], 0.0).then_inc(att_masked, 1)
            for h in range(HEADS):
                pool.wait_ge(att_lower_taken, h + 1)
                pool.wait_ge(att_upper_taken, 2 * h + 2)
                a = attT[h % 2]
                nc.gpsimd.affine_select(out=a[:, 0:S], in_=a[:, 0:S], compare_op=ALU.is_ge, fill=0.0, base=0,
                                        pattern=[[1, S]], channel_multiplier=-1).then_inc(att_masked, 1)
                nc.gpsimd.affine_select(out=a[:, S:], in_=a[:, S:], compare_op=ALU.is_ge, fill=0.0, base=0,
                                        pattern=[[1, P]], channel_multiplier=-1).then_inc(att_masked, 1)
            pool.wait_ge(pair_taken[0], PH["conv_b"].j0)
            pool.wait_ge(pair_taken[1], PH["conv_b"].j0)
            for t in range(TT):
                nc.gpsimd.tensor_tensor(ccv[:, t, 0:CONV], ccv[:, t, 0:CONV], ccv[:, t, CONV:], ALU.mult)\
                         .then_inc(conv_u, 1)
            turned_before(pool, T_U)
            chain(nc.gpsimd.memset(uT[:, :, 0:2], 0.0))
            turned_before(pool, T_MERGED)
            for c in range(KC):
                tap = [pcol[:, W_CONV + k * KC + c:W_CONV + k * KC + c + 1] for k in range(3)]
                chain(nc.gpsimd.tensor_scalar(conv[:, c, :], uT[:, c, 2:S + 2], tap[0], 1.0, ALU.mult, ALU.mult))
                for k in (1, 2):
                    chain(nc.gpsimd.tensor_scalar(conv_t[:], uT[:, c, 2 - k:S + 2 - k], tap[k], 1.0,
                                                  ALU.mult, ALU.mult))
                    chain(nc.gpsimd.tensor_tensor(conv[:, c, :], conv[:, c, :], conv_t[:], ALU.add))
                nc.gpsimd.tensor_tensor(conv[:, c, :], conv[:, c, :], cbT[:, c, :], ALU.mult)\
                         .then_inc(conv_out, 1)
            pool.wait_ge(mm_done, TOTAL_Q)
            chain(nc.gpsimd.iota(slot_no[:], pattern=[[1, SLOTS]], base=0, channel_multiplier=0,
                                 allow_small_or_imprecise_dtypes=True))
            chain(nc.gpsimd.memset(ones[:], 1.0))
            chain(nc.gpsimd.memset(tri[:], 1.0))
            chain(nc.gpsimd.affine_select(out=tri[:], in_=tri[:], compare_op=ALU.is_gt, fill=0.0, base=0,
                                          pattern=[[1, P]], channel_multiplier=-1))
            nc.gpsimd.iota(rt[:, 0, 0:4], pattern=[[-1, 4]], base=4, channel_multiplier=0,
                           allow_small_or_imprecise_dtypes=True).then_inc(consts_made, 1)
            pool.wait_ge(turned, T_XN + KD // 2)
            for t in range(TT):
                pool.wait_ge(xn_hi_ready, t + 1)
                nc.gpsimd.tensor_tensor(xn_lo[:, t, :], xn[:, t, :], xn_hi[:, t, :].bitcast(f32),
                                        ALU.subtract).then_inc(xn_split, 1)
            pool.dma_start(g_fin[:], norm_final.rearrange("(a d) -> a d", a=1).to_broadcast([P, D]))\
                .then_inc(gfin_in, 16)

        @block.scalar
        def _(act):
            A_ = nc.scalar
            chained = [0]

            def chain(ins):
                chained[0] += 1
                ins.then_inc(act_chain, 1)
                act.wait_ge(act_chain, chained[0])

            def turn_hi(u0, dst, gain=None):
                for c in range(KD):
                    if c % 2 == 0:
                        act.wait_ge(turned, u0 + c // 2 + 1)
                    A_.activation(dst[:, c, :], half(turn_bank(u0 + c // 2), c % 2), ACT.Copy,
                                  scale=1.0 if gain is None else pcol[:, gain + c:gain + c + 1])\
                      .then_inc(hi_written, 1)

            def turn_copy(u0, dst):
                for u in range(u0 + 1, u0 + KC // 2, 2):
                    act.wait_ge(turned, u + 1)
                    c = 2 * (u - u0)
                    A_.copy(dst[:, c:c + 2, :], turn_bank(u)[:].rearrange("p (c s) -> p c s", c=2))\
                      .then_inc(turn_taken[u % 2], 1)

            def square_sum(src, k):
                if k:
                    act.wait_ge(sq_ready, k)
                A_.activation(junk[:], src, ACT.Square, accum_out=stat[:, k:k + 1]).then_inc(sq_ready, 1)

            for k in range(2 * TT):
                act.wait_ge((x_in + mem_in)[k], 16)
                square_sum((x_tok if k < TT else mem_tok)[:, k % TT, :], k)
                if k % TT == 1:
                    act.wait_ge(ms_ready, k // TT + 1)
                    A_.activation(stat[:, 8 + k - 1:8 + k + 1], stat[:, 4 + k - 1:4 + k + 1], ACT.Sqrt)\
                      .then_inc(rms_ready, 1)

            def split_hi(ph, q, it):
                n = ph.q0 + q + SPLIT_SLOTS
                if isinstance(it, int) and n + it * ph.per >= TOTAL_Q:
                    return
                slot = n // 2 % RAW_SLOTS
                if n % 2 == 0:
                    act.wait_ge(raw_loaded[slot], 16 * (n // 2 // RAW_SLOTS + 1) + it * (ph.per * 2))
                act.wait_ge(mm_done, ph.q0 + q + 1 + it * ph.per)
                A_.activation(w_hi[:, n % SPLIT_SLOTS, :], raw[:, slot, n % 2 * 1024:n % 2 * 1024 + 1024],
                              ACT.Copy).then_inc(hi_split, 1)

            def run(name, take):
                ph = PH[name]
                with rounds_of(act, ph.iters) as it:
                    q = 0
                    for jb, granules in enumerate(ph.granules):
                        for _ in range(granules):
                            split_hi(ph, q, it)
                            q += 1
                        act.wait_ge(mm_done, ph.q0 + q + it * ph.per)
                        take(ph, jb, it)

            def store_tile0(dst, col=0):
                def take(ph, jb, it):
                    A_.copy(dst[:, 0, bass.ds(it * 2 * BLK + col + jb * BLK, BLK)], pair[jb % 2][0][:])\
                      .then_inc(pair_taken[jb % 2], 1)
                return take

            def gate(ph, jb, it):
                if jb % 2 == 0:
                    act.wait_ge(pair_taken[1], ph.j0 + jb + it * ph.jobs)
                    for t in range(TT):
                        A_.activation(sig[:, t, :], pair[0][t][:], ACT.Sigmoid).then_inc(pair_taken[0], 1)

            for n in range(SPLIT_SLOTS):
                if n % 2 == 0:
                    act.wait_ge(raw_loaded[n // 2], 16)
                A_.activation(w_hi[:, n, :], raw[:, n // 2, n % 2 * 1024:n % 2 * 1024 + 1024], ACT.Copy)\
                  .then_inc(hi_split, 1)
            act.wait_ge(params_ready, 1)
            turn_hi(T_H, h_hi, G_MIX)
            turn_hi(T_MEM, y_hi, G_MEM)

            run("mem_kv", store_tile0(kv))
            run("mem_q", store_tile0(mq))

            turn_copy(T_MEMK, kT[:])
            turn_copy(T_MEMQ, qT[:])

            def exponentials(h):
                act.wait_ge(max_ready, h + 1)
                for t in range(TT):
                    A_.activation(prob[:, h, t, :], half(aux_bank(U_MEM["s", h]), t), ACT.Exp, scale=DK ** -0.5,
                                  bias=stat[:, 16 + 2 * h + t:17 + 2 * h + t],
                                  accum_out=stat[:, 24 + 2 * h + t:25 + 2 * h + t])\
                      .then_inc(prob_raw, 1)

            def memory_out_hi(h):
                u = U_MEM["y", h]
                act.wait_ge(aux_done, u + 1)
                A_.copy(y_hi[:, 2 * h:2 * h + 2, :], aux_bank(u)[:].rearrange("p (c s) -> p c s", c=2))\
                  .then_inc(hi_written, 1)

            for kind, h in MEM_ORDER:
                (exponentials if kind == "s" else memory_out_hi)(h)
            run("branch_m", gate)

            act.wait_ge(pair_taken[1], PH["branch_m"].j_end)
            act.wait_ge(aux_done, U_GA + 1)
            A_.copy(a_lr[:], aux_bank(U_GA)[0:RANK, 0:S]).then_inc(a_lr_ready, 1)
            act.wait_ge(a_lr_ready, 1)
            for c in range(KC):
                act.wait_ge(aux_done, U_A2 + c // 2 + 1)
                A_.activation(dec_k[:, c, :], half(aux_bank(U_A2 + c // 2), c % 2), ACT.Identity,
                              bias=pcol[:, B_A2 + c:B_A2 + c + 1]).then_inc(pre_ready, 1)
            run("gla_qk", store_tile0(gqk))
            act.wait_ge(pre_ready, KC)
            chain(A_.activation(dec_end[:], dec_k[:], ACT.Abs))
            chain(A_.activation(dec_end[:], dec_end[:], ACT.Exp, scale=-1.0))
            A_.activation(dec_end[:], dec_end[:], ACT.Ln, bias=1.0).then_inc(soft_ready, 1)
            run("gla_v", store_tile0(gv))
            act.wait_ge(decay_sum_ready, 1)
            A_.activation(dec_k[:], dec_q[:], ACT.Exp, scale=-1.0 / 16).then_inc(decay_ready, 1)
            A_.activation(dec_end[:], dec_end[:], ACT.Exp, scale=-1.0 / 16).then_inc(decay_ready, 1)
            A_.activation(decay_last[:], decay_last[:], ACT.Exp, scale=1.0 / 16).then_inc(decay_ready, 1)
            act.wait_ge(decay_ready, 3)
            A_.activation(dec_q[:], dec_q[:], ACT.Exp, scale=1.0 / 16).then_inc(decay_ready, 1)

            def scores_out(h):
                act.wait_ge(att_done, h + 1)
                act.wait_ge(att_masked, 2 if h < 2 else 2 + 2 * (h - 1))
                if h >= 2:
                    act.wait_ge(o_done, 2 * (h - 1))
                A_.copy(attT[h % 2][0:CH, :], bank[4 + h % 2][0:CH, 0:3 * P]).then_inc(att_lower_taken, 1)

            def squares(h):
                for t in range(TT):
                    act.wait_ge(o_done, 2 * h + t + 1)
                    if h or t:
                        act.wait_ge(o_sq, 2 * h + t)
                    A_.activation(sq_junk[:], bank[6 + t][:], ACT.Square,
                                  accum_out=stat[:, 32 + 2 * h + t:33 + 2 * h + t]).then_inc(o_sq, 1)

            for h in range(HEADS):
                scores_out(h)
                if h >= 1:
                    squares(h - 1)
            squares(HEADS - 1)
            act.wait_ge(ms_ready, 3)
            A_.activation(stat[:, 48:56], stat[:, 40:48], ACT.Sqrt).then_inc(rms_ready, 1)
            run("gla_r", store_tile0(gr))
            act.wait_ge(pair_taken[0], PH["gla_r"].j_end)
            act.wait_ge(pair_taken[1], PH["gla_r"].j_end)
            for t in range(TT):
                A_.activation(gr[:, t, :], gr[:, t, :], ACT.Silu).then_inc(swish_ready, 1)
            run("conv_cv", store_tile0(ccv))
            act.wait_ge(yb_ready, HEADS * TT)
            run("conv_b", store_tile0(cb))
            turn_hi(T_YB, y_hi, G_GLA)
            turn_copy(T_U, uT[:, :, 2:])
            turn_copy(T_CB, cbT[:])
            run("branch_b", gate)
            act.wait_ge(conv_out, KC)
            A_.copy(y_hi[:, 0:KC, :], conv[:]).then_inc(hi_written, 1)
            run("branch_a", gate)
            turn_hi(T_MERGED, h_hi)
            act.wait_ge(turned, T_XN)
            act.dma_start(x2[:], x_v).then_inc(x_again, 16)
            nothing = lambda ph, jb, it: None
            run("out_a", nothing)
            run("out_b", nothing)

            def residual_squares(first, ready, value):
                for t in range(TT):
                    act.wait_ge(ready, value)
                    act.wait_ge(sq_ready, 4 + first + t)
                    A_.activation(fin[:, t, :], x2[:, t, :], ACT.Square,
                                  accum_out=stat[:, t:t + 1]).then_inc(sq_ready, 1)

            residual_squares(0, residual_ready, 1)
            act.wait_ge(ms_ready, 4)
            A_.activation(stat[:, 8:10], stat[:, 4:6], ACT.Sqrt).then_inc(rms_ready, 1)
            for u in range(1, KD // 2, 2):
                act.wait_ge(turned, T_XN + u + 1)
                for c in (2 * u, 2 * u + 1):
                    ins = A_.activation(hT[:, c, :], half(turn_bank(u), c % 2), ACT.Copy,
                                        scale=pcol[:, G_FFN + c:G_FFN + c + 1])
                    ins.then_inc(act_chain if c % 2 == 0 else turn_taken[1], 1)
                chained[0] += 1
            for t in range(TT):
                A_.copy(xn_hi[:, t, :], xn[:, t, :]).then_inc(xn_hi_ready, 1)
            for i in range(2):
                act.wait_ge(router_d, i + 1)
                A_.activation(rt[:, 3, 0:8], rt[:, 2, 0:8], ACT.Exp).then_inc(router_exp, 1)

            act.wait_ge(rounds_ready, 1)
            act.sem_inc(gt_taken[1], START)
            rounds = act.value_load(n_rounds[0:1, 0:1], min_val=1, max_val=S // SLOTS)
            with act.Fori(0, rounds) as r, act.Fori(0, N_GROUPS) as g:
                it = r * N_GROUPS + g
                for u in range(KD // 2):
                    act.wait_ge(gt_done, it * GT_USES + GATHER + u + 1 + START)
                    for c in (2 * u, 2 * u + 1):
                        A_.activation(hT[:, c, :], half(turn_bank(u), c % 2), ACT.Copy,
                                      scale=pcol[:, G_FFN + c:G_FFN + c + 1])\
                          .then_inc(gathered if c % 2 == 0 else gt_taken[u % 2], 1)
                for kind, i in MOE_ORDER:
                    if kind == "gu":
                        act.wait_ge(gu_done, it * EPG + i + 1)
                        act.sem_inc(moe_freed["scalar"], 1)
                        act.wait_ge(hid_ready, it * EPG + i + START)
                        A_.activation(act_gate[SLOTS:, :], bank[i % 2][0:SLOTS, :], ACT.Silu)\
                          .then_inc(silu_ready, 1)
                    elif kind == "ht":
                        u = HIDDEN + i
                        act.wait_ge(gt_done, it * GT_USES + u + 1 + START)
                        A_.copy(hidT[:].rearrange("p k s -> p (k s)"), turn_bank(u)[:])\
                          .then_inc(gt_taken[u % 2], 1)
                    elif kind == "d":
                        for b in range(4):
                            act.wait_ge(down_done, it * 8 + 4 * i + b + 1)
                            if b == 3:
                                act.sem_inc(moe_freed["scalar"], 1)
                            A_.activation(out_hi[:, b, :], out_bank[b][:], ACT.Copy, scale=slot_w[:, i:i + 1])\
                              .then_inc(hi_scaled, 1)

            residual_squares(2, acc_done, rounds * (N_EXPERTS * 4) + START)
            act.wait_ge(ms_ready, 5)
            A_.activation(stat[:, 8:10], stat[:, 4:6], ACT.Sqrt).then_inc(rms_ready, 1)

        @block.vector
        def _(dve):
            V = nc.vector
            chained, hi_n = [0], [0]

            def chain(ins):
                chained[0] += 1
                ins.then_inc(dve_chain, 1)
                dve.wait_ge(dve_chain, chained[0])

            def turn_lo(u0, dst_lo, dst_hi, gain=None):
                for c in range(KD):
                    if c % 2 == 0:
                        hi_n[0] += 2
                        dve.wait_ge(hi_written, hi_n[0])
                    u = u0 + c // 2
                    ins = V.scalar_tensor_tensor(out=dst_lo[:, c, :], in0=half(turn_bank(u), c % 2),
                                                 scalar=1.0 if gain is None else pcol[:, gain + c:gain + c + 1],
                                                 in1=dst_hi[:, c, :].bitcast(f32),
                                                 op0=ALU.mult, op1=ALU.subtract)
                    ins.then_inc(lo_written if c % 2 == 0 else turn_taken[u % 2], 1)

            def turn_copy(u0, dst):
                for u in range(u0, u0 + KC // 2, 2):
                    dve.wait_ge(turned, u + 1)
                    c = 2 * (u - u0)
                    V.tensor_copy(dst[:, c:c + 2, :], turn_bank(u)[:].rearrange("p (c s) -> p c s", c=2))\
                     .then_inc(turn_taken[u % 2], 1)

            def inverse_rms(lo, n, width, count):
                V.tensor_scalar(stat[:, lo + 4:lo + 4 + n], stat[:, lo:lo + n], 1.0 / width, EPS,
                                ALU.mult, ALU.add).then_inc(ms_ready, 1)
                dve.wait_ge(rms_ready, count)
                chain(V.reciprocal(stat[:, lo + 8:lo + 8 + n], stat[:, lo + 8:lo + 8 + n]))

            dve.wait_ge(params_in, 16 * 6)
            dve.wait_ge(aux_done, U_PARAMS + 1)
            V.tensor_copy(pcol[:], aux_bank(U_PARAMS)[:, 0:96]).then_inc(params_ready, 1)
            dve.wait_ge(params_ready, 1)
            dve.sem_inc(aux_taken[U_PARAMS % 2], 1)
            for k, src in ((0, x_tok), (2, mem_tok)):
                dve.wait_ge(sq_ready, k + 2)
                inverse_rms(k, TT, D, k // 2 + 1)
                for t in range(TT):
                    V.tensor_scalar(src[:, t, :], src[:, t, :], stat[:, 8 + k + t:9 + k + t], None, ALU.mult)\
                     .then_inc(normed, 1)

            def split_lo(ph, q, it):
                n = ph.q0 + q + SPLIT_SLOTS
                if isinstance(it, int) and n + it * ph.per >= TOTAL_Q:
                    return
                slot = n // 2 % RAW_SLOTS
                dve.wait_ge(hi_split, n + 1 + it * ph.per)
                V.tensor_tensor(w_lo[:, n % SPLIT_SLOTS, :], raw[:, slot, n % 2 * 1024:n % 2 * 1024 + 1024],
                                w_hi[:, n % SPLIT_SLOTS, :].bitcast(f32), ALU.subtract).then_inc(lo_split, 1)

            def run(name, take):
                ph = PH[name]
                with rounds_of(dve, ph.iters) as it:
                    q = 0
                    for jb, granules in enumerate(ph.granules):
                        for _ in range(granules):
                            split_lo(ph, q, it)
                            q += 1
                        dve.wait_ge(mm_done, ph.q0 + q + it * ph.per)
                        take(ph, jb, it)

            def store_tile1(dst, col=0):
                def take(ph, jb, it):
                    V.tensor_copy(dst[:, 1, bass.ds(it * 2 * BLK + col + jb * BLK, BLK)], pair[jb % 2][1][:])\
                     .then_inc(pair_taken[jb % 2], 1)
                return take

            def branch(first, adds):
                def take(ph, jb, it):
                    if jb % 2 == 0:
                        return
                    done = ph.j0 + jb - 1 + it * ph.jobs
                    dve.wait_ge(pair_taken[0], done + 2)
                    for t in range(TT):
                        cols = bass.ds(it * (ph.jobs // 2) * BLK + jb // 2 * BLK, BLK)
                        if first:
                            V.tensor_tensor(merged[:, t, cols], sig[:, t, :], pair[1][t][:], ALU.mult)\
                             .then_inc(pair_taken[1], 1)
                            continue
                        dve.wait_ge(merged_done, adds + jb // 2 * 2 + it * ph.jobs)
                        V.tensor_tensor(gated[:, t, :], sig[:, t, :], pair[1][t][:], ALU.mult)\
                         .then_inc(pair_taken[1], 1)
                        dve.wait_ge(pair_taken[1], done + t + 1)
                        V.tensor_tensor(merged[:, t, cols], merged[:, t, cols], gated[:, t, :], ALU.add)\
                         .then_inc(merged_done, 1)
                return take

            for n in range(SPLIT_SLOTS):
                dve.wait_ge(hi_split, n + 1)
                V.tensor_tensor(w_lo[:, n, :], raw[:, n // 2, n % 2 * 1024:n % 2 * 1024 + 1024],
                                w_hi[:, n, :].bitcast(f32), ALU.subtract).then_inc(lo_split, 1)
            turn_lo(T_H, h_lo, h_hi, G_MIX)
            turn_lo(T_MEM, y_lo, y_hi, G_MEM)

            run("mem_kv", store_tile1(kv))
            run("mem_q", store_tile1(mq))

            turn_copy(T_MEMK, kT[:])
            turn_copy(T_MEMQ, qT[:])

            def row_max(h):
                u, k = U_MEM["s", h], 16 + 2 * h
                dve.wait_ge(aux_done, u + 1)
                chain(V.reduce_max(stat[:, k:k + 2].unsqueeze(2),
                                   aux_bank(u)[:].rearrange("p (t m) -> p t m", t=TT), AX.X))
                V.tensor_scalar(stat[:, k:k + 2], stat[:, k:k + 2], -DK ** -0.5, None, ALU.mult)\
                 .then_inc(max_ready, 1)

            def normalise(h):
                k = 24 + 2 * h
                dve.wait_ge(prob_raw, TT * h + TT)
                dve.sem_inc(aux_taken[U_MEM["s", h] % 2], 1)
                chain(V.reciprocal(stat[:, k:k + 2], stat[:, k:k + 2]))
                for t in range(TT):
                    V.tensor_scalar(prob[:, h, t, :], prob[:, h, t, :], stat[:, k + t:k + t + 1], None, ALU.mult)\
                     .then_inc(prob_ready, 1)

            def memory_out(h):
                u = T_PROB + h
                dve.wait_ge(turned, u + 1)
                V.tensor_copy(probT[:, h], turn_bank(u)[:].rearrange("p (c s) -> p c s", c=2))\
                 .then_inc(turn_taken[u % 2], 1)
                u = U_MEM["y", h]
                hi_n[0] += 1
                dve.wait_ge(hi_written, hi_n[0])
                V.tensor_tensor(y_lo[:, 2 * h:2 * h + 2, :], aux_bank(u)[:].rearrange("p (c s) -> p c s", c=2),
                                y_hi[:, 2 * h:2 * h + 2, :].bitcast(f32), ALU.subtract)\
                 .then_inc(aux_taken[u % 2], 1)

            for kind, h in MEM_ORDER:
                if kind == "s":
                    row_max(h)
                else:
                    if h == 0:
                        normalise(0)
                    memory_out(h)
                    if h < HEADS - 1:
                        normalise(h + 1)
            run("branch_m", branch(True, 0))
            dve.wait_ge(a_lr_ready, 1)
            dve.sem_inc(aux_taken[U_GA % 2], 1)
            for i in range(KC // 2):
                dve.wait_ge(pre_ready, 2 * i + 2)
                dve.sem_inc(aux_taken[(U_A2 + i) % 2], 1)
            run("gla_qk", store_tile1(gqk))
            dve.wait_ge(soft_ready, 1)
            chain(V.scalar_tensor_tensor(out=dec_k[:], in0=dec_k[:], scalar=0.0, in1=dec_end[:],
                                         op0=ALU.min, op1=ALU.subtract))
            for c in range(KC):
                ins = V.tensor_tensor_scan(dec_q[:, c, :], chunk_keep[:], dec_k[:, c, :], 0.0, ALU.mult, ALU.add)
                if c < KC - 1:
                    ins.then_inc(dve_chain, 1)
                    chained[0] += 1
            chain(ins)
            run("gla_v", store_tile1(gv))
            sums = dec_q[:].rearrange("p c (n s) -> p (c n) s", s=CH)
            last = decay_last[:].rearrange("p c n -> p (c n)").unsqueeze(2)
            chain(V.tensor_copy(last, sums[:, :, CH - 1:CH]))
            V.tensor_tensor(dec_end[:].rearrange("p c (n s) -> p (c n) s", s=CH), sums,
                            last.to_broadcast([P, KC * NCH, CH]), ALU.subtract).then_inc(decay_sum_ready, 1)
            dve.wait_ge(decay_ready, 4)
            for c in range(KC):
                u = T_GQ + c // 2
                dve.wait_ge(turned, u + 1)
                V.scalar_tensor_tensor(out=dec_q[:, c, :], in0=half(turn_bank(u), c % 2), scalar=DK ** -0.5,
                                       in1=dec_q[:, c, :], op0=ALU.mult, op1=ALU.mult)\
                 .then_inc(dve_chain if c % 2 == 0 else turn_taken[u % 2], 1)
                chained[0] += 1 - c % 2
            for c in range(KC):
                u = T_GK + c // 2
                dve.wait_ge(turned, u + 1)
                chain(V.tensor_tensor(dec_k[:, c, :], half(turn_bank(u), c % 2), dec_k[:, c, :], ALU.mult))
                V.tensor_tensor(dec_end[:, c, :], half(turn_bank(u), c % 2), dec_end[:, c, :], ALU.mult)\
                 .then_inc(dve_chain if c % 2 == 0 else turn_taken[u % 2], 1)
                chained[0] += 1 - c % 2
            turned_before(dve, T_YB)

            def chunk_decay(n):
                return decay_last[:, :, n:n + 1].to_broadcast([P, KC, CH])

            V.tensor_tensor(q_far[:, :, 0:CH], dec_q[:, :, 2 * CH:3 * CH], chunk_decay(1), ALU.mult)\
             .then_inc(dve_chain, 1)
            chained[0] += 1
            chain(V.tensor_tensor(q_skip[:], dec_q[:, :, 3 * CH:4 * CH], chunk_decay(2), ALU.mult))
            V.tensor_tensor(q_far[:, :, CH:], q_skip[:], chunk_decay(1), ALU.mult).then_inc(decayed_qk, 1)

            def scores_out(h):
                a = attT[h % 2]
                dve.wait_ge(att_done, h + 1)
                dve.wait_ge(att_masked, 2 if h < 2 else 2 + 2 * (h - 1))
                if h >= 2:
                    dve.wait_ge(o_done, 2 * (h - 1))
                V.tensor_copy(a[CH:, CH:S], bank[4 + h % 2][CH:, CH:S]).then_inc(att_upper_taken, 1)
                V.tensor_copy(a[CH:, S + CH:], bank[4 + h % 2][CH:, S + CH:3 * P]).then_inc(att_upper_taken, 1)

            def outputs_out(h):
                dve.wait_ge(o_done, 2 * h + 2)
                for t in range(TT):
                    dve.wait_ge(o_sq, 2 * h + t + 1)
                    V.tensor_copy(gv[:, t, h * DV:(h + 1) * DV], bank[6 + t][:]).then_inc(o_taken, 1)

            for h in range(HEADS):
                scores_out(h)
                if h >= 1:
                    outputs_out(h - 1)
            outputs_out(HEADS - 1)
            dve.wait_ge(o_sq, HEADS * TT)
            V.tensor_scalar(stat[:, 40:48], stat[:, 32:40], 1.0 / DV, EPS, ALU.mult, ALU.add)\
             .then_inc(ms_ready, 1)
            run("gla_r", store_tile1(gr))
            dve.wait_ge(rms_ready, 3)
            chain(V.reciprocal(stat[:, 48:56], stat[:, 48:56]))
            dve.wait_ge(o_taken, HEADS * TT)
            for t in range(TT):
                dve.wait_ge(swish_ready, t + 1)
                for h in range(HEADS):
                    cols = slice(h * DV, (h + 1) * DV)
                    k = 48 + 2 * h + t
                    V.scalar_tensor_tensor(out=gv[:, t, cols], in0=gv[:, t, cols], scalar=stat[:, k:k + 1],
                                           in1=gr[:, t, cols], op0=ALU.mult, op1=ALU.mult)\
                     .then_inc(yb_ready, 1)
            run("conv_cv", store_tile1(ccv))
            run("conv_b", store_tile1(cb))
            turn_lo(T_YB, y_lo, y_hi, G_GLA)
            turn_copy(T_U, uT[:, :, 2:])
            turn_copy(T_CB, cbT[:])
            run("branch_b", branch(False, 0))
            hi_n[0] += 1
            dve.wait_ge(hi_written, hi_n[0])
            V.tensor_tensor(y_lo[:, 0:KC, :], conv[:], y_hi[:, 0:KC, :].bitcast(f32), ALU.subtract)\
             .then_inc(y_ready, 1)
            run("branch_a", branch(False, 8))
            turn_lo(T_MERGED, h_lo, h_hi)

            def add_residual(ph, jb, it):
                if jb == 0 and ph is PH["out_a"]:
                    dve.wait_ge(x_again, 16)
                n = (ph.j0 - PH["out_a"].j0 + jb)
                for t in range(TT):
                    dst = x2[:, t, n * BLK:(n + 1) * BLK]
                    V.tensor_tensor(dst, pair[jb % 2][t][:], dst, ALU.add).then_inc(pair_taken[jb % 2], 1)

            run("out_a", add_residual)
            run("out_b", add_residual)
            for i in range(2):
                dve.wait_ge(pair_taken[i], PH["out_b"].j_end)
            dve.sem_inc(residual_ready, 1)

            dve.wait_ge(sq_ready, 6)
            V.tensor_scalar(stat[:, 4:6], stat[:, 0:2], 1.0 / D, EPS, ALU.mult, ALU.add).then_inc(ms_ready, 1)
            dve.wait_ge(rms_ready, 4)
            chain(V.reciprocal(stat[:, 8:10], stat[:, 8:10]))
            for t in range(TT):
                V.tensor_scalar(xn[:, t, :], x2[:, t, :], stat[:, 8 + t:9 + t], None, ALU.mult).then_inc(normed, 1)
            for u in range(0, KD // 2, 2):
                dve.wait_ge(turned, T_XN + u + 1)
                for c in (2 * u, 2 * u + 1):
                    V.tensor_scalar(hT[:, c, :], half(turn_bank(u), c % 2), pcol[:, G_FFN + c:G_FFN + c + 1],
                                    None, ALU.mult).then_inc(dve_chain if c % 2 == 0 else turn_taken[0], 1)
                chained[0] += 1
            dve.wait_ge(aux_done, U_LOGIT + 1)
            V.tensor_copy(logitT[:], aux_bank(U_LOGIT)[0:N_GROUPS + N_EXPERTS, 0:S])\
             .then_inc(aux_taken[U_LOGIT % 2], 1)
            dve.wait_ge(turned, T_ROUTE + 1)
            NE = N_GROUPS + N_EXPERTS
            logit = rt[:, 30:32, :].rearrange("p a b -> p (a b)")[:, 0:TT * NE].rearrange("p (t e) -> p t e", e=NE)
            V.tensor_copy(logit, turn_bank(T_ROUTE)[:, 0:TT * NE].rearrange("p (t e) -> p t e", e=NE))\
             .then_inc(turn_taken[T_ROUTE % 2], 1)
            dve.wait_ge(turn_taken[T_ROUTE % 2], T_ROUTE // 2 + 1)
            dve.wait_ge(consts_made, 2)

            def four(k):
                return rt[:, k, 0:8].rearrange("p (t e) -> p t e", e=4)

            def one(k):
                return rt[:, k, 0:2].unsqueeze(2)

            def wide(k):
                return one(k).to_broadcast([P, TT, 4])

            def sixteen(k):
                return rt[:, k, 0:32].rearrange("p (t g e) -> p t g e", g=N_GROUPS, e=EPG)

            rank = rt[:, 0, 0:4].unsqueeze(1).to_broadcast([P, TT, 4])

            def softmax(src, dst, n):
                chain(V.reduce_max(one(1), src, AX.X))
                V.tensor_tensor(four(2), src, wide(1), ALU.subtract).then_inc(router_d, 1)
                dve.wait_ge(router_exp, n)
                chain(V.tensor_reduce(one(4), four(3), AX.X, ALU.add))
                chain(V.reciprocal(one(5), one(4)))
                chain(V.tensor_tensor(dst, four(3), wide(5), ALU.mult))

            def first_largest(src, best, pick):
                chain(V.reduce_max(one(best), src, AX.X))
                chain(V.tensor_tensor(four(6), src, wide(best), ALU.is_equal))
                chain(V.tensor_tensor(four(7), four(6), rank, ALU.mult))
                chain(V.reduce_max(one(8), four(7), AX.X))
                chain(V.tensor_tensor(four(pick), four(7), wide(8), ALU.is_equal))

            softmax(logit[:, :, 0:N_GROUPS], four(9), 1)
            first_largest(four(9), 10, 11)
            picked = four(11).unsqueeze(3).to_broadcast([P, TT, N_GROUPS, EPG])
            chain(V.tensor_tensor(sixteen(12), logit[:, :, N_GROUPS:].rearrange("p t (g e) -> p t g e", e=EPG),
                                  picked, ALU.mult))
            chain(V.tensor_reduce(four(13), sixteen(12).rearrange("p t g e -> p t e g"), AX.X, ALU.add))
            softmax(four(13), four(14), 2)
            first_largest(four(14), 15, 16)
            chain(V.scalar_tensor_tensor(out=four(17), in0=four(16), scalar=-2.0, in1=four(14),
                                         op0=ALU.mult, op1=ALU.add))
            first_largest(four(17), 18, 19)
            chain(V.tensor_tensor(one(20), one(15), one(18), ALU.add))
            chain(V.reciprocal(one(20), one(20)))
            chain(V.tensor_tensor(one(21), one(15), one(20), ALU.mult))
            chain(V.tensor_tensor(one(22), one(18), one(20), ALU.mult))
            chain(V.tensor_tensor(four(23), four(16), wide(21), ALU.mult))
            chain(V.tensor_tensor(four(24), four(19), wide(22), ALU.mult))
            chain(V.tensor_tensor(four(23), four(23), four(24), ALU.add))
            chain(V.tensor_tensor(four(23), four(23), wide(10), ALU.mult))
            chain(V.tensor_tensor(four(25), four(16), four(19), ALU.add))
            WEIGHT, CHOSEN, PLACE = 26, 27, 28
            for src, dst in ((23, WEIGHT), (25, CHOSEN)):
                chain(V.tensor_tensor(sixteen(dst), four(src).unsqueeze(2).to_broadcast([P, TT, N_GROUPS, EPG]),
                                      picked, ALU.mult))
            dve.sem_inc(route_ready, 1)
            dve.wait_ge(pos_done, 1)
            places = bank[6][:, 0:48]
            chain(V.tensor_scalar(rt[:, PLACE, :], rt[:, CHOSEN, :], -1024.0, 1024.0, ALU.mult, ALU.add))
            chain(V.tensor_tensor(rt[:, PLACE, :], rt[:, PLACE, :], places[:, 0:32], ALU.add))
            longest, more = rt[:, 29, 0:1], rt[:, 29, 1:4]
            chain(V.reduce_max(longest, places[:, 32:48], AX.X))
            for k in range(1, S // SLOTS):
                chain(V.tensor_scalar(more[:, k - 1:k], longest, float(SLOTS * k), None, ALU.is_gt))
            chain(V.tensor_reduce(rt[:, 29, 4:5], more, AX.X, ALU.add))
            V.tensor_scalar(n_rounds[:], rt[:, 29, 4:5], 1.0, None, ALU.add).then_inc(rounds_ready, 1)
            for dst, row in ((place, PLACE), (weight, WEIGHT)):
                chain(V.tensor_copy(dst[:, :, 0:N_EXPERTS],
                                    rt[:, row, :].rearrange("p (t e) -> p t e", e=N_EXPERTS)))
            chain(V.tensor_copy(weight[:, :, N_EXPERTS:], weight[:, :, 0:EPG]))
            chain(V.tensor_scalar(place[:, :, N_EXPERTS:], place[:, :, 0:EPG], -float(SLOTS), None, ALU.add))

            def dispatch(group):
                experts = bass.ds(group * EPG, EPG)
                for t in range(TT):
                    V.tensor_tensor(disp[:, t, :].rearrange("p (e s) -> p e s", s=SLOTS),
                                    slot_no[:].unsqueeze(1).to_broadcast([P, EPG, SLOTS]),
                                    place[:, t, experts].unsqueeze(2).to_broadcast([P, EPG, SLOTS]),
                                    ALU.is_equal).then_inc(disp_ready, 1)
                V.tensor_copy(group_w[:], weight[:, :, experts]).then_inc(disp_ready, 1)

            dve.wait_ge(mm_done, TOTAL_Q)
            dispatch(0)
            dve.wait_ge(rounds_ready, 1)
            for started in (gt_taken[0], hid_ready, acc_done):
                dve.sem_inc(started, START)
            rounds = dve.value_load(n_rounds[0:1, 0:1], min_val=1, max_val=S // SLOTS)

            with dve.Fori(0, rounds) as r:
                with dve.Fori(0, N_GROUPS) as g:
                    it = r * N_GROUPS + g
                    dve.wait_ge(gt_done, it * GT_USES + BACK + 1 + START)
                    V.tensor_copy(dispT[:].rearrange("p e s -> p (e s)"), turn_bank(BACK)[:])\
                     .then_inc(gt_taken[BACK % 2], 1)
                    dve.wait_ge(gt_done, it * GT_USES + SLOT_W + 1 + START)
                    both = turn_bank(SLOT_W)[:, 0:EPG].rearrange("p (i e) -> p i e", e=2)
                    V.tensor_copy(slot_w[0:SLOTS, :].unsqueeze(2), both[0:SLOTS, :, 0:1]).then_inc(gathered_w, 1)
                    V.tensor_copy(slot_w[SLOTS:, :].unsqueeze(2), both[SLOTS:, :, 1:2])\
                     .then_inc(gt_taken[SLOT_W % 2], 1)
                    for kind, i in MOE_ORDER:
                        if kind == "gu":
                            dve.wait_ge(silu_ready, it * EPG + i + 1)
                            rows = slice(i % 2 * SLOTS, (i % 2 + 1) * SLOTS)
                            V.tensor_tensor(hid[rows, i // 2, :], act_gate[SLOTS:, :], bank[i % 2][SLOTS:, :],
                                            ALU.mult).then_inc(hid_ready, 1)
                            if i == EPG - 1:
                                dispatch(g + 1)
                        elif kind == "d":
                            for b in range(4):
                                dve.wait_ge(hi_scaled, it * 8 + 4 * i + b + 1)
                                V.scalar_tensor_tensor(out=out_lo[:, b, :], in0=out_bank[b][:],
                                                       scalar=slot_w[:, i:i + 1],
                                                       in1=out_hi[:, b, :].bitcast(f32),
                                                       op0=ALU.mult, op1=ALU.subtract).then_inc(y_taken, 1)
                        elif kind == "c":
                            for k in range(8):
                                b, t = k // 2, k % 2
                                dve.wait_ge(comb_done, it * 16 + 8 * i + k + 1)
                                dve.wait_ge(acc_done, it * 16 + 8 * i + START)
                                dst = x2[:, t, b * BLK:(b + 1) * BLK]
                                V.tensor_tensor(dst, dst, out_bank[k % 4][:], ALU.add).then_inc(acc_done, 1)
                dve.wait_ge(disp_ready, r * (N_GROUPS * 3) + (N_GROUPS + 1) * 3)
                V.tensor_scalar(place[:], place[:], -float(SLOTS), None, ALU.add)\
                 .then_inc(pos_done, 1)
                dve.wait_ge(pos_done, r + 2)

            dve.wait_ge(sq_ready, 8)
            V.tensor_scalar(stat[:, 4:6], stat[:, 0:2], 1.0 / D, EPS, ALU.mult, ALU.add).then_inc(ms_ready, 1)
            dve.wait_ge(rms_ready, 5)
            chain(V.reciprocal(stat[:, 8:10], stat[:, 8:10]))
            dve.wait_ge(gfin_in, 16)
            for t in range(TT):
                V.scalar_tensor_tensor(out=fin[:, t, :], in0=x2[:, t, :], scalar=stat[:, 8 + t:9 + t],
                                       in1=g_fin[:], op0=ALU.mult, op1=ALU.mult).then_inc(stored, 1)

        @block.tensor
        def _(pe):
            T = nc.tensor

            def turn(u0, n, src, col=0):
                for c in range(n):
                    u = u0 + c // 2
                    if c % 2 == 0 and u >= 2:
                        pe.wait_ge(turn_taken[u % 2], u // 2)
                    for t in range(TT):
                        ins = T.transpose(half(turn_bank(u), c % 2)[:, t * P:(t + 1) * P],
                                          src[:, t, col + c * P:col + (c + 1) * P], ident[:])
                    if c % 2:
                        ins.then_inc(turned, 1)

            def aux_free(u):
                if u >= 2:
                    pe.wait_ge(aux_taken[u % 2], u // 2)
                return aux_bank(u)

            def multiply(name, lhs):
                ph = PH[name]
                with rounds_of(pe, ph.iters) as it:
                    q = 0
                    for jb, granules in enumerate(ph.granules):
                        hi, lo = lhs[jb % len(lhs)]
                        pe.wait_ge(pair_taken[jb % 2], (ph.j0 + jb) // 2 * 2 + it * ph.jobs)
                        for g in range(granules):
                            n = ph.q0 + q
                            pe.wait_ge(lo_split, n + 1 + it * ph.per)
                            for c in range(2):
                                k = 2 * g + c
                                wh = w_hi[:, n % SPLIT_SLOTS, c * BLK:(c + 1) * BLK]
                                wl = w_lo[:, n % SPLIT_SLOTS, c * BLK:(c + 1) * BLK]
                                for t in range(TT):
                                    acc = pair[jb % 2][t][:]
                                    tok = slice(t * P, (t + 1) * P)
                                    last = k == 2 * granules - 1
                                    T.matmul(acc, hi[:, k, tok], wh, start=k == 0, stop=False)
                                    T.matmul(acc, hi[:, k, tok], wl, start=False, stop=False)
                                    ins = T.matmul(acc, lo[:, k, tok], wh, start=False, stop=last)
                            ins.then_inc(mm_done, 1)
                            q += 1

            H, Y = (h_hi, h_lo), (y_hi, y_lo)
            pe.wait_ge(consts_made, 1)
            pe.wait_ge(params_in, 16 * 6)
            T.transpose(aux_bank(U_PARAMS)[:, 0:96], prow[:], ident[0:96, 0:96]).then_inc(aux_done, 1)
            pe.wait_ge(normed, TT)
            turn(T_H, KD, x_tok)
            pe.wait_ge(normed, 2 * TT)
            turn(T_MEM, KD, mem_tok)
            turned_before(pe, T_MEMK)
            multiply("mem_kv", [Y])
            multiply("mem_q", [H])

            for p in range(2):
                pe.wait_ge(pair_taken[p], PH["mem_q"].j_end)
            turn(T_MEMK, KC, kv)
            turn(T_MEMQ, KC, mq)
            turned_before(pe, T_PROB)
            for kind, h in MEM_ORDER:
                acc = aux_free(U_MEM[kind, h])
                if kind == "s":
                    for t in range(TT):
                        for i in range(2):
                            ins = T.matmul(half(acc, t), qT[:, 2 * h + i, t * P:(t + 1) * P], kT[:, 2 * h + i, :],
                                           start=i == 0, stop=i == 1)
                    ins.then_inc(aux_done, 1)
                    continue
                pe.wait_ge(prob_ready, TT * h + TT)
                turn(T_PROB + h, TT, prob[:, h])
                turned_before(pe, T_PROB + h + 1)
                for i in range(2):
                    col = CONV + h * DK + i * P
                    for m in range(TT):
                        ins = T.matmul(half(acc, i), kv[:, m, col:col + P], probT[:, h, m, :],
                                       start=m == 0, stop=m == 1)
                ins.then_inc(aux_done, 1)
            aux_before(pe, U_GA)
            multiply("branch_m", [H, Y])

            pe.wait_ge(h_full_ready, 1)
            pe.wait_ge(small_in, 48)
            acc = aux_free(U_GA)
            for c in range(KD):
                ins = T.matmul(acc[0:RANK, 0:S], w_ga[:, c, :], h_full[:, c, :], start=c == 0, stop=c == KD - 1)
            ins.then_inc(aux_done, 1)
            pe.wait_ge(a_lr_ready, 1)
            pe.wait_ge(a2_in, 16)
            for c in range(KC):
                if c % 2 == 0:
                    acc = aux_free(U_A2 + c // 2)
                ins = T.matmul(half(acc, c % 2), w_a2[:, c * P:(c + 1) * P], a_lr[:], start=True, stop=True)
                if c % 2:
                    ins.then_inc(aux_done, 1)
            multiply("gla_qk", [H])
            multiply("gla_v", [H])

            turn(T_GQ, KC, gqk)
            turn(T_GK, KC, gqk, col=CONV)
            for p in range(2):
                pe.wait_ge(pair_taken[p], PH["gla_v"].j_end)
            pe.wait_ge(decayed_qk, 1)

            def scores(h):
                att = bank[4 + h % 2]
                if h >= 2:
                    pe.wait_ge(att_lower_taken, h - 1)
                    pe.wait_ge(att_upper_taken, 2 * (h - 1))
                blocks = []
                for n in range(NCH):
                    part = slice(n % 2 * CH, n % 2 * CH + CH)
                    base_col = 0 if n < 2 else P
                    cols = lambda a, b: slice(base_col + a * CH, base_col + b * CH)
                    keys = slice(n * CH, (n + 1) * CH)
                    blocks.append((part, cols(n, n + 1), dec_k, keys, dec_q, slice(n * CH, (n + 1) * CH)))
                    if n + 1 < NCH:
                        blocks.append((part, cols(n + 1, n + 2), dec_end, keys, dec_q,
                                       slice((n + 1) * CH, (n + 2) * CH)))
                    if n == 0:
                        blocks.append((part, cols(2, 4), dec_end, keys, q_far, slice(0, 2 * CH)))
                    if n == 1:
                        blocks.append((part, cols(3, 4), dec_end, keys, q_skip, slice(0, CH)))
                for part, cols, k_side, keys, q_side, queries in blocks:
                    for i in range(2):
                        ins = T.matmul(att[part, cols], k_side[:, 2 * h + i, keys],
                                       q_side[:, 2 * h + i, queries], start=i == 0, stop=i == 1)
                ins.then_inc(att_done, 1)

            def outputs(h):
                pe.wait_ge(att_masked, 2 + 2 * (h + 1))
                if h >= 1:
                    pe.wait_ge(o_taken, 2 * h)
                    pe.wait_ge(o_sq, 2 * h)
                a, cols = attT[h % 2], slice(h * DV, (h + 1) * DV)
                T.matmul(bank[6][:], a[:, 0:P], gv[:, 0, cols], start=True, stop=True).then_inc(o_done, 1)
                T.matmul(bank[7][:], a[:, P:S], gv[:, 0, cols], start=True, stop=False)
                T.matmul(bank[7][:], a[:, S:], gv[:, 1, cols], start=False, stop=True).then_inc(o_done, 1)

            aux_before(pe, U_LOGIT)
            for h in range(HEADS):
                scores(h)
                if h >= 1:
                    outputs(h - 1)
            outputs(HEADS - 1)
            multiply("gla_r", [H])
            multiply("conv_cv", [H])
            multiply("conv_b", [H])
            pe.wait_ge(yb_ready, HEADS * TT)
            pe.wait_ge(att_lower_taken, HEADS)
            pe.wait_ge(att_upper_taken, 2 * HEADS)
            turn(T_YB, KD, gv)
            pe.wait_ge(conv_u, TT)
            for p in range(2):
                pe.wait_ge(pair_taken[p], PH["conv_b"].j_end)
            turn(T_U, KC, ccv)
            turn(T_CB, KC, cb)
            multiply("branch_b", [H, Y])
            pe.wait_ge(y_ready, 1)
            multiply("branch_a", [H, Y])
            pe.wait_ge(merged_done, 16)
            turn(T_MERGED, KD, merged)
            turned_before(pe, T_XN)
            multiply("out_a", [H])
            multiply("out_b", [H])

            pe.wait_ge(normed, 3 * TT)
            turn(T_XN, KD, xn)
            turned_before(pe, T_ROUTE)
            pe.wait_ge(o_taken, HEADS * TT)
            pe.wait_ge(o_sq, HEADS * TT)
            NE = N_GROUPS + N_EXPERTS
            for c in range(KD):
                ins = T.matmul(aux_bank(U_LOGIT)[0:NE, 0:S], w_rt[:, c, :], hT[:, c, :], start=c == 0, stop=c == KD - 1)
            ins.then_inc(aux_done, 1)
            aux_before(pe, U_LOGIT + 1)
            for t in range(TT):
                ins = T.transpose(turn_bank(T_ROUTE)[:, t * NE:(t + 1) * NE], logitT[:, t * P:(t + 1) * P],
                                  ident[0:NE, 0:NE])
            ins.then_inc(turned, 1)
            pe.wait_ge(route_ready, 1)
            CHOSEN = 27
            chosen = [rt[:, CHOSEN, t * 16:(t + 1) * 16] for t in range(TT)]
            T.matmul(bank[6][:, 0:16], tri[:], chosen[0], start=True, stop=True)
            T.matmul(bank[6][:, 16:32], ones[:], chosen[0], start=True, stop=False)
            T.matmul(bank[6][:, 16:32], tri[:], chosen[1], start=False, stop=True)
            T.matmul(bank[6][:, 32:48], ones[:], chosen[0], start=True, stop=False)
            T.matmul(bank[6][:, 32:48], ones[:], chosen[1], start=False, stop=True).then_inc(pos_done, 1)

            pe.wait_ge(rounds_ready, 1)
            pe.sem_inc(gt_done, START)
            rounds = pe.value_load(n_rounds[0:1, 0:1], min_val=1, max_val=S // SLOTS)
            turned_before(pe, T_ROUTE + 1)
            pe.wait_ge(xn_split, TT)
            with pe.Fori(0, rounds) as r, pe.Fori(0, N_GROUPS) as g:
                it = r * N_GROUPS + g

                def gt_bank(u):
                    pe.wait_ge(gt_taken[u % 2], it * (GT_USES // 2) + u // 2 + START)
                    return turn_bank(u)

                pe.wait_ge(disp_ready, it * 3 + 3)
                for c in range(KD):
                    if c % 2 == 0:
                        acc = gt_bank(GATHER + c // 2)
                    for t in range(TT):
                        for part in (xn_hi, xn_lo):
                            ins = T.matmul(half(acc, c % 2), part[:, t, c * P:(c + 1) * P], disp[:, t, :],
                                           start=t == 0 and part is xn_hi, stop=t == 1 and part is xn_lo)
                    if c % 2:
                        ins.then_inc(gt_done, 1)
                acc = gt_bank(BACK)
                pairs = [slice(i * 2 * SLOTS, (i + 1) * 2 * SLOTS) for i in range(EPG // 2)]
                for i, slots in enumerate(pairs):
                    for t in range(TT):
                        ins = T.transpose(half(acc, i)[:, t * P:(t + 1) * P], disp[:, t, slots].bitcast(f32), ident[:])
                ins.then_inc(gt_done, 1)
                acc = gt_bank(SLOT_W)
                for i, slots in enumerate(pairs):
                    for t in range(TT):
                        ins = T.matmul(acc[:, 2 * i:2 * i + 2], disp[:, t, slots].bitcast(f32),
                                       group_w[:, t, 2 * i:2 * i + 2], start=t == 0, stop=t == 1)
                ins.then_inc(gt_done, 1)
                for s in range(2):
                    pe.wait_ge(gt_taken[s], it * (GT_USES // 2) + HIDDEN // 2 + START)
                n = 0
                rows = [slice(0, SLOTS), slice(SLOTS, P)]

                def moe_wait(n):
                    pe.wait_ge(moe_loaded[n % MOE_SLOTS],
                               it * (MOE_LOADS // MOE_SLOTS * 16) + 16 * (n // MOE_SLOTS + 1))

                for kind, i in MOE_ORDER:
                    if kind == "gu":
                        acc = bank[i % 2]
                        pe.wait_ge(hid_ready, it * EPG + max(i - 1, 0) + START)
                        for l in range(4):
                            moe_wait(n)
                            moe_wait(n + 1)
                            for k in range(4):
                                c = 4 * l + k
                                for side in range(2):
                                    w = moe_raw[:, moe_slot(n + side), k * BLK:(k + 1) * BLK]
                                    ins = T.matmul(acc[rows[side], :], hT[:, c, i * SLOTS:(i + 1) * SLOTS], w,
                                                   start=c == 0, stop=c == KD - 1)
                                    if k == 3 and l * 2 + side < 7:
                                        ins.then_inc(moe_freed["tensor"], 1)
                            n += 2
                        ins.then_inc(gu_done, 1)
                    elif kind == "ht":
                        slot = gt_bank(HIDDEN + i)
                        pe.wait_ge(hid_ready, it * EPG + 2 * i + 2 + START)
                        for k in range(KE):
                            ins = T.transpose(slot[:, k * P:(k + 1) * P], hid[:, i, k * P:(k + 1) * P], ident[:])
                        ins.then_inc(gt_done, 1)
                    elif kind == "d":
                        u = HIDDEN + i
                        pe.wait_ge(gt_taken[u % 2], it * (GT_USES // 2) + u // 2 + 1 + START)
                        pe.wait_ge(acc_done, it * 16 + 8 * i + START)
                        for l in range(KE):
                            moe_wait(n)
                            moe_wait(n + 1)
                            for b in range(4):
                                for side in range(2):
                                    w = moe_raw[:, moe_slot(n + side), b * BLK:(b + 1) * BLK]
                                    ins = T.matmul(out_bank[b][rows[side], :],
                                                   hidT[:, l, side * SLOTS:(side + 1) * SLOTS], w,
                                                   start=l == 0, stop=l == KE - 1)
                                    if b == 3 and l * 2 + side < 7:
                                        ins.then_inc(moe_freed["tensor"], 1)
                                if l == KE - 1:
                                    ins.then_inc(down_done, 1)
                            n += 2
                    elif kind == "c":
                        for k in range(8):
                            b, t = k // 2, k % 2
                            if k < 4:
                                pe.wait_ge(y_taken, it * 8 + 4 * i + k + 1)
                            else:
                                pe.wait_ge(acc_done, it * 16 + 8 * i + k - 3 + START)
                            T.matmul(out_bank[k % 4][:], dispT[:, i, t * P:(t + 1) * P], out_hi[:, b, :],
                                     start=True, stop=False)
                            T.matmul(out_bank[k % 4][:], dispT[:, i, t * P:(t + 1) * P], out_lo[:, b, :],
                                     start=False, stop=True).then_inc(comb_done, 1)


MOE_ORDER = [("gu", 0), ("gu", 1), ("gu", 2), ("ht", 0), ("d", 0), ("gu", 3), ("c", 0), ("ht", 1),
             ("d", 1), ("c", 1)]
MOE_LOADS = 8 * sum(kind in ("gu", "d") for kind, _ in MOE_ORDER)


def moe_frees():
    out, count = [], {"tensor": 0, "scalar": 0}
    for kind, _ in MOE_ORDER:
        for l in range(8 if kind in ("gu", "d") else 0):
            by = "scalar" if l == 7 else "tensor"
            count[by] += 1
            out.append((by, count[by]))
    return out, count


_INS = ["x", "mem", "norm_mix", "w_in", "conv_w", "gla_w_a2", "gla_b_a2", "gla_norm", "norm_mem",
        "w_mem_kv", "w_br_conv", "w_br_gla", "w_br_mem", "w_o", "norm_ffn", "w_router_group",
        "w_router_expert", "w_gate", "w_up", "w_down", "norm_final"]


def kernel(**inputs):
    import numpy as _np
    import concourse.bacc as _bacc
    from concourse import mybir as _mybir
    from concourse.bass_utils import run_bass_kernel_spmd as _run

    nc = _bacc.Bacc("TRN2", target_bir_lowering=False, num_devices=1)
    arrays, args = {}, []
    for name in _INS:
        a = _np.ascontiguousarray(inputs[name])
        arrays[f"in_{name}_dram"] = a
        args.append(nc.dram_tensor(f"in_{name}_dram", a.shape, _mybir.dt.from_np(a.dtype),
                                   kind="ExternalInput").ap())
    args.append(nc.dram_tensor("out_dram", (1, S, D), _mybir.dt.float32, kind="ExternalOutput").ap())
    hybrid_layer(nc, *args)
    r = _run(nc, [arrays], core_ids=[0])
    return r.results[0]["out_dram"]
```

```python
import concourse.bass as bass
from concourse import mybir
from contextlib import ExitStack, contextmanager

P = 128
S = 256
TT = S // P
D = 2048
KD = D // P
BLK = 512
CONV = 1024
KC = CONV // P
HEADS = 4
DK = 256
DV = 512
CH = 64
NCH = S // CH
RANK = 16
EPS = 1e-6
N_GROUPS = 4
EPG = 4
N_EXPERTS = 16
DE = 512
KE = DE // P
SLOTS = 64
COL_CONV, COL_GQ, COL_GV, COL_GR = 0, 3072, 5120, 7168
COL_GA, COL_MQ, COL_GATE_A, COL_GATE_B, COL_GATE_M = 9216, 9232, 10256, 12304, 14352

RAW_SLOTS = 4
SPLIT_SLOTS = 4
MOE_SLOTS = 12
START = 1


class Phase:

    def __init__(self, iters, granules, q0, j0):
        self.iters, self.granules, self.q0, self.j0 = iters, granules, q0, j0
        self.per = sum(granules)
        self.jobs = len(granules)
        self.q_end = q0 + iters * self.per
        self.j_end = j0 + iters * self.jobs


def phases():
    out, q, j = {}, 0, 0
    for name, iters, granules in (
        ("mem_q", 1, (8, 8)), ("mem_k", 1, (8, 8)), ("mem_v", 1, (8, 8)),
        ("branch_m", 2, (8, 4, 8, 4)), ("gla_q", 1, (8, 8)), ("gla_k", 1, (8, 8)),
        ("gla_v_first", 1, (8, 8)), ("gla_v_last", 1, (8, 8)), ("gla_r", 2, (8, 8)),
        ("conv_cv", 2, (8, 8)), ("conv_b", 1, (8, 8)), ("branch_b", 4, (8, 8)),
        ("branch_a", 2, (8, 4, 8, 4)), ("out_a", 1, (8, 8)), ("out_b", 1, (8, 8)),
    ):
        out[name] = Phase(iters, granules, q, j)
        q, j = out[name].q_end, out[name].j_end
    return out, q


@contextmanager
def rounds_of(eng, n):
    if n == 1:
        yield 0
    else:
        with eng.Fori(0, n) as it:
            yield it


def hybrid_layer(nc, x, mem, norm_mix, w_in, conv_w, gla_w_a2, gla_b_a2, gla_norm, norm_mem,
                 w_mem_kv, w_br_conv, w_br_gla, w_br_mem, w_o, norm_ffn, w_router_group,
                 w_router_expert, w_gate, w_up, w_down, norm_final, out):
    f32, f32r, i32 = mybir.dt.float32, mybir.dt.float32r, mybir.dt.int32
    ALU, ACT, AX = mybir.AluOpType, mybir.ActivationFunctionType, mybir.AxisListType
    PH, TOTAL_Q = phases()

    def k_major(w):
        return w.rearrange("(kc p) n -> p kc n", p=P)

    x_v = x[0].rearrange("(t p) d -> p t d", p=P)
    mem_v = mem[0].rearrange("(t p) d -> p t d", p=P)
    out_v = out[0].rearrange("(t p) d -> p t d", p=P)
    in_v, kv_v, o_v = k_major(w_in[0]), k_major(w_mem_kv[0]), k_major(w_o[0])
    bra_v, brb_v, brm_v = k_major(w_br_conv[0]), k_major(w_br_gla[0]), k_major(w_br_mem[0])
    gate_v = w_gate[0].rearrange("e (kc p) n -> p e kc n", p=P)
    up_v = w_up[0].rearrange("e (kc p) n -> p e kc n", p=P)
    down_v = w_down[0].rearrange("e (kc p) n -> p e kc n", p=P)

    KB = 1024
    base = (nc.sbuf_base + 31) // 32 * 32

    def at(name, kb, shape, dt=f32):
        return nc.alloc_sbuf_tensor_at(name, shape, dt, offset=base + int(kb * KB))

    ident = at("ident", 0, [P, P])
    pcol = at("pcol", 0.5, [P, 96])
    w_ga = at("w_ga", 1, [P, KD, RANK])
    w_ga_lo = at("w_ga_lo", 1, [P, KD, RANK], f32r)
    w_ga_hi = at("w_ga_hi", 5, [P, KD, RANK], f32r)
    w_rt = at("w_rt", 2, [P, KD, N_GROUPS + N_EXPERTS])
    chunk_keep = at("chunk_keep", 3.25, [P, S])
    decay_last = at("decay_last", 4.25, [P, KC, NCH])
    stat = at("stat", 4.5, [P, 64])
    n_rounds = at("n_rounds", 4.75, [P, 1], i32)
    merged = at("merged", 6, [P, TT, D])
    x2 = at("x2", 6, [P, TT, D])
    junk = at("junk", 6, [P, D])
    raw = at("raw", 22, [P, RAW_SLOTS, 4 * BLK])
    w_hi = at("w_hi", 54, [P, SPLIT_SLOTS, 2 * BLK], f32r)
    w_lo = at("w_lo", 70, [P, SPLIT_SLOTS, 2 * BLK], f32r)
    h_hi = at("h_hi", 86, [P, KD, S], f32r)
    h_lo = at("h_lo", 102, [P, KD, S], f32r)
    y_hi = at("y_hi", 118, [P, KD, S], f32r)
    y_lo = at("y_lo", 134, [P, KD, S], f32r)
    A, B, C = 150, 166, 182
    x_tok = at("x_tok", A, [P, TT, D])
    mem_tok = at("mem_tok", B, [P, TT, D])
    prow = at("prow", C, [96, P])
    kv = at("kv", A, [P, TT, D])
    mq = at("mq", C + 16, [P, TT, CONV])
    kT = at("kT", B + 8, [P, KC, S])
    qT = at("qT", C, [P, KC, S])
    prob = at("prob", C + 8, [P, HEADS, TT, S])
    probT = at("probT", C + 16, [P, HEADS, TT, S])
    sig = at("sig", C, [P, TT, BLK])
    gated = at("gated", C + 4, [P, TT, BLK])
    gqk = at("gqk", A, [P, TT, D])
    gv = at("gv", B, [P, TT, D])
    w_a2 = at("w_a2", A, [RANK, CONV])
    a_lr = at("a_lr", C + 24, [RANK, S])
    dec_k = at("dec_k", C, [P, KC, S])
    dec_end = at("dec_end", C + 8, [P, KC, S])
    dec_q = at("dec_q", C + 16, [P, KC, S])
    q_far = at("q_far", A, [P, KC, 2 * CH])
    q_skip = at("q_skip", A + 4, [P, KC, CH])
    attT = [at(f"attT{i}", A + 6 + 1.5 * i, [P, 3 * P]) for i in range(2)]
    sq_junk = at("sq_junk", A + 9, [P, BLK])
    gr = at("gr", C, [P, TT, D])
    ccv = at("ccv", A, [P, TT, D])
    cb = at("cb", C + 16, [P, TT, CONV])
    uT = at("uT", B, [P, KC, S + 2])
    cbT = at("cbT", C + 8, [P, KC, S])
    conv = at("conv", A, [P, KC, S])
    conv_t = at("conv_t", A + 8, [P, S])
    xn = at("xn", 22, [P, TT, D])
    xn_lo = at("xn_lo", 22, [P, TT, D], f32r)
    hT = at("hT", 38, [P, KD, S])
    dispT = at("dispT", 54, [P, EPG // 2, S], f32r)
    disp = at("disp", 56, [P, TT, EPG * SLOTS], f32r)
    out_hi = at("out_hi", 58, [P, D // BLK, BLK], f32r)
    out_lo = at("out_lo", 66, [P, D // BLK, BLK], f32r)
    hidT = at("hidT", 74, [P, KE, 2 * SLOTS])
    act_gate = at("act_gate", 76, [P, BLK])
    hid = at("hid", 78, [P, EPG // 2, BLK])
    g_fin = at("g_fin", 82, [P, D])
    rt = at("rt", 90, [P, 32, TT * 16])
    slot_no = at("slot_no", 94, [P, SLOTS])
    place = at("place", 94.25, [P, TT, N_EXPERTS + EPG])
    weight = at("weight", 94.5, [P, TT, N_EXPERTS + EPG])
    group_w = at("group_w", 94.75, [P, TT, EPG])
    slot_w = at("slot_w", 94.875, [P, EPG // 2])
    xn_hi = at("xn_hi", 95, [P, TT, D], f32r)
    logitT = at("logitT", 1, [N_GROUPS + N_EXPERTS, S])
    tri = at("tri", 3.25, [P, P])
    ones = at("ones", 3.75, [P, P])
    fin = at("fin", 22, [P, TT, D])
    sq_scratch = at("sq_scratch", 54, [P, D])
    moe_raw = at("moe_raw", 111.75, [P, MOE_SLOTS, 4 * BLK])
    G_MIX, G_MEM, G_GLA, G_FFN, B_A2, W_CONV = 0, 16, 32, 48, 64, 72

    ctx = ExitStack()
    with ctx:
        bank = [ctx.enter_context(nc.psum_tensor(f"bank{i}", [P, BLK], f32)) for i in range(8)]
        pair = [bank[0:2], bank[2:4]]

        def turn_bank(u):
            return bank[4 + u % 4]

        def aux_bank(u):
            return bank[AUX[u]]

        def half(b, i):
            return b[:, i * S:(i + 1) * S]

        def sem(name):
            return ctx.enter_context(nc.semaphore(name))

        consts_made = sem("consts_made")
        params_in = sem("params_in")
        x_in = [sem(f"x_in{t}") for t in range(TT)]
        mem_in = [sem(f"mem_in{t}") for t in range(TT)]
        small_in = sem("small_in")
        a2_in = sem("a2_in")
        x_again = sem("x_again")
        gfin_in, out_stored = sem("gfin_in"), sem("out_stored")
        raw_loaded = [sem(f"raw_loaded{i}") for i in range(RAW_SLOTS)]
        hi_split, lo_split = sem("hi_split"), sem("lo_split")
        mm_done = sem("mm_done")
        pair_taken = [sem(f"pair_taken{i}") for i in range(2)]
        sq_ready, ms_ready, rms_ready, normed = (sem("sq_ready"), sem("ms_ready"),
                                                 sem("rms_ready"), sem("normed"))
        mem_rms_ready, mem_normed = sem("mem_rms_ready"), sem("mem_normed")
        turned = sem("turned")
        turn_taken = [sem(f"turn_taken{i}") for i in range(4)]
        aux_done = sem("aux_done")
        aux_taken = [sem(f"aux_taken{i}") for i in range(4)]
        hi_written, lo_written = sem("hi_written"), sem("lo_written")
        params_ready = sem("params_ready")
        act_chain, dve_chain, pool_chain = sem("act_chain"), sem("dve_chain"), sem("pool_chain")
        max_ready, prob_raw, prob_ready = sem("max_ready"), sem("prob_raw"), sem("prob_ready")
        w_ga_split, a_lr_ready = sem("w_ga_split"), sem("a_lr_ready")
        pre_ready, soft_ready, decay_sum_ready = (sem("pre_ready"), sem("soft_ready"),
                                                  sem("decay_sum_ready"))
        decay_ready, decayed_qk = sem("decay_ready"), sem("decayed_qk")
        att_done, att_masked = sem("att_done"), sem("att_masked")
        att_lower_taken, att_upper_taken = sem("att_lower_taken"), sem("att_upper_taken")
        o_done, o_sq, o_taken = sem("o_done"), sem("o_sq"), sem("o_taken")
        swish_ready, yb_ready = sem("swish_ready"), sem("yb_ready")
        conv_u, conv_out = sem("conv_u"), sem("conv_out")
        merged_done, residual_ready = sem("merged_done"), sem("residual_ready")
        y_ready = sem("y_ready")
        router_exp, router_d = sem("router_exp"), sem("router_d")
        route_ready, pos_done, rounds_ready = sem("route_ready"), sem("pos_done"), sem("rounds_ready")
        moe_loaded = [sem(f"moe_loaded{i}") for i in range(MOE_SLOTS)]
        moe_freed = {by: sem(f"moe_freed_by_{by}") for by in ("tensor", "scalar")}
        freed_loads, freed_in_group = moe_frees()
        disp_ready = sem("disp_ready")
        gt_done, gathered = sem("gt_done"), sem("gathered")
        lower_weights_ready = sem("lower_weights_ready")
        gt_taken = [sem(f"gt_taken{i}") for i in range(2)]
        gu_done, silu_ready, hid_ready = sem("gu_done"), sem("silu_ready"), sem("hid_ready")
        down_done = sem("down_done")
        hi_scaled, y_taken = sem("hi_scaled"), sem("y_taken")
        xn_hi_ready, xn_split = sem("xn_hi_ready"), sem("xn_split")
        comb_done = sem("comb_done")
        acc_done = sem("acc_done")
        stored = sem("stored")

        T_H, T_MEM, T_MEMQ, T_MEMK, T_PROB = 0, 8, 16, 20, 24
        T_GQ, T_GK, T_YB, T_U, T_CB, T_MERGED, T_XN, T_ROUTE = 28, 32, 36, 44, 48, 52, 60, 68
        U_PARAMS = 0
        MEM_ORDER = [("low", 0), ("s", 0), ("s", 1), ("s", 2), ("s", 3), ("t", 0), ("t", 1), ("y", 0),
                     ("t", 2), ("y", 1), ("t", 3), ("y", 2), ("y", 3)]
        U_MEM = {what: 1 + n for n, what in enumerate(w for w in MEM_ORDER if w[0] != "t")}
        U_GA, U_A2, U_LOGIT = U_MEM["low", 0], 10, 14
        AUX = (0,) + (1, 0, 2, 3, 1, 0, 2, 3, 1) + (0, 1, 2, 3) + (0,)
        GATHER, BACK, SLOT_W, HIDDEN, GT_USES = 0, 8, 9, 10, 12

        def group_bank(u):
            return bank[4 + u % 2]

        out_bank = [bank[b] for b in (2, 3, 6, 7)]

        def moe_slot(n):
            return (n + 1) % MOE_SLOTS

        def turned_before(eng, u):
            for s in range(4):
                if u > s:
                    eng.wait_ge(turn_taken[s], (u + 3 - s) // 4)

        def aux_before(eng, u):
            for b in range(4):
                if AUX[:u].count(b):
                    eng.wait_ge(aux_taken[b], AUX[:u].count(b))

        OUT_PARTS = [slice(0, D // 2), slice(D // 2, D)]

        block = ctx.enter_context(nc.Block())

        @block.sync
        def _(sp):
            vecs = ((norm_mix[0], 16, G_MIX), (norm_mem[0], 16, G_MEM), (gla_norm[0], 16, G_GLA),
                    (norm_ffn[0], 16, G_FFN), (gla_b_a2[0], 8, B_A2))
            sp.dma_start(x_tok[:, 0, :], x_v[:, 0, :]).then_inc(x_in[0], 16)
            sp.dma_start(x_tok[:, 1, :], x_v[:, 1, :]).then_inc(x_in[1], 16)
            for v, n, row in vecs:
                sp.dma_start(prow[row:row + n, :], v.rearrange("(a b) -> a b", b=P))\
                  .then_inc(params_in, 16)
            sp.dma_start(prow[W_CONV:W_CONV + 24, :],
                         conv_w[0].rearrange("k (c b) -> (k c) b", b=P)).then_inc(params_in, 16)
            def load(ph, load_no, it, src, slots=1):
                n = ph.q0 // 2 + load_no
                if slots and not (isinstance(it, int) and n + it * ph.per // 2 < RAW_SLOTS):
                    sp.wait_ge(lo_split, 2 * (n - RAW_SLOTS) + 2 * slots + it * ph.per)
                sp.dma_start(raw[:, n % RAW_SLOTS, :].rearrange("p (k n) -> p k n", k=4), src)\
                  .then_inc(raw_loaded[n % RAW_SLOTS], 16)

            def load_columns(name, view, col):
                ph = PH[name]
                with rounds_of(sp, ph.iters) as it:
                    off = it * 2 * BLK if isinstance(it, int) else sp.snap(it * (2 * BLK))
                    for jb in range(2):
                        for l in range(4):
                            if name == "mem_q" and jb == 0 and l == 3:
                                for t in range(TT):
                                    sp.dma_start(mem_tok[:, t, :], mem_v[:, t, :]).then_inc(mem_in[t], 16)
                            load(ph, 4 * jb + l, it, view[:, 4 * l:4 * l + 4, bass.ds(off + (col + jb * BLK), BLK)])

            def load_branch(name, gate_col, branch_v):
                ph = PH[name]
                kl = [g // 2 for g in ph.granules]
                with rounds_of(sp, ph.iters) as it:
                    off = sp.snap(it * (ph.jobs // 2 * BLK))
                    n = 0
                    for jb in range(ph.jobs):
                        view, col = ((in_v, gate_col), (branch_v, 0))[jb % 2]
                        for l in range(kl[jb]):
                            load(ph, n, it, view[:, 4 * l:4 * l + 4,
                                                 bass.ds(off + (col + jb // 2 * BLK), BLK)],
                                 slots=2 if jb % 2 == 0 and l == kl[jb] - 1 else 0 if jb % 2 and l == 0 else 1)
                            n += 1

            load_columns("mem_q", in_v, COL_MQ)
            load_columns("mem_k", kv_v, 0)
            load_columns("mem_v", kv_v, CONV)
            load_branch("branch_m", COL_GATE_M, brm_v)
            load_columns("gla_q", in_v, COL_GQ)
            load_columns("gla_k", in_v, COL_GQ + CONV)
            load_columns("gla_v_first", in_v, COL_GV)
            load_columns("gla_v_last", in_v, COL_GV + CONV)
            load_columns("gla_r", in_v, COL_GR)
            load_columns("conv_cv", in_v, COL_CONV + CONV)
            load_columns("conv_b", in_v, COL_CONV)
            load_branch("branch_b", COL_GATE_B, brb_v)
            load_branch("branch_a", COL_GATE_A, bra_v)
            load_columns("out_a", o_v, 0)
            load_columns("out_b", o_v, 2 * BLK)

            turned_before(sp, T_XN)
            for by in ("tensor", "scalar"):
                sp.sem_inc(moe_freed[by], freed_in_group[by])

            def expert_loads(group, per_group, in_dense=False):
                def load_moe(n, src):
                    by, count = freed_loads[n - MOE_SLOTS]
                    groups = 1 if n >= MOE_SLOTS else 0
                    sp.wait_ge(moe_freed[by], (per_group + groups) * freed_in_group[by] + count)
                    sp.dma_start(moe_raw[:, moe_slot(n), :].rearrange("p (k n) -> p k n", n=src.shape[-1]),
                                 src).then_inc(moe_loaded[n % MOE_SLOTS], 16)
                n = 0
                for kind, i in MOE_ORDER:
                    if kind not in ("gu", "d"):
                        continue
                    for l in range(4):
                        for side in range(2):
                            if kind == "gu":
                                e = bass.ds(group * EPG + i, 1)
                                load_moe(n, (gate_v, up_v)[side][:, e, 4 * l:4 * l + 4, :]
                                         .rearrange("p e k n -> p (e k) n"))
                            else:
                                e = bass.ds(group * EPG + (2 * i + side), 1)
                                load_moe(n, down_v[:, e, l:l + 1, :].rearrange("p e k n -> p (e k) n"))
                            n += 1
                            if in_dense and n == MOE_SLOTS - 1:
                                sp.wait_ge(mm_done, TOTAL_Q)

            with sp.Fori(0, N_GROUPS) as g:
                expert_loads(g, g, in_dense=True)
            sp.wait_ge(rounds_ready, 1)
            rounds = sp.value_load(n_rounds[0:1, 0:1], min_val=1, max_val=S // SLOTS)
            with sp.If(rounds > 1):
                with sp.Fori(1, rounds) as r:
                    with sp.Fori(0, N_GROUPS) as g:
                        expert_loads(g, r * N_GROUPS + g)
            for t in range(TT):
                for n, cols in enumerate(OUT_PARTS):
                    sp.wait_ge(stored, t * len(OUT_PARTS) + n + 1)
                    sp.dma_start(out_v[:, t, cols], fin[:, t, cols]).then_inc(out_stored, 16)
            sp.wait_ge(out_stored, 16 * TT * len(OUT_PARTS))

        @block.gpsimd
        def _(pool):
            n = [0]

            def chain(ins):
                n[0] += 1
                ins.then_inc(pool_chain, 1)
                pool.wait_ge(pool_chain, n[0])

            chain(nc.gpsimd.memset(ident[:], 0.0))
            nc.gpsimd.affine_select(out=ident[:], in_=ident[:], compare_op=ALU.not_equal, fill=1.0, base=0,
                                    pattern=[[-1, P]], channel_multiplier=1).then_inc(consts_made, 1)
            pool.wait_ge(mem_rms_ready, 1)
            for t in range(TT):
                nc.gpsimd.tensor_scalar(mem_tok[:, t, :], mem_tok[:, t, :], stat[:, 10 + t:11 + t], 1.0,
                                        ALU.mult, ALU.mult).then_inc(mem_normed, 1)
            chain(nc.gpsimd.memset(chunk_keep[:], 1.0))
            chain(nc.gpsimd.memset(chunk_keep[:].rearrange("p (n c) -> p n c", c=CH)[:, :, 0:1], 0.0))
            pool.dma_start(w_ga[:], in_v[:, :, COL_GA:COL_GA + RANK]).then_inc(small_in, 16)
            pool.dma_start(w_rt[:, :, 0:N_GROUPS], k_major(w_router_group[0])).then_inc(small_in, 16)
            pool.dma_start(w_rt[:, :, N_GROUPS:], k_major(w_router_expert[0])).then_inc(small_in, 16)
            turned_before(pool, T_GQ)
            aux_before(pool, U_A2)
            pool.dma_start(w_a2[:], gla_w_a2[0]).then_inc(a2_in, 16)
            pool.wait_ge(decayed_qk, 1)
            for i in range(2):
                nc.gpsimd.memset(attT[i][:], 0.0).then_inc(att_masked, 1)
            for h in range(HEADS):
                pool.wait_ge(att_lower_taken, h + 1)
                pool.wait_ge(att_upper_taken, 2 * h + 2)
                a = attT[h % 2]
                nc.gpsimd.affine_select(out=a[:, 0:S], in_=a[:, 0:S], compare_op=ALU.is_ge, fill=0.0, base=0,
                                        pattern=[[1, S]], channel_multiplier=-1).then_inc(att_masked, 1)
                nc.gpsimd.affine_select(out=a[:, S:], in_=a[:, S:], compare_op=ALU.is_ge, fill=0.0, base=0,
                                        pattern=[[1, P]], channel_multiplier=-1).then_inc(att_masked, 1)
            pool.wait_ge(pair_taken[0], PH["conv_b"].j0)
            pool.wait_ge(pair_taken[1], PH["conv_b"].j0)
            for t in range(TT):
                nc.gpsimd.tensor_tensor(ccv[:, t, 0:CONV], ccv[:, t, 0:CONV], ccv[:, t, CONV:], ALU.mult)\
                         .then_inc(conv_u, 1)
            turned_before(pool, T_U)
            chain(nc.gpsimd.memset(uT[:, :, 0:2], 0.0))
            turned_before(pool, T_MERGED)
            for c in range(KC):
                tap = [pcol[:, W_CONV + k * KC + c:W_CONV + k * KC + c + 1] for k in range(3)]
                chain(nc.gpsimd.tensor_scalar(conv[:, c, :], uT[:, c, 2:S + 2], tap[0], 1.0, ALU.mult, ALU.mult))
                for k in (1, 2):
                    chain(nc.gpsimd.tensor_scalar(conv_t[:], uT[:, c, 2 - k:S + 2 - k], tap[k], 1.0,
                                                  ALU.mult, ALU.mult))
                    chain(nc.gpsimd.tensor_tensor(conv[:, c, :], conv[:, c, :], conv_t[:], ALU.add))
                nc.gpsimd.tensor_tensor(conv[:, c, :], conv[:, c, :], cbT[:, c, :], ALU.mult)\
                         .then_inc(conv_out, 1)
            pool.wait_ge(mm_done, TOTAL_Q)
            chain(nc.gpsimd.iota(slot_no[:], pattern=[[1, SLOTS]], base=0, channel_multiplier=0,
                                 allow_small_or_imprecise_dtypes=True))
            chain(nc.gpsimd.memset(ones[:], 1.0))
            chain(nc.gpsimd.memset(tri[:], 1.0))
            chain(nc.gpsimd.affine_select(out=tri[:], in_=tri[:], compare_op=ALU.is_gt, fill=0.0, base=0,
                                          pattern=[[1, P]], channel_multiplier=-1))
            nc.gpsimd.iota(rt[:, 0, 0:4], pattern=[[-1, 4]], base=4, channel_multiplier=0,
                           allow_small_or_imprecise_dtypes=True)
            nc.gpsimd.iota(rt[:, 0, 4:8], pattern=[[SLOTS, 4]], base=0, channel_multiplier=0,
                           allow_small_or_imprecise_dtypes=True).then_inc(consts_made, 1)
            for t in range(TT):
                pool.wait_ge(xn_hi_ready, t + 1)
                nc.gpsimd.tensor_tensor(xn_lo[:, t, :], xn[:, t, :], xn_hi[:, t, :].bitcast(f32),
                                        ALU.subtract).then_inc(xn_split, 1)
            pool.dma_start(g_fin[:], norm_final.rearrange("(a d) -> a d", a=1).to_broadcast([P, D]))\
                .then_inc(gfin_in, 16)

        @block.scalar
        def _(act):
            A_ = nc.scalar
            chained = [0]

            def chain(ins):
                chained[0] += 1
                ins.then_inc(act_chain, 1)
                act.wait_ge(act_chain, chained[0])

            def turn_hi(u0, dst, gain=None, between={}):
                if gain is None:
                    for u in range(u0, u0 + KD // 2):
                        c = 2 * (u - u0)
                        act.wait_ge(turned, u + 1)
                        A_.copy(dst[:, c:c + 2, :], turn_bank(u)[:].rearrange("p (c s) -> p c s", c=2))\
                          .then_inc(hi_written, 1)
                    return
                for c in range(KD):
                    if c in between:
                        between[c]()
                    if c % 2 == 0:
                        act.wait_ge(turned, u0 + c // 2 + 1)
                    A_.activation(dst[:, c, :], half(turn_bank(u0 + c // 2), c % 2), ACT.Copy,
                                  scale=pcol[:, gain + c:gain + c + 1])\
                      .then_inc(hi_written, 1)

            def turn_copy(u0, dst):
                for u in range(u0 + 1, u0 + KC // 2, 2):
                    act.wait_ge(turned, u + 1)
                    c = 2 * (u - u0)
                    A_.copy(dst[:, c:c + 2, :], turn_bank(u)[:].rearrange("p (c s) -> p c s", c=2))\
                      .then_inc(turn_taken[u % 4], 1)

            def square_sum(src, k):
                if k:
                    act.wait_ge(sq_ready, k)
                A_.activation(junk[:], src, ACT.Square, accum_out=stat[:, k:k + 1]).then_inc(sq_ready, 1)

            def root(lo, n, count):
                act.wait_ge(ms_ready, count)
                A_.activation(stat[:, lo + 8:lo + 8 + n], stat[:, lo + 4:lo + 4 + n], ACT.Sqrt)\
                  .then_inc(rms_ready, 1)

            act.wait_ge(consts_made, 1)
            chain(A_.activation(junk[:, 0:1], ident[:, 0:1], ACT.Sqrt))
            for t in range(TT):
                act.wait_ge(x_in[t], 16)
                square_sum(x_tok[:, t, :], t)
                root(t, 1, t + 1)

            def split_hi(ph, q, it):
                n = ph.q0 + q + SPLIT_SLOTS
                if isinstance(it, int) and n + it * ph.per >= TOTAL_Q:
                    return
                slot = n // 2 % RAW_SLOTS
                if n % 2 == 0:
                    act.wait_ge(raw_loaded[slot], 16 * (n // 2 // RAW_SLOTS + 1) + it * (ph.per * 2))
                act.wait_ge(mm_done, ph.q0 + q + 1 + it * ph.per)
                A_.activation(w_hi[:, n % SPLIT_SLOTS, :], raw[:, slot, n % 2 * 1024:n % 2 * 1024 + 1024],
                              ACT.Copy).then_inc(hi_split, 1)

            def run(name, take, after={}):
                ph = PH[name]
                with rounds_of(act, ph.iters) as it:
                    q = 0
                    for jb, granules in enumerate(ph.granules):
                        for _ in range(granules):
                            split_hi(ph, q, it)
                            q += 1
                        act.wait_ge(mm_done, ph.q0 + q + it * ph.per)
                        take(ph, jb, it)
                        if jb in after:
                            after[jb]()

            def store_tile0(dst, col=0):
                def take(ph, jb, it):
                    A_.copy(dst[:, 0, bass.ds(it * 2 * BLK + col + jb * BLK, BLK)], pair[jb % 2][0][:])\
                      .then_inc(pair_taken[jb % 2], 1)
                return take

            def gate(ph, jb, it):
                if jb % 2 == 0:
                    act.wait_ge(pair_taken[1], ph.j0 + jb + it * ph.jobs)
                    for t in range(TT):
                        A_.activation(sig[:, t, :], pair[0][t][:], ACT.Sigmoid).then_inc(pair_taken[0], 1)

            def first_hi(n):
                if n % 2 == 0:
                    act.wait_ge(raw_loaded[n // 2], 16)
                A_.activation(w_hi[:, n, :], raw[:, n // 2, n % 2 * 1024:n % 2 * 1024 + 1024], ACT.Copy)\
                  .then_inc(hi_split, 1)

            act.wait_ge(params_ready, 1)
            turn_hi(T_H, h_hi, G_MIX, {6: lambda: first_hi(0)})
            for n in range(1, SPLIT_SLOTS):
                first_hi(n)
            for t in range(TT):
                act.wait_ge(mem_in[t], 16)
                square_sum(mem_tok[:, t, :], TT + t)
            root(TT, TT, 3)
            run("mem_q", store_tile0(mq))
            turn_hi(T_MEM, y_hi, G_MEM)
            run("mem_k", store_tile0(kv))

            turn_copy(T_MEMQ, qT[:])
            turn_copy(T_MEMK, kT[:])
            act.wait_ge(small_in, 48)
            A_.copy(w_ga_hi[:], w_ga[:]).then_inc(w_ga_split, 1)
            run("mem_v", store_tile0(kv, CONV))

            def exponentials(h):
                act.wait_ge(max_ready, h + 1)
                for t in range(TT):
                    A_.activation(prob[:, h, t, :], half(aux_bank(U_MEM["s", h]), t), ACT.Exp, scale=DK ** -0.5,
                                  bias=stat[:, 16 + 2 * h + t:17 + 2 * h + t],
                                  accum_out=stat[:, 24 + 2 * h + t:25 + 2 * h + t])\
                      .then_inc(prob_raw, 1)

            def memory_out_hi(h):
                u = U_MEM["y", h]
                act.wait_ge(aux_done, u + 1)
                A_.copy(y_hi[:, 2 * h:2 * h + 2, :], aux_bank(u)[:].rearrange("p (c s) -> p c s", c=2))\
                  .then_inc(hi_written, 1)

            def low_rank(_):
                act.wait_ge(aux_done, U_GA + 1)
                A_.copy(a_lr[:], aux_bank(U_GA)[0:RANK, 0:S]).then_inc(a_lr_ready, 1)

            for kind, h in MEM_ORDER:
                if kind != "t":
                    {"s": exponentials, "low": low_rank, "y": memory_out_hi}[kind](h)
            run("branch_m", gate)

            act.wait_ge(pair_taken[1], PH["branch_m"].j_end)
            for c in range(KC):
                act.wait_ge(aux_done, U_A2 + c // 2 + 1)
                A_.activation(dec_k[:, c, :], half(aux_bank(U_A2 + c // 2), c % 2), ACT.Identity,
                              bias=pcol[:, B_A2 + c:B_A2 + c + 1]).then_inc(pre_ready, 1)

            def soft_part():
                act.wait_ge(pre_ready, KC)
                chain(A_.activation(dec_end[:], dec_k[:], ACT.Abs))
                chain(A_.activation(dec_end[:], dec_end[:], ACT.Exp, scale=-1.0))
                A_.activation(dec_end[:], dec_end[:], ACT.Ln, bias=1.0).then_inc(soft_ready, 1)

            def decays():
                act.wait_ge(decay_sum_ready, 1)
                A_.activation(dec_k[:], dec_q[:], ACT.Exp, scale=-1.0 / 16).then_inc(decay_ready, 1)
                A_.activation(dec_end[:], dec_end[:], ACT.Exp, scale=-1.0 / 16).then_inc(decay_ready, 1)
                A_.activation(decay_last[:], decay_last[:], ACT.Exp, scale=1.0 / 16).then_inc(decay_ready, 1)
                act.wait_ge(decay_ready, 3)
                A_.activation(dec_q[:], dec_q[:], ACT.Exp, scale=1.0 / 16).then_inc(decay_ready, 1)

            run("gla_q", store_tile0(gqk), after={0: soft_part})
            run("gla_k", store_tile0(gqk, CONV))
            run("gla_v_first", store_tile0(gv), after={0: decays})
            run("gla_v_last", store_tile0(gv, CONV))

            def scores_out(h):
                act.wait_ge(att_done, h + 1)
                act.wait_ge(att_masked, 2 if h < 2 else 2 + 2 * (h - 1))
                if h >= 2:
                    act.wait_ge(o_done, 2 * (h - 1))
                A_.copy(attT[h % 2][0:CH, :], bank[4 + h % 2][0:CH, 0:3 * P]).then_inc(att_lower_taken, 1)

            def squares(h):
                for t in range(TT):
                    act.wait_ge(o_done, 2 * h + t + 1)
                    if h or t:
                        act.wait_ge(o_sq, 2 * h + t)
                    A_.activation(sq_junk[:], pair[1][t][:], ACT.Square,
                                  accum_out=stat[:, 32 + 2 * h + t:33 + 2 * h + t]).then_inc(o_sq, 1)

            for h in range(HEADS):
                scores_out(h)
                if h >= 1:
                    squares(h - 1)
            squares(HEADS - 1)
            act.wait_ge(ms_ready, 4)
            A_.activation(stat[:, 48:56], stat[:, 40:48], ACT.Sqrt).then_inc(rms_ready, 1)
            run("gla_r", store_tile0(gr))
            act.wait_ge(pair_taken[0], PH["gla_r"].j_end)
            act.wait_ge(pair_taken[1], PH["gla_r"].j_end)
            for t in range(TT):
                A_.activation(gr[:, t, :], gr[:, t, :], ACT.Silu).then_inc(swish_ready, 1)
            run("conv_cv", store_tile0(ccv))
            act.wait_ge(yb_ready, HEADS * TT)
            run("conv_b", store_tile0(cb))
            turn_hi(T_YB, y_hi, G_GLA)
            turn_copy(T_U, uT[:, :, 2:])
            turn_copy(T_CB, cbT[:])
            run("branch_b", gate)
            act.wait_ge(conv_out, KC)
            A_.copy(y_hi[:, 0:KC, :], conv[:]).then_inc(hi_written, 1)
            run("branch_a", gate)
            turn_hi(T_MERGED, h_hi)
            act.wait_ge(turned, T_XN)
            act.dma_start(x2[:], x_v).then_inc(x_again, 16)
            nothing = lambda ph, jb, it: None
            run("out_a", nothing)
            run("out_b", nothing)

            def residual_square(t, count):
                act.wait_ge(sq_ready, count)
                A_.activation(sq_scratch[:], x2[:, t, :], ACT.Square, accum_out=stat[:, t:t + 1])\
                  .then_inc(sq_ready, 1)

            for u in range(1, KD // 2, 2):
                act.wait_ge(turned, T_XN + u + 1)
                for c in (2 * u, 2 * u + 1):
                    ins = A_.activation(hT[:, c, :], half(turn_bank(u), c % 2), ACT.Copy,
                                        scale=pcol[:, G_FFN + c:G_FFN + c + 1])
                    ins.then_inc(act_chain if c % 2 == 0 else turn_taken[u % 4], 1)
                chained[0] += 1
            act.wait_ge(residual_ready, 1)
            for t in range(TT):
                residual_square(t, 4 + t)
            root(0, TT, 5)
            for t in range(TT):
                act.wait_ge(normed, TT + t + 1)
                A_.copy(xn_hi[:, t, :], xn[:, t, :]).then_inc(xn_hi_ready, 1)
                act.wait_ge(router_d, t + 1)
                A_.activation(rt[:, 3, 0:8], rt[:, 2, 0:8], ACT.Exp).then_inc(router_exp, 1)

            act.wait_ge(rounds_ready, 1)
            act.sem_inc(gt_taken[1], START)
            rounds = act.value_load(n_rounds[0:1, 0:1], min_val=1, max_val=S // SLOTS)
            with act.Fori(0, rounds) as r, act.Fori(0, N_GROUPS) as g:
                it = r * N_GROUPS + g
                for u in range(KD // 2):
                    act.wait_ge(gt_done, it * GT_USES + GATHER + u + 1 + START)
                    for c in (2 * u, 2 * u + 1):
                        A_.activation(hT[:, c, :], half(group_bank(u), c % 2), ACT.Copy,
                                      scale=pcol[:, G_FFN + c:G_FFN + c + 1])\
                          .then_inc(gathered if c % 2 == 0 else gt_taken[u % 2], 1)
                for kind, i in MOE_ORDER:
                    if kind == "gu":
                        act.wait_ge(gu_done, it * EPG + i + 1)
                        act.sem_inc(moe_freed["scalar"], 1)
                        act.wait_ge(hid_ready, it * EPG + i + START)
                        A_.activation(act_gate[SLOTS:, :], bank[i % 2][0:SLOTS, :], ACT.Silu)\
                          .then_inc(silu_ready, 1)
                    elif kind == "ht":
                        u = HIDDEN + i
                        act.wait_ge(gt_done, it * GT_USES + u + 1 + START)
                        A_.copy(hidT[:].rearrange("p k s -> p (k s)"), group_bank(u)[:])\
                          .then_inc(gt_taken[u % 2], 1)
                    elif kind == "d":
                        for b in range(4):
                            act.wait_ge(down_done, it * 8 + 4 * i + b + 1)
                            if b == 3:
                                act.sem_inc(moe_freed["scalar"], 1)
                            A_.activation(out_hi[:, b, :], out_bank[b][:], ACT.Copy, scale=slot_w[:, i:i + 1])\
                              .then_inc(hi_scaled, 1)

            act.wait_ge(acc_done, rounds * (N_EXPERTS * 4) + START)
            for t in range(TT):
                residual_square(t, 6 + t)
                root(t, 1, 6 + t)

        @block.vector
        def _(dve):
            V = nc.vector
            chained, hi_n = [0], [0]

            def chain(ins):
                chained[0] += 1
                ins.then_inc(dve_chain, 1)
                dve.wait_ge(dve_chain, chained[0])

            def turn_lo(u0, dst_lo, dst_hi, gain=None, between={}):
                if gain is None:
                    for u in range(u0, u0 + KD // 2):
                        c = 2 * (u - u0)
                        hi_n[0] += 1
                        dve.wait_ge(hi_written, hi_n[0])
                        V.tensor_tensor(dst_lo[:, c:c + 2, :], turn_bank(u)[:].rearrange("p (c s) -> p c s", c=2),
                                        dst_hi[:, c:c + 2, :].bitcast(f32), ALU.subtract)\
                         .then_inc(turn_taken[u % 4], 1)
                    return
                for c in range(KD):
                    if c in between:
                        between[c]()
                    if c % 2 == 0:
                        hi_n[0] += 2
                        dve.wait_ge(hi_written, hi_n[0])
                    u = u0 + c // 2
                    ins = V.scalar_tensor_tensor(out=dst_lo[:, c, :], in0=half(turn_bank(u), c % 2),
                                                 scalar=pcol[:, gain + c:gain + c + 1],
                                                 in1=dst_hi[:, c, :].bitcast(f32),
                                                 op0=ALU.mult, op1=ALU.subtract)
                    ins.then_inc(lo_written if c % 2 == 0 else turn_taken[u % 4], 1)

            def turn_copy(u0, dst):
                for u in range(u0, u0 + KC // 2, 2):
                    dve.wait_ge(turned, u + 1)
                    c = 2 * (u - u0)
                    V.tensor_copy(dst[:, c:c + 2, :], turn_bank(u)[:].rearrange("p (c s) -> p c s", c=2))\
                     .then_inc(turn_taken[u % 4], 1)

            def inverse_rms(lo, n, width, count):
                V.tensor_scalar(stat[:, lo + 4:lo + 4 + n], stat[:, lo:lo + n], 1.0 / width, EPS,
                                ALU.mult, ALU.add).then_inc(ms_ready, 1)
                dve.wait_ge(rms_ready, count)
                chain(V.reciprocal(stat[:, lo + 8:lo + 8 + n], stat[:, lo + 8:lo + 8 + n]))

            for t in range(TT):
                dve.wait_ge(sq_ready, t + 1)
                inverse_rms(t, 1, D, t + 1)
                V.tensor_scalar(x_tok[:, t, :], x_tok[:, t, :], stat[:, 8 + t:9 + t], None, ALU.mult)\
                 .then_inc(normed, 1)
            dve.wait_ge(params_in, 16 * 6)
            dve.wait_ge(aux_done, U_PARAMS + 1)
            V.tensor_copy(pcol[:], aux_bank(U_PARAMS)[:, 0:96]).then_inc(params_ready, 1)
            dve.wait_ge(params_ready, 1)
            dve.sem_inc(aux_taken[AUX[U_PARAMS]], 1)

            def split_lo(ph, q, it):
                n = ph.q0 + q + SPLIT_SLOTS
                if isinstance(it, int) and n + it * ph.per >= TOTAL_Q:
                    return
                slot = n // 2 % RAW_SLOTS
                dve.wait_ge(hi_split, n + 1 + it * ph.per)
                V.tensor_tensor(w_lo[:, n % SPLIT_SLOTS, :], raw[:, slot, n % 2 * 1024:n % 2 * 1024 + 1024],
                                w_hi[:, n % SPLIT_SLOTS, :].bitcast(f32), ALU.subtract).then_inc(lo_split, 1)

            def run(name, take, after={}):
                ph = PH[name]
                with rounds_of(dve, ph.iters) as it:
                    q = 0
                    for jb, granules in enumerate(ph.granules):
                        for _ in range(granules):
                            split_lo(ph, q, it)
                            q += 1
                        dve.wait_ge(mm_done, ph.q0 + q + it * ph.per)
                        take(ph, jb, it)
                        if jb in after:
                            after[jb]()

            def store_tile1(dst, col=0):
                def take(ph, jb, it):
                    V.tensor_copy(dst[:, 1, bass.ds(it * 2 * BLK + col + jb * BLK, BLK)], pair[jb % 2][1][:])\
                     .then_inc(pair_taken[jb % 2], 1)
                return take

            def branch(first, adds):
                def take(ph, jb, it):
                    if jb % 2 == 0:
                        return
                    done = ph.j0 + jb - 1 + it * ph.jobs
                    dve.wait_ge(pair_taken[0], done + 2)
                    for t in range(TT):
                        cols = bass.ds(it * (ph.jobs // 2) * BLK + jb // 2 * BLK, BLK)
                        if first:
                            V.tensor_tensor(merged[:, t, cols], sig[:, t, :], pair[1][t][:], ALU.mult)\
                             .then_inc(pair_taken[1], 1)
                            continue
                        dve.wait_ge(merged_done, START + adds + jb // 2 * 2 + it * ph.jobs)
                        V.tensor_tensor(gated[:, t, :], sig[:, t, :], pair[1][t][:], ALU.mult)\
                         .then_inc(pair_taken[1], 1)
                        dve.wait_ge(pair_taken[1], done + t + 1)
                        V.tensor_tensor(merged[:, t, cols], merged[:, t, cols], gated[:, t, :], ALU.add)\
                         .then_inc(merged_done, 1)
                return take

            def first_lo(n):
                dve.wait_ge(hi_split, n + 1)
                V.tensor_tensor(w_lo[:, n, :], raw[:, n // 2, n % 2 * 1024:n % 2 * 1024 + 1024],
                                w_hi[:, n, :].bitcast(f32), ALU.subtract).then_inc(lo_split, 1)

            turn_lo(T_H, h_lo, h_hi, G_MIX, {6: lambda: first_lo(0)})
            for n in range(1, SPLIT_SLOTS):
                first_lo(n)
            dve.wait_ge(sq_ready, 2 * TT)
            inverse_rms(TT, TT, D, 3)
            dve.sem_inc(mem_rms_ready, 1)
            run("mem_q", store_tile1(mq))
            turn_lo(T_MEM, y_lo, y_hi, G_MEM)
            run("mem_k", store_tile1(kv))

            turn_copy(T_MEMQ, qT[:])
            turn_copy(T_MEMK, kT[:])
            dve.wait_ge(w_ga_split, 1)
            V.tensor_tensor(w_ga_lo[:], w_ga[:], w_ga_hi[:].bitcast(f32), ALU.subtract).then_inc(w_ga_split, 1)
            run("mem_v", store_tile1(kv, CONV))

            def row_max(h):
                u, k = U_MEM["s", h], 16 + 2 * h
                dve.wait_ge(aux_done, u + 1)
                chain(V.reduce_max(stat[:, k:k + 2].unsqueeze(2),
                                   aux_bank(u)[:].rearrange("p (t m) -> p t m", t=TT), AX.X))
                V.tensor_scalar(stat[:, k:k + 2], stat[:, k:k + 2], -DK ** -0.5, None, ALU.mult)\
                 .then_inc(max_ready, 1)

            def normalise(h):
                k = 24 + 2 * h
                dve.wait_ge(prob_raw, TT * h + TT)
                dve.sem_inc(aux_taken[AUX[U_MEM["s", h]]], 1)
                chain(V.reciprocal(stat[:, k:k + 2], stat[:, k:k + 2]))
                for t in range(TT):
                    V.tensor_scalar(prob[:, h, t, :], prob[:, h, t, :], stat[:, k + t:k + t + 1], None, ALU.mult)\
                     .then_inc(prob_ready, 1)

            def probabilities_out(h):
                u = T_PROB + h
                dve.wait_ge(turned, u + 1)
                V.tensor_copy(probT[:, h], turn_bank(u)[:].rearrange("p (c s) -> p c s", c=2))\
                 .then_inc(turn_taken[u % 4], 1)

            def memory_out(h):
                u = U_MEM["y", h]
                hi_n[0] += 1
                dve.wait_ge(hi_written, hi_n[0])
                V.tensor_tensor(y_lo[:, 2 * h:2 * h + 2, :], aux_bank(u)[:].rearrange("p (c s) -> p c s", c=2),
                                y_hi[:, 2 * h:2 * h + 2, :].bitcast(f32), ALU.subtract)\
                 .then_inc(aux_taken[AUX[u]], 1)

            for kind, h in MEM_ORDER:
                if kind == "low":
                    dve.wait_ge(a_lr_ready, 1)
                    dve.sem_inc(aux_taken[AUX[U_GA]], 1)
                elif kind == "s":
                    row_max(h)
                    if h:
                        normalise(h - 1)
                elif kind == "t":
                    if h == 0:
                        normalise(HEADS - 1)
                    probabilities_out(h)
                else:
                    memory_out(h)
            run("branch_m", branch(True, 0))
            for i in range(KC // 2):
                dve.wait_ge(pre_ready, 2 * i + 2)
                dve.sem_inc(aux_taken[AUX[U_A2 + i]], 1)

            def decay_sums():
                dve.wait_ge(soft_ready, 1)
                chain(V.scalar_tensor_tensor(out=dec_k[:], in0=dec_k[:], scalar=0.0, in1=dec_end[:],
                                             op0=ALU.min, op1=ALU.subtract))
                for c in range(KC):
                    ins = V.tensor_tensor_scan(dec_q[:, c, :], chunk_keep[:], dec_k[:, c, :], 0.0, ALU.mult,
                                               ALU.add)
                    if c < KC - 1:
                        ins.then_inc(dve_chain, 1)
                        chained[0] += 1
                chain(ins)

            def decay_ends():
                sums = dec_q[:].rearrange("p c (n s) -> p (c n) s", s=CH)
                last = decay_last[:].rearrange("p c n -> p (c n)").unsqueeze(2)
                chain(V.tensor_copy(last, sums[:, :, CH - 1:CH]))
                V.tensor_tensor(dec_end[:].rearrange("p c (n s) -> p (c n) s", s=CH), sums,
                                last.to_broadcast([P, KC * NCH, CH]), ALU.subtract).then_inc(decay_sum_ready, 1)

            run("gla_q", store_tile1(gqk))
            run("gla_k", store_tile1(gqk, CONV), after={0: decay_sums, 1: decay_ends})
            run("gla_v_first", store_tile1(gv))
            dve.wait_ge(decay_ready, 4)
            for c in range(KC):
                u = T_GQ + c // 2
                dve.wait_ge(turned, u + 1)
                V.scalar_tensor_tensor(out=dec_q[:, c, :], in0=half(turn_bank(u), c % 2), scalar=DK ** -0.5,
                                       in1=dec_q[:, c, :], op0=ALU.mult, op1=ALU.mult)\
                 .then_inc(dve_chain if c % 2 == 0 else turn_taken[u % 4], 1)
                chained[0] += 1 - c % 2
            for c in range(KC):
                u = T_GK + c // 2
                dve.wait_ge(turned, u + 1)
                chain(V.tensor_tensor(dec_k[:, c, :], half(turn_bank(u), c % 2), dec_k[:, c, :], ALU.mult))
                V.tensor_tensor(dec_end[:, c, :], half(turn_bank(u), c % 2), dec_end[:, c, :], ALU.mult)\
                 .then_inc(dve_chain if c % 2 == 0 else turn_taken[u % 4], 1)
                chained[0] += 1 - c % 2

            def chunk_decay(n):
                return decay_last[:, :, n:n + 1].to_broadcast([P, KC, CH])

            def far_queries():
                turned_before(dve, T_YB)
                V.tensor_tensor(q_far[:, :, 0:CH], dec_q[:, :, 2 * CH:3 * CH], chunk_decay(1), ALU.mult)\
                 .then_inc(dve_chain, 1)
                chained[0] += 1
                chain(V.tensor_tensor(q_skip[:], dec_q[:, :, 3 * CH:4 * CH], chunk_decay(2), ALU.mult))
                V.tensor_tensor(q_far[:, :, CH:], q_skip[:], chunk_decay(1), ALU.mult).then_inc(decayed_qk, 1)

            run("gla_v_last", store_tile1(gv, CONV), after={0: far_queries})

            def scores_out(h):
                a = attT[h % 2]
                dve.wait_ge(att_done, h + 1)
                dve.wait_ge(att_masked, 2 if h < 2 else 2 + 2 * (h - 1))
                if h >= 2:
                    dve.wait_ge(o_done, 2 * (h - 1))
                V.tensor_copy(a[CH:, CH:S], bank[4 + h % 2][CH:, CH:S]).then_inc(att_upper_taken, 1)
                V.tensor_copy(a[CH:, S + CH:], bank[4 + h % 2][CH:, S + CH:3 * P]).then_inc(att_upper_taken, 1)

            def outputs_out(h):
                dve.wait_ge(o_done, 2 * h + 2)
                for t in range(TT):
                    dve.wait_ge(o_sq, 2 * h + t + 1)
                    V.tensor_copy(gv[:, t, h * DV:(h + 1) * DV], pair[1][t][:]).then_inc(o_taken, 1)

            for h in range(HEADS):
                scores_out(h)
                if h >= 1:
                    outputs_out(h - 1)
            outputs_out(HEADS - 1)
            dve.wait_ge(o_sq, HEADS * TT)
            V.tensor_scalar(stat[:, 40:48], stat[:, 32:40], 1.0 / DV, EPS, ALU.mult, ALU.add)\
             .then_inc(ms_ready, 1)
            run("gla_r", store_tile1(gr))
            dve.wait_ge(rms_ready, 4)
            chain(V.reciprocal(stat[:, 48:56], stat[:, 48:56]))
            dve.wait_ge(o_taken, HEADS * TT)
            for t in range(TT):
                dve.wait_ge(swish_ready, t + 1)
                for h in range(HEADS):
                    cols = slice(h * DV, (h + 1) * DV)
                    k = 48 + 2 * h + t
                    V.scalar_tensor_tensor(out=gv[:, t, cols], in0=gv[:, t, cols], scalar=stat[:, k:k + 1],
                                           in1=gr[:, t, cols], op0=ALU.mult, op1=ALU.mult)\
                     .then_inc(yb_ready, 1)
            run("conv_cv", store_tile1(ccv))
            run("conv_b", store_tile1(cb))
            turn_lo(T_YB, y_lo, y_hi, G_GLA)
            turn_copy(T_U, uT[:, :, 2:])
            turn_copy(T_CB, cbT[:])
            dve.sem_inc(merged_done, START)
            run("branch_b", branch(False, 0))
            hi_n[0] += 1
            dve.wait_ge(hi_written, hi_n[0])
            V.tensor_tensor(y_lo[:, 0:KC, :], conv[:], y_hi[:, 0:KC, :].bitcast(f32), ALU.subtract)\
             .then_inc(y_ready, 1)
            run("branch_a", branch(False, 8))
            turn_lo(T_MERGED, h_lo, h_hi)

            def add_residual(ph, jb, it):
                if jb == 0 and ph is PH["out_a"]:
                    dve.wait_ge(x_again, 16)
                n = (ph.j0 - PH["out_a"].j0 + jb)
                for t in range(TT):
                    dst = x2[:, t, n * BLK:(n + 1) * BLK]
                    V.tensor_tensor(dst, pair[jb % 2][t][:], dst, ALU.add).then_inc(pair_taken[jb % 2], 1)

            run("out_a", add_residual)
            run("out_b", add_residual)
            for i in range(2):
                dve.wait_ge(pair_taken[i], PH["out_b"].j_end)
            dve.sem_inc(residual_ready, 1)

            for u in range(0, KD // 2, 2):
                dve.wait_ge(turned, T_XN + u + 1)
                for c in (2 * u, 2 * u + 1):
                    V.tensor_scalar(hT[:, c, :], half(turn_bank(u), c % 2), pcol[:, G_FFN + c:G_FFN + c + 1],
                                    None, ALU.mult).then_inc(dve_chain if c % 2 == 0 else turn_taken[u % 4], 1)
                chained[0] += 1
            dve.wait_ge(sq_ready, 6)
            V.tensor_scalar(stat[:, 4:6], stat[:, 0:2], 1.0 / D, EPS, ALU.mult, ALU.add).then_inc(ms_ready, 1)
            dve.wait_ge(rms_ready, 5)
            chain(V.reciprocal(stat[:, 8:10], stat[:, 8:10]))
            for t in range(TT):
                V.tensor_scalar(xn[:, t, :], x2[:, t, :], stat[:, 8 + t:9 + t], None, ALU.mult).then_inc(normed, 1)
            dve.wait_ge(aux_done, U_LOGIT + 1)
            V.tensor_copy(logitT[:], aux_bank(U_LOGIT)[0:N_GROUPS + N_EXPERTS, 0:S])\
             .then_inc(aux_taken[AUX[U_LOGIT]], 1)
            dve.wait_ge(turned, T_ROUTE + 1)
            NE = N_GROUPS + N_EXPERTS
            logit = rt[:, 30:32, :].rearrange("p a b -> p (a b)")[:, 0:TT * NE].rearrange("p (t e) -> p t e", e=NE)
            V.tensor_tensor(logit, turn_bank(T_ROUTE)[:, 0:TT * NE].rearrange("p (t e) -> p t e", e=NE),
                            stat[:, 8:10].unsqueeze(2).to_broadcast([P, TT, NE]), ALU.mult)\
             .then_inc(turn_taken[T_ROUTE % 4], 1)
            dve.wait_ge(turn_taken[T_ROUTE % 4], T_ROUTE // 4 + 1)
            dve.wait_ge(consts_made, 2)

            def four(k):
                return rt[:, k, 0:8].rearrange("p (t e) -> p t e", e=4)

            def one(k):
                return rt[:, k, 0:2].unsqueeze(2)

            def wide(k):
                return one(k).to_broadcast([P, TT, 4])

            def sixteen(k):
                return rt[:, k, 0:32].rearrange("p (t g e) -> p t g e", g=N_GROUPS, e=EPG)

            rank = rt[:, 0, 0:4].unsqueeze(1).to_broadcast([P, TT, 4])

            def less_max(src, best):
                chain(V.reduce_max(one(best), src, AX.X))
                V.tensor_tensor(four(2), src, wide(best), ALU.subtract).then_inc(router_d, 1)

            def first_largest(src, best, pick):
                chain(V.tensor_tensor(four(6), src, wide(best), ALU.is_equal))
                chain(V.tensor_tensor(four(7), four(6), rank, ALU.mult))
                chain(V.reduce_max(one(8), four(7), AX.X))
                chain(V.tensor_tensor(four(pick), four(7), wide(8), ALU.is_equal))

            less_max(logit[:, :, 0:N_GROUPS], 10)
            first_largest(logit[:, :, 0:N_GROUPS], 10, 11)
            dve.wait_ge(router_exp, 1)
            chain(V.tensor_reduce(one(9), four(3), AX.X, ALU.add))
            picked = four(11).unsqueeze(3).to_broadcast([P, TT, N_GROUPS, EPG])
            chain(V.tensor_tensor(sixteen(12), logit[:, :, N_GROUPS:].rearrange("p t (g e) -> p t g e", e=EPG),
                                  picked, ALU.mult))
            chain(V.tensor_reduce(four(13), sixteen(12).rearrange("p t g e -> p t e g"), AX.X, ALU.add))
            less_max(four(13), 15)
            first_largest(four(13), 15, 16)
            dve.wait_ge(router_exp, 2)
            chain(V.scalar_tensor_tensor(out=four(17), in0=four(16), scalar=-2.0, in1=four(3),
                                         op0=ALU.mult, op1=ALU.add))
            chain(V.reduce_max(one(18), four(17), AX.X))
            first_largest(four(17), 18, 19)
            chain(V.tensor_tensor(four(25), four(16), four(19), ALU.add))
            CHOSEN = 27

            def to_experts(dst, k):
                return V.tensor_tensor(dst.rearrange("p t (g e) -> p t g e", g=N_GROUPS),
                                       four(k).unsqueeze(2).to_broadcast([P, TT, N_GROUPS, EPG]), picked, ALU.mult)

            chosen = rt[:, CHOSEN, 0:TT * N_EXPERTS].rearrange("p (t e) -> p t e", e=N_EXPERTS)
            to_experts(chosen, 25).then_inc(route_ready, 1)
            chain(V.scalar_tensor_tensor(out=one(20), in0=one(18), scalar=1.0, in1=one(9),
                                         op0=ALU.add, op1=ALU.mult))
            chain(V.reciprocal(one(21), one(20)))
            chain(V.tensor_tensor(one(22), one(18), one(21), ALU.mult))
            chain(V.tensor_tensor(four(23), four(16), wide(21), ALU.mult))
            chain(V.tensor_tensor(four(24), four(19), wide(22), ALU.mult))
            chain(V.tensor_tensor(four(23), four(23), four(24), ALU.add))
            chain(to_experts(weight[:, :, 0:N_EXPERTS], 23))
            chain(V.tensor_copy(weight[:, :, N_EXPERTS:], weight[:, :, 0:EPG]))
            dve.wait_ge(route_ready, 1)
            far = rt[:, 28, :].rearrange("p (t e) -> p t e", e=N_EXPERTS)
            chain(V.tensor_scalar(far, chosen, -1024.0, 1024.0, ALU.mult, ALU.add))
            dve.wait_ge(pos_done, 1)
            places = turn_bank(T_ROUTE + 1)[:, 0:48]
            longest, more = rt[:, 29, 0:1], rt[:, 29, 4:8]
            chain(V.reduce_max(longest, places[:, 32:48], AX.X))
            chain(V.tensor_tensor(more, longest.to_broadcast([P, 4]), rt[:, 0, 4:8], ALU.is_gt))
            chain(V.tensor_reduce(rt[:, 29, 1:2], more, AX.X, ALU.add))
            V.tensor_copy(n_rounds[:], rt[:, 29, 1:2]).then_inc(rounds_ready, 1)
            chain(V.tensor_tensor(place[:, :, 0:N_EXPERTS], far,
                                  places[:, 0:32].rearrange("p (t e) -> p t e", e=N_EXPERTS), ALU.add))
            chain(V.tensor_scalar(place[:, :, N_EXPERTS:], place[:, :, 0:EPG], -float(SLOTS), None, ALU.add))

            def dispatch(group):
                experts = bass.ds(group * EPG, EPG)
                for t in range(TT):
                    V.tensor_tensor(disp[:, t, :].rearrange("p (e s) -> p e s", s=SLOTS),
                                    slot_no[:].unsqueeze(1).to_broadcast([P, EPG, SLOTS]),
                                    place[:, t, experts].unsqueeze(2).to_broadcast([P, EPG, SLOTS]),
                                    ALU.is_equal).then_inc(disp_ready, 1)
                V.tensor_copy(group_w[:], weight[:, :, experts]).then_inc(disp_ready, 1)

            dve.wait_ge(mm_done, TOTAL_Q)
            dispatch(0)
            dve.wait_ge(rounds_ready, 1)
            for started in (gt_taken[0], hid_ready, acc_done):
                dve.sem_inc(started, START)
            rounds = dve.value_load(n_rounds[0:1, 0:1], min_val=1, max_val=S // SLOTS)

            with dve.Fori(0, rounds) as r:
                with dve.Fori(0, N_GROUPS) as g:
                    it = r * N_GROUPS + g
                    dve.wait_ge(gt_done, it * GT_USES + BACK + 1 + START)
                    V.tensor_copy(dispT[:].rearrange("p e s -> p (e s)"), group_bank(BACK)[:])\
                     .then_inc(gt_taken[BACK % 2], 1)
                    dve.wait_ge(gt_done, it * GT_USES + SLOT_W + 1 + START)
                    both = group_bank(SLOT_W)[:, 0:EPG].rearrange("p (i e) -> p i e", e=2)
                    V.tensor_copy(slot_w[0:SLOTS, :].unsqueeze(2), both[0:SLOTS, :, 0:1]).then_inc(lower_weights_ready, 1)
                    V.tensor_copy(slot_w[SLOTS:, :].unsqueeze(2), both[SLOTS:, :, 1:2])\
                     .then_inc(gt_taken[SLOT_W % 2], 1)
                    for kind, i in MOE_ORDER:
                        if kind == "gu":
                            dve.wait_ge(silu_ready, it * EPG + i + 1)
                            rows = slice(i % 2 * SLOTS, (i % 2 + 1) * SLOTS)
                            V.tensor_tensor(hid[rows, i // 2, :], act_gate[SLOTS:, :], bank[i % 2][SLOTS:, :],
                                            ALU.mult).then_inc(hid_ready, 1)
                            if i == EPG - 1:
                                dispatch(g + 1)
                        elif kind == "d":
                            for b in range(4):
                                dve.wait_ge(hi_scaled, it * 8 + 4 * i + b + 1)
                                V.scalar_tensor_tensor(out=out_lo[:, b, :], in0=out_bank[b][:],
                                                       scalar=slot_w[:, i:i + 1],
                                                       in1=out_hi[:, b, :].bitcast(f32),
                                                       op0=ALU.mult, op1=ALU.subtract).then_inc(y_taken, 1)
                        elif kind == "c":
                            for k in range(8):
                                b, t = k // 2, k % 2
                                dve.wait_ge(comb_done, it * 16 + 8 * i + k + 1)
                                dve.wait_ge(acc_done, it * 16 + 8 * i + START)
                                dst = x2[:, t, b * BLK:(b + 1) * BLK]
                                V.tensor_tensor(dst, dst, out_bank[k % 4][:], ALU.add).then_inc(acc_done, 1)
                dve.wait_ge(disp_ready, r * (N_GROUPS * 3) + (N_GROUPS + 1) * 3)
                V.tensor_scalar(place[:], place[:], -float(SLOTS), None, ALU.add)\
                 .then_inc(pos_done, 1)
                dve.wait_ge(pos_done, r + 2)

            dve.wait_ge(gfin_in, 16)
            for t in range(TT):
                dve.wait_ge(sq_ready, 7 + t)
                inverse_rms(t, 1, D, 6 + t)
                for cols in OUT_PARTS:
                    V.scalar_tensor_tensor(out=fin[:, t, cols], in0=x2[:, t, cols], scalar=stat[:, 8 + t:9 + t],
                                           in1=g_fin[:, cols], op0=ALU.mult, op1=ALU.mult).then_inc(stored, 1)

        @block.tensor
        def _(pe):
            T = nc.tensor

            def pairs_free(name):
                for p in range(2):
                    pe.wait_ge(pair_taken[p], PH[name].j_end)

            def turn(u0, n, src, col=0, first=0):
                for c in range(first, n):
                    u = u0 + c // 2
                    if c % 2 == 0 and u >= 4:
                        pe.wait_ge(turn_taken[u % 4], u // 4)
                    for t in range(TT):
                        ins = T.transpose(half(turn_bank(u), c % 2)[:, t * P:(t + 1) * P],
                                          src[:, t, col + c * P:col + (c + 1) * P], ident[:])
                    if c % 2:
                        ins.then_inc(turned, 1)

            def aux_free(u):
                if AUX[u] in AUX[:u]:
                    pe.wait_ge(aux_taken[AUX[u]], AUX[:u].count(AUX[u]))
                return aux_bank(u)

            def multiply(name, lhs, before_second=None):
                ph = PH[name]
                with rounds_of(pe, ph.iters) as it:
                    q = 0
                    for jb, granules in enumerate(ph.granules):
                        hi, lo = lhs[jb % len(lhs)]
                        if jb % 2 and before_second:
                            before_second()
                        pe.wait_ge(pair_taken[jb % 2], (ph.j0 + jb) // 2 * 2 + it * ph.jobs)
                        for g in range(granules):
                            n = ph.q0 + q
                            pe.wait_ge(lo_split, n + 1 + it * ph.per)
                            for c in range(2):
                                k = 2 * g + c
                                wh = w_hi[:, n % SPLIT_SLOTS, c * BLK:(c + 1) * BLK]
                                wl = w_lo[:, n % SPLIT_SLOTS, c * BLK:(c + 1) * BLK]
                                for t in range(TT):
                                    acc = pair[jb % 2][t][:]
                                    tok = slice(t * P, (t + 1) * P)
                                    last = k == 2 * granules - 1
                                    T.matmul(acc, hi[:, k, tok], wh, start=k == 0, stop=False)
                                    T.matmul(acc, hi[:, k, tok], wl, start=False, stop=False)
                                    ins = T.matmul(acc, lo[:, k, tok], wh, start=False, stop=last)
                            ins.then_inc(mm_done, 1)
                            q += 1

            H, Y = (h_hi, h_lo), (y_hi, y_lo)
            pe.wait_ge(consts_made, 1)
            pe.wait_ge(params_in, 16 * 6)
            T.transpose(aux_bank(U_PARAMS)[:, 0:96], prow[:], ident[0:96, 0:96]).then_inc(aux_done, 1)
            pe.wait_ge(normed, TT)
            turn(T_H, KD, x_tok)
            turned_before(pe, T_MEM)
            multiply("mem_q", [H])
            pe.wait_ge(mem_normed, TT)
            turn(T_MEM, KD, mem_tok)
            turned_before(pe, T_MEMQ)
            multiply("mem_k", [Y])

            pairs_free("mem_q")
            turn(T_MEMQ, KC, mq)
            pairs_free("mem_k")
            turn(T_MEMK, KC, kv)
            multiply("mem_v", [Y])
            turned_before(pe, T_PROB)
            pe.wait_ge(pair_taken[0], PH["mem_v"].j_end)
            pe.wait_ge(w_ga_split, 2)
            for kind, h in MEM_ORDER:
                if kind == "t":
                    pe.wait_ge(prob_ready, TT * h + TT)
                    turn(T_PROB + h, TT, prob[:, h])
                    continue
                if (kind, h) == ("s", 1):
                    pairs_free("mem_v")
                acc = aux_free(U_MEM[kind, h])
                if kind == "s":
                    for t in range(TT):
                        for i in range(2):
                            ins = T.matmul(half(acc, t), qT[:, 2 * h + i, t * P:(t + 1) * P], kT[:, 2 * h + i, :],
                                           start=i == 0, stop=i == 1)
                    ins.then_inc(aux_done, 1)
                    continue
                if kind == "low":
                    for c in range(KD):
                        for k, (left, right) in enumerate(((w_ga_hi, h_hi), (w_ga_hi, h_lo), (w_ga_lo, h_hi))):
                            ins = T.matmul(acc[0:RANK, 0:S], left[:, c, :], right[:, c, :],
                                           start=c == 0 and k == 0, stop=c == KD - 1 and k == 2)
                    ins.then_inc(aux_done, 1)
                    continue
                turned_before(pe, T_PROB + h + 1)
                for i in range(2):
                    col = CONV + h * DK + i * P
                    for m in range(TT):
                        ins = T.matmul(half(acc, i), kv[:, m, col:col + P], probT[:, h, m, :],
                                       start=m == 0, stop=m == 1)
                ins.then_inc(aux_done, 1)
            turned_before(pe, T_GQ)
            aux_before(pe, U_A2)
            multiply("branch_m", [H, Y])
            pe.wait_ge(pair_taken[0], PH["branch_m"].j_end)
            pe.wait_ge(a2_in, 16)
            for c in range(KC):
                if c == KC // 2:
                    pairs_free("branch_m")
                if c % 2 == 0:
                    acc = aux_free(U_A2 + c // 2)
                ins = T.matmul(half(acc, c % 2), w_a2[:, c * P:(c + 1) * P], a_lr[:], start=True, stop=True)
                if c % 2:
                    ins.then_inc(aux_done, 1)
            aux_before(pe, U_A2 + 2)
            multiply("gla_q", [H], lambda: aux_before(pe, U_LOGIT))
            multiply("gla_k", [H])
            multiply("gla_v_first", [H])
            pairs_free("gla_k")
            turn(T_GQ, KC, gqk)
            turn(T_GK, KC, gqk, col=CONV)
            multiply("gla_v_last", [H])

            pe.wait_ge(decayed_qk, 1)

            def scores(h):
                att = bank[4 + h % 2]
                if h >= 2:
                    pe.wait_ge(att_lower_taken, h - 1)
                    pe.wait_ge(att_upper_taken, 2 * (h - 1))
                blocks = []
                for n in range(NCH):
                    part = slice(n % 2 * CH, n % 2 * CH + CH)
                    base_col = 0 if n < 2 else P
                    cols = lambda a, b: slice(base_col + a * CH, base_col + b * CH)
                    keys = slice(n * CH, (n + 1) * CH)
                    blocks.append((part, cols(n, n + 1), dec_k, keys, dec_q, slice(n * CH, (n + 1) * CH)))
                    if n + 1 < NCH:
                        blocks.append((part, cols(n + 1, n + 2), dec_end, keys, dec_q,
                                       slice((n + 1) * CH, (n + 2) * CH)))
                    if n == 0:
                        blocks.append((part, cols(2, 4), dec_end, keys, q_far, slice(0, 2 * CH)))
                    if n == 1:
                        blocks.append((part, cols(3, 4), dec_end, keys, q_skip, slice(0, CH)))
                for part, cols, k_side, keys, q_side, queries in blocks:
                    for i in range(2):
                        ins = T.matmul(att[part, cols], k_side[:, 2 * h + i, keys],
                                       q_side[:, 2 * h + i, queries], start=i == 0, stop=i == 1)
                ins.then_inc(att_done, 1)

            def outputs(h):
                pe.wait_ge(att_masked, 2 + 2 * (h + 1))
                if h >= 1:
                    pe.wait_ge(o_taken, 2 * h)
                    pe.wait_ge(o_sq, 2 * h)
                a, cols = attT[h % 2], slice(h * DV, (h + 1) * DV)
                T.matmul(pair[1][0][:], a[:, 0:P], gv[:, 0, cols], start=True, stop=True).then_inc(o_done, 1)
                T.matmul(pair[1][1][:], a[:, P:S], gv[:, 0, cols], start=True, stop=False)
                T.matmul(pair[1][1][:], a[:, S:], gv[:, 1, cols], start=False, stop=True).then_inc(o_done, 1)

            aux_before(pe, U_LOGIT)
            turned_before(pe, T_YB)
            for h in range(HEADS):
                scores(h)
                if h == 0:
                    pairs_free("gla_v_last")
                if h >= 1:
                    outputs(h - 1)
            outputs(HEADS - 1)

            def outputs_taken():
                pe.wait_ge(o_taken, HEADS * TT)
                pe.wait_ge(o_sq, HEADS * TT)

            multiply("gla_r", [H], outputs_taken)
            multiply("conv_cv", [H])
            multiply("conv_b", [H])
            pe.wait_ge(yb_ready, HEADS * TT)
            pe.wait_ge(att_lower_taken, HEADS)
            pe.wait_ge(att_upper_taken, 2 * HEADS)
            turn(T_YB, KD, gv)
            pe.wait_ge(conv_u, TT)
            turn(T_U, KC, ccv)
            pairs_free("conv_b")
            turn(T_CB, KC, cb)
            multiply("branch_b", [H, Y], lambda: turned_before(pe, T_MERGED))
            multiply("branch_a", [H, Y], lambda: pe.wait_ge(y_ready, 1))
            pe.wait_ge(merged_done, START + 14)
            turn(T_MERGED, 12, merged)
            pe.wait_ge(merged_done, START + 16)
            turn(T_MERGED, KD, merged, first=12)
            turned_before(pe, T_XN)
            multiply("out_a", [H])
            multiply("out_b", [H])

            pe.wait_ge(pair_taken[0], PH["out_b"].j_end)
            pe.wait_ge(pair_taken[1], PH["out_b"].j0)
            turn(T_XN, 12, x2)
            pairs_free("out_b")
            turn(T_XN, KD, x2, first=12)
            turned_before(pe, T_ROUTE)
            pe.wait_ge(o_taken, HEADS * TT)
            pe.wait_ge(o_sq, HEADS * TT)
            NE = N_GROUPS + N_EXPERTS
            for c in range(KD):
                ins = T.matmul(aux_bank(U_LOGIT)[0:NE, 0:S], w_rt[:, c, :], hT[:, c, :], start=c == 0, stop=c == KD - 1)
            ins.then_inc(aux_done, 1)
            aux_before(pe, U_LOGIT + 1)
            for t in range(TT):
                ins = T.transpose(turn_bank(T_ROUTE)[:, t * NE:(t + 1) * NE], logitT[:, t * P:(t + 1) * P],
                                  ident[0:NE, 0:NE])
            ins.then_inc(turned, 1)
            pe.wait_ge(route_ready, 1)
            CHOSEN = 27
            chosen = [rt[:, CHOSEN, t * 16:(t + 1) * 16] for t in range(TT)]
            T.matmul(turn_bank(T_ROUTE + 1)[:, 0:16], tri[:], chosen[0], start=True, stop=True)
            T.matmul(turn_bank(T_ROUTE + 1)[:, 16:32], ones[:], chosen[0], start=True, stop=False)
            T.matmul(turn_bank(T_ROUTE + 1)[:, 16:32], tri[:], chosen[1], start=False, stop=True)
            T.matmul(turn_bank(T_ROUTE + 1)[:, 32:48], ones[:], chosen[0], start=True, stop=False)
            T.matmul(turn_bank(T_ROUTE + 1)[:, 32:48], ones[:], chosen[1], start=False, stop=True).then_inc(pos_done, 1)

            pe.wait_ge(rounds_ready, 1)
            pe.sem_inc(gt_done, START)
            rounds = pe.value_load(n_rounds[0:1, 0:1], min_val=1, max_val=S // SLOTS)
            turned_before(pe, T_ROUTE + 1)
            pe.wait_ge(xn_split, TT)
            with pe.Fori(0, rounds) as r, pe.Fori(0, N_GROUPS) as g:
                it = r * N_GROUPS + g

                def gt_bank(u):
                    pe.wait_ge(gt_taken[u % 2], it * (GT_USES // 2) + u // 2 + START)
                    return group_bank(u)

                pe.wait_ge(disp_ready, it * 3 + 3)
                for c in range(KD):
                    if c % 2 == 0:
                        acc = gt_bank(GATHER + c // 2)
                    for t in range(TT):
                        for part in (xn_hi, xn_lo):
                            ins = T.matmul(half(acc, c % 2), part[:, t, c * P:(c + 1) * P], disp[:, t, :],
                                           start=t == 0 and part is xn_hi, stop=t == 1 and part is xn_lo)
                    if c % 2:
                        ins.then_inc(gt_done, 1)
                for s in range(2):
                    pe.wait_ge(gt_taken[s], it * (GT_USES // 2) + BACK // 2 + START)
                n = 0
                rows = [slice(0, SLOTS), slice(SLOTS, P)]

                def way_back():
                    acc = gt_bank(BACK)
                    pairs = [slice(i * 2 * SLOTS, (i + 1) * 2 * SLOTS) for i in range(EPG // 2)]
                    for i, slots in enumerate(pairs):
                        for t in range(TT):
                            ins = T.transpose(half(acc, i)[:, t * P:(t + 1) * P], disp[:, t, slots].bitcast(f32), ident[:])
                    ins.then_inc(gt_done, 1)
                    acc = gt_bank(SLOT_W)
                    for i, slots in enumerate(pairs):
                        for t in range(TT):
                            ins = T.matmul(acc[:, 2 * i:2 * i + 2], disp[:, t, slots].bitcast(f32),
                                           group_w[:, t, 2 * i:2 * i + 2], start=t == 0, stop=t == 1)
                    ins.then_inc(gt_done, 1)

                def moe_wait(n):
                    pe.wait_ge(moe_loaded[n % MOE_SLOTS],
                               it * (MOE_LOADS // MOE_SLOTS * 16) + 16 * (n // MOE_SLOTS + 1))

                for kind, i in MOE_ORDER:
                    if kind == "gu":
                        acc = bank[i % 2]
                        pe.wait_ge(hid_ready, it * EPG + max(i - 1, 0) + START)
                        for l in range(4):
                            moe_wait(n)
                            moe_wait(n + 1)
                            for k in range(4):
                                c = 4 * l + k
                                for side in range(2):
                                    w = moe_raw[:, moe_slot(n + side), k * BLK:(k + 1) * BLK]
                                    ins = T.matmul(acc[rows[side], :], hT[:, c, i * SLOTS:(i + 1) * SLOTS], w,
                                                   start=c == 0, stop=c == KD - 1)
                                    if k == 3 and l * 2 + side < 7:
                                        ins.then_inc(moe_freed["tensor"], 1)
                            n += 2
                        ins.then_inc(gu_done, 1)
                        if i == 0:
                            way_back()
                    elif kind == "ht":
                        slot = gt_bank(HIDDEN + i)
                        pe.wait_ge(hid_ready, it * EPG + 2 * i + 2 + START)
                        for k in range(KE):
                            ins = T.transpose(slot[:, k * P:(k + 1) * P], hid[:, i, k * P:(k + 1) * P], ident[:])
                        ins.then_inc(gt_done, 1)
                    elif kind == "d":
                        u = HIDDEN + i
                        pe.wait_ge(gt_taken[u % 2], it * (GT_USES // 2) + u // 2 + 1 + START)
                        pe.wait_ge(acc_done, it * 16 + 8 * i + START)
                        for l in range(KE):
                            moe_wait(n)
                            moe_wait(n + 1)
                            for b in range(4):
                                for side in range(2):
                                    w = moe_raw[:, moe_slot(n + side), b * BLK:(b + 1) * BLK]
                                    ins = T.matmul(out_bank[b][rows[side], :],
                                                   hidT[:, l, side * SLOTS:(side + 1) * SLOTS], w,
                                                   start=l == 0, stop=l == KE - 1)
                                    if b == 3 and l * 2 + side < 7:
                                        ins.then_inc(moe_freed["tensor"], 1)
                                if l == KE - 1:
                                    ins.then_inc(down_done, 1)
                            n += 2
                    elif kind == "c":
                        for k in range(8):
                            b, t = k // 2, k % 2
                            if k < 4:
                                pe.wait_ge(y_taken, it * 8 + 4 * i + k + 1)
                            else:
                                pe.wait_ge(acc_done, it * 16 + 8 * i + k - 3 + START)
                            T.matmul(out_bank[k % 4][:], dispT[:, i, t * P:(t + 1) * P], out_hi[:, b, :],
                                     start=True, stop=False)
                            T.matmul(out_bank[k % 4][:], dispT[:, i, t * P:(t + 1) * P], out_lo[:, b, :],
                                     start=False, stop=True).then_inc(comb_done, 1)


MOE_ORDER = [("gu", 0), ("gu", 1), ("gu", 2), ("ht", 0), ("d", 0), ("gu", 3), ("c", 0), ("ht", 1),
             ("d", 1), ("c", 1)]
MOE_LOADS = 8 * sum(kind in ("gu", "d") for kind, _ in MOE_ORDER)


def moe_frees():
    out, count = [], {"tensor": 0, "scalar": 0}
    for kind, _ in MOE_ORDER:
        for l in range(8 if kind in ("gu", "d") else 0):
            by = "scalar" if l == 7 else "tensor"
            count[by] += 1
            out.append((by, count[by]))
    return out, count


_INS = ["x", "mem", "norm_mix", "w_in", "conv_w", "gla_w_a2", "gla_b_a2", "gla_norm", "norm_mem",
        "w_mem_kv", "w_br_conv", "w_br_gla", "w_br_mem", "w_o", "norm_ffn", "w_router_group",
        "w_router_expert", "w_gate", "w_up", "w_down", "norm_final"]


def kernel(**inputs):
    import numpy as _np
    import concourse.bacc as _bacc
    from concourse import mybir as _mybir
    from concourse.bass_utils import run_bass_kernel_spmd as _run

    nc = _bacc.Bacc("TRN2", target_bir_lowering=False, num_devices=1)
    arrays, args = {}, []
    for name in _INS:
        a = _np.ascontiguousarray(inputs[name])
        arrays[f"in_{name}_dram"] = a
        args.append(nc.dram_tensor(f"in_{name}_dram", a.shape, _mybir.dt.from_np(a.dtype),
                                   kind="ExternalInput").ap())
    args.append(nc.dram_tensor("out_dram", (1, S, D), _mybir.dt.float32, kind="ExternalOutput").ap())
    hybrid_layer(nc, *args)
    r = _run(nc, [arrays], core_ids=[0])
    return r.results[0]["out_dram"]
```
